# Optimizing a Trainium2 kernel written in Bass

```python
import math
import jax
import jax.numpy as jnp
from jax import lax
import numpy as np

D_MODEL = 2048
BATCH = 1
SEQ = 256
DEPTH = 1
DEC_BATCH = 1
DEC_SEQ = 64
PAST_LEN = 512

CHUNK = 64
Q_BLOCK = 128
EPS = 1e-6
NEG_INF = -1e30
D_FF = 5632
DA_HEADS = 8
DA_HALF = 64
DA_HEAD_DIM = 2 * DA_HALF
DA_WIDTH = DA_HEADS * DA_HEAD_DIM
MLA_HEADS = 8
Q_LORA = 512
KV_LORA = 256
QK_NOPE = 128
QK_ROPE = 64
QK_HEAD = QK_NOPE + QK_ROPE
V_HEAD = 128
MLA_WIDTH = MLA_HEADS * V_HEAD
MIX_WIDTH = DA_WIDTH + MLA_WIDTH
IN_COLS = 3 * DA_WIDTH + Q_LORA + KV_LORA + QK_ROPE
ROPE_THETA = 10000.0

kernel_name = "hymba_diffattn_mla_macaron_stream"

def _rmsnorm(x, g):
    xf = x.astype(jnp.float32)
    y = xf * lax.rsqrt(jnp.mean(xf * xf, axis=-1, keepdims=True) + EPS)
    return (y * g.astype(jnp.float32)).astype(x.dtype)

def _swiglu(x, w_gate, w_up, w_down):
    return (jax.nn.silu(x @ w_gate) * (x @ w_up)) @ w_down

def _alibi_slopes(n):
    return jnp.asarray(np.array([2.0 ** (-8.0 * (i + 1) / n) for i in range(n)], np.float32))

def _rope(x, pos):
    half = x.shape[-1] // 2
    inv = ROPE_THETA ** (-jnp.arange(half, dtype=jnp.float32) / half)
    ang = pos.astype(jnp.float32)[:, None] * inv[None, :]
    cos = jnp.cos(ang)[:, None, :]
    sin = jnp.sin(ang)[:, None, :]
    xf = x.astype(jnp.float32)
    x1, x2 = xf[..., :half], xf[..., half:]
    return jnp.concatenate([x1 * cos - x2 * sin, x1 * sin + x2 * cos], axis=-1).astype(x.dtype)

def _chunk_mask(qpos, kpos):
    return (kpos[None, :] // CHUNK) <= (qpos[:, None] // CHUNK)

def _diff_attn_core(q, qpos, k, v, kpos, lam, slopes):
    mask = _chunk_mask(qpos, kpos)
    dist = jnp.abs(qpos[:, None] - kpos[None, :]).astype(jnp.float32)
    bias = -slopes[:, None, None] * dist[None]
    scale = DA_HALF ** -0.5

    def probs(qa, ka):
        s = jnp.einsum("bqhd,bkhd->bhqk", qa, ka, preferred_element_type=jnp.float32) * scale + bias
        return jax.nn.softmax(jnp.where(mask, s, NEG_INF), axis=-1)

    a = probs(q[..., :DA_HALF], k[..., :DA_HALF]) - lam * probs(q[..., DA_HALF:], k[..., DA_HALF:])
    return jnp.einsum("bhqk,bkhd->bqhd", a.astype(v.dtype), v)

def _mla_core(q, qpos, k, v, kpos):
    mask = _chunk_mask(qpos, kpos)
    s = jnp.einsum("bqhd,bkhd->bhqk", q, k, preferred_element_type=jnp.float32) * (QK_HEAD ** -0.5)
    p = jax.nn.softmax(jnp.where(mask, s, NEG_INF), axis=-1)
    return jnp.einsum("bhqk,bkhd->bqhd", p.astype(v.dtype), v)

def _attend(fn, q, qpos, blocked):
    if not blocked:
        return fn(q, qpos)
    B, T = q.shape[0], q.shape[1]
    nb = T // Q_BLOCK
    qb = jnp.moveaxis(q.reshape((B, nb, Q_BLOCK) + q.shape[2:]), 1, 0)
    pb = qpos.reshape(nb, Q_BLOCK)
    out = lax.map(lambda a: fn(a[0], a[1]), (qb, pb))
    return jnp.moveaxis(out, 0, 1).reshape((B, T) + out.shape[3:])

def _token_mix(h, qpos, past, w_in, lq1, lk1, lq2, lk2, da_subln, q_norm, w_uq,
               kv_norm, w_ukv, w_out, layer_idx, blocked):
    B, T, _ = h.shape
    z = h @ w_in
    o1, o2, o3 = DA_WIDTH, 2 * DA_WIDTH, 3 * DA_WIDTH
    o4, o5 = o3 + Q_LORA, o3 + Q_LORA + KV_LORA
    da_q = z[..., :o1].reshape(B, T, DA_HEADS, DA_HEAD_DIM)
    da_k = z[..., o1:o2].reshape(B, T, DA_HEADS, DA_HEAD_DIM)
    da_v = z[..., o2:o3].reshape(B, T, DA_HEADS, DA_HEAD_DIM)
    c_q = z[..., o3:o4]
    c_kv = _rmsnorm(z[..., o4:o5], kv_norm)
    k_r = _rope(z[..., o5:][:, :, None, :], qpos)[:, :, 0, :]

    q_m = (_rmsnorm(c_q, q_norm) @ w_uq).reshape(B, T, MLA_HEADS, QK_HEAD)
    q_m = jnp.concatenate([q_m[..., :QK_NOPE], _rope(q_m[..., QK_NOPE:], qpos)], axis=-1)

    if past is None:
        k_all, v_all, ckv_all, kr_all = da_k, da_v, c_kv, k_r
        kpos = qpos
    else:
        ck, cv, cckv, ckr = past
        k_all = jnp.concatenate([ck, da_k], axis=1)
        v_all = jnp.concatenate([cv, da_v], axis=1)
        ckv_all = jnp.concatenate([cckv, c_kv], axis=1)
        kr_all = jnp.concatenate([ckr, k_r], axis=1)
        kpos = jnp.arange(ck.shape[1] + T, dtype=jnp.int32)
    Tk = k_all.shape[1]

    lam_init = 0.8 - 0.6 * math.exp(-0.3 * layer_idx)
    lam = (jnp.exp(jnp.sum(lq1.astype(jnp.float32) * lk1.astype(jnp.float32)))
           - jnp.exp(jnp.sum(lq2.astype(jnp.float32) * lk2.astype(jnp.float32))) + lam_init)
    slopes = _alibi_slopes(DA_HEADS)
    out_da = _attend(lambda qb, pb: _diff_attn_core(qb, pb, k_all, v_all, kpos, lam, slopes),
                     da_q, qpos, blocked)
    out_da = _rmsnorm(out_da, da_subln) * (1.0 - lam_init)

    kv = (ckv_all @ w_ukv).reshape(B, Tk, MLA_HEADS, QK_NOPE + V_HEAD)
    k_m = jnp.concatenate(
        [kv[..., :QK_NOPE], jnp.broadcast_to(kr_all[:, :, None, :], (B, Tk, MLA_HEADS, QK_ROPE))], axis=-1)
    v_m = kv[..., QK_NOPE:]
    out_mla = _attend(lambda qb, pb: _mla_core(qb, pb, k_m, v_m, kpos), q_m, qpos, blocked)

    merged = jnp.concatenate([out_da.reshape(B, T, DA_WIDTH), out_mla.reshape(B, T, MLA_WIDTH)], axis=-1)
    return merged @ w_out, (da_k, da_v, c_kv, k_r)

def _trunk(x, qpos, caches, w, blocked):
    (ffn1_norm, ffn1_w_gate, ffn1_w_up, ffn1_w_down, mix_norm, w_in,
     lq1, lk1, lq2, lk2, da_subln, q_norm, w_uq, kv_norm, w_ukv, w_out,
     ffn2_norm, ffn2_w_gate, ffn2_w_up, ffn2_w_down, final_norm) = w
    states = []
    for l in range(DEPTH):
        x = x + 0.5 * _swiglu(_rmsnorm(x, ffn1_norm[l]), ffn1_w_gate[l], ffn1_w_up[l], ffn1_w_down[l])
        past = None if caches is None else (caches[0][l], caches[1][l], caches[2][l], caches[3][l])
        y, st = _token_mix(_rmsnorm(x, mix_norm[l]), qpos, past, w_in[l], lq1[l], lk1[l], lq2[l], lk2[l],
                           da_subln[l], q_norm[l], w_uq[l], kv_norm[l], w_ukv[l], w_out[l], l, blocked)
        x = x + y
        x = x + 0.5 * _swiglu(_rmsnorm(x, ffn2_norm[l]), ffn2_w_gate[l], ffn2_w_up[l], ffn2_w_down[l])
        states.append(st)
    y = _rmsnorm(x, final_norm)
    new_state = tuple(jnp.stack([s[i] for s in states], axis=0) for i in range(4))
    return y, new_state

def setup_inputs(seed: int = 0) -> dict:
    key = jax.random.key(seed)
    ks = jax.random.split(key, 32)
    f32 = jnp.float32
    L = DEPTH

    def nrm(k, shape, scale=1.0):
        return jax.random.normal(k, shape, f32) * scale

    def gain(k, n):
        return 1.0 + 0.05 * nrm(k, (L, n))

    return {
        "x_prompt": nrm(ks[0], (BATCH, SEQ, D_MODEL)),
        "x_sample": nrm(ks[1], (DEC_BATCH, DEC_SEQ, D_MODEL)),
        "cache_da_k": nrm(ks[2], (L, DEC_BATCH, PAST_LEN, DA_HEADS, DA_HEAD_DIM)),
        "cache_da_v": nrm(ks[3], (L, DEC_BATCH, PAST_LEN, DA_HEADS, DA_HEAD_DIM)),
        "cache_mla_ckv": nrm(ks[4], (L, DEC_BATCH, PAST_LEN, KV_LORA)),
        "cache_mla_krope": nrm(ks[5], (L, DEC_BATCH, PAST_LEN, QK_ROPE)),
        "ffn1_norm": gain(ks[6], D_MODEL),
        "ffn1_w_gate": nrm(ks[7], (L, D_MODEL, D_FF), D_MODEL ** -0.5),
        "ffn1_w_up": nrm(ks[8], (L, D_MODEL, D_FF), D_MODEL ** -0.5),
        "ffn1_w_down": nrm(ks[9], (L, D_FF, D_MODEL), D_FF ** -0.5),
        "mix_norm": gain(ks[10], D_MODEL),
        "w_in": nrm(ks[11], (L, D_MODEL, IN_COLS), D_MODEL ** -0.5),
        "da_lambda_q1": nrm(ks[12], (L, DA_HALF), 0.1),
        "da_lambda_k1": nrm(ks[13], (L, DA_HALF), 0.1),
        "da_lambda_q2": nrm(ks[14], (L, DA_HALF), 0.1),
        "da_lambda_k2": nrm(ks[15], (L, DA_HALF), 0.1),
        "da_subln": gain(ks[16], DA_HEAD_DIM),
        "mla_q_norm": gain(ks[17], Q_LORA),
        "mla_w_uq": nrm(ks[18], (L, Q_LORA, MLA_HEADS * QK_HEAD), Q_LORA ** -0.5),
        "mla_kv_norm": gain(ks[19], KV_LORA),
        "mla_w_ukv": nrm(ks[20], (L, KV_LORA, MLA_HEADS * (QK_NOPE + V_HEAD)), KV_LORA ** -0.5),
        "w_out": nrm(ks[21], (L, MIX_WIDTH, D_MODEL), MIX_WIDTH ** -0.5),
        "ffn2_norm": gain(ks[22], D_MODEL),
        "ffn2_w_gate": nrm(ks[23], (L, D_MODEL, D_FF), D_MODEL ** -0.5),
        "ffn2_w_up": nrm(ks[24], (L, D_MODEL, D_FF), D_MODEL ** -0.5),
        "ffn2_w_down": nrm(ks[25], (L, D_FF, D_MODEL), D_FF ** -0.5),
        "final_norm": 1.0 + 0.05 * nrm(ks[26], (D_MODEL,)),
    }

def reference(x_prompt, x_sample, cache_da_k, cache_da_v, cache_mla_ckv, cache_mla_krope,
              ffn1_norm, ffn1_w_gate, ffn1_w_up, ffn1_w_down, mix_norm, w_in,
              da_lambda_q1, da_lambda_k1, da_lambda_q2, da_lambda_k2, da_subln,
              mla_q_norm, mla_w_uq, mla_kv_norm, mla_w_ukv, w_out,
              ffn2_norm, ffn2_w_gate, ffn2_w_up, ffn2_w_down, final_norm):
    w = (ffn1_norm, ffn1_w_gate, ffn1_w_up, ffn1_w_down, mix_norm, w_in,
         da_lambda_q1, da_lambda_k1, da_lambda_q2, da_lambda_k2, da_subln,
         mla_q_norm, mla_w_uq, mla_kv_norm, mla_w_ukv, w_out,
         ffn2_norm, ffn2_w_gate, ffn2_w_up, ffn2_w_down, final_norm)

    pos_p = jnp.arange(x_prompt.shape[1], dtype=jnp.int32)
    y_prompt, st_p = _trunk(x_prompt, pos_p, None, w, True)

    past_len = cache_da_k.shape[2]
    pos_s = past_len + jnp.arange(x_sample.shape[1], dtype=jnp.int32)
    y_sample, st_s = _trunk(x_sample, pos_s,
                            (cache_da_k, cache_da_v, cache_mla_ckv, cache_mla_krope), w, False)

    new_da_k_p, new_da_v_p, new_ckv_p, new_kr_p = st_p
    new_da_k_s, new_da_v_s, new_ckv_s, new_kr_s = st_s
    return (y_prompt, y_sample, new_da_k_p, new_da_v_p, new_ckv_p, new_kr_p,
            new_da_k_s, new_da_v_s, new_ckv_s, new_kr_s)


_drawn_inputs = setup_inputs


def setup_inputs(seed=0):
    import zlib

    import numpy as np

    out = dict(_drawn_inputs(seed))
    spreads = {}
    factors = {'cache_mla_krope': 2.711, 'da_lambda_q2': 8.0, 'mla_q_norm': 8.0, 'ffn2_norm': 3.25}
    for name, (base, spread) in spreads.items():
        noise = np.random.default_rng([zlib.crc32(name.encode()), seed]).standard_normal(out[name].shape)
        drawn = base * np.exp(spread * noise) if base else spread * noise
        out[name] = jnp.asarray(drawn.astype(out[name].dtype))
    for name, factor in factors.items():
        out[name] = (out[name] * factor).astype(out[name].dtype)
    return out
```

```python
from contextlib import ExitStack

import numpy as np

import concourse.bass as bass
from concourse import mybir

F32 = mybir.dt.float32
F32R = mybir.dt.float32r
ALU = mybir.AluOpType
ACT = mybir.ActivationFunctionType
AX_X = mybir.AxisListType.X

P = 128
D = 2048
KT = D // P
SEQ = 256
DEC = 64
T = SEQ + DEC
PAST = 512
CHUNK = 64
KEYS = PAST + DEC
F = 5632
UC = 512
UK = 4
PARTS = F // UC
HEADS = 8
DH = 128
HALF = 64
QL = 512
KVL = 256
ROPE = 64
QKH = DH + ROPE
ROPE_THETA = 10000.0
EPS = 1e-6
LAM_INIT = 0.2
JOB_CC, JOB_CTOK, JOB_KV, JOB_Y = 20, 23, 26, 56
DA_SCALE = HALF ** -0.5
MLA_SCALE = QKH ** -0.5
NEG = -1e30
BIG = 1e30
SLOPES = [2.0 ** (-8.0 * (i + 1) / HEADS) for i in range(HEADS)]
HB = 4
RAW_SLOTS = 4
SPLIT_SLOTS = 2
TOK = [(0, P), (P, P), (SEQ, DEC)]
NTOK = T + PAST

C_ID, C_STACK, C_SWAP = 0, 128, 192
C_COS, C_SIN, C_DIST, C_DISTS, C_ALL = 320, 640, 960, 1344, 1920

G_F1, G_MIX, G_F2, G_FIN, G_SUB, G_Q, G_KV, G_ALL = 0, 16, 32, 48, 64, 65, 69, 71

FFN_UNITS, FFN_GROUPS = 12 * PARTS, 6 * PARTS
U_Z = FFN_UNITS
U_UQ = U_Z + 32
U_UKV = U_UQ + 3
U_OUT = U_UKV + 2
U_F2 = U_OUT + 16
U_END = U_F2 + FFN_UNITS
GR_Z = FFN_GROUPS
GR_UQ = GR_Z + 8
GR_OUT = GR_UQ + 3
GR_F2 = GR_OUT + 4

Z_COLS = [0, 1024, 2048, 512, 1536, 2560, 3072, 3584]
Z_WIDTH = [UC] * 7 + [KVL + ROPE]

W_ALL = 15488
X_TOK = 0
F_GS, F_H, F_SQ, F_ACC, F_V, F_T = 6144, 7424, 8704, 9984, 11264, 11584
D_QT, D_KT, D_VTOK, D_CKT, D_CV, D_P, D_AT, D_DG, D_CST, D_O0 = (
    0, 1280, 2560, 4096, 6144, 8192, 10880, 11584, 12160, 14208)
D_VT, D_KTOK, D_O1 = D_AT, D_P, D_P
M_QN, M_QR, M_KN, M_VM, M_KR, M_P, M_AT, M_DG = 0, 2560, 3840, 7168, 10752, 11584, 12928, 14336
M_CQ, M_CKV, M_KRAW, M_SQ, M_V, M_Y, M_T, M_CTOK = 0, 3840, 4480, 4800, 6080, 6400, 6720, 9472
M_SQ2, M_CCT, M_CCKV, M_CKR, M_RT = 7168, 8192, 11584, 12608, 13120
PW = 1344
PH = SEQ + P
SEGS = [(0, SEQ), (PH, SEQ), (SEQ, P), (PH + SEQ, P), (2 * PH, KEYS)]
KV_COLS = [(0, 0, KVL + ROPE), (KVL + ROPE, KVL, ROPE)]
Y_TOK = 0


def build(nc, x_prompt, x_sample, cache_k, cache_v, cache_ckv, cache_kr,
          ffn1_norm, ffn1_gate, ffn1_up, ffn1_down, mix_norm, w_in,
          lq1, lk1, lq2, lk2, da_subln, q_norm, w_uq, kv_norm, w_ukv, w_out,
          ffn2_norm, ffn2_gate, ffn2_up, ffn2_down, final_norm, table,
          y_prompt, y_sample, k_prompt, v_prompt, ckv_prompt, kr_prompt,
          k_sample, v_sample, ckv_sample, kr_sample):
    ctx = ExitStack()
    with ctx:
        def sb(name, shape, dt):
            return ctx.enter_context(nc.sbuf_tensor(name, shape, dt))

        def sem(name):
            return ctx.enter_context(nc.semaphore(name))

        xT = sb("xT", [P, KT, T], F32)
        mov_hi = sb("mov_hi", [P, KT, T], F32R)
        mov_lo = sb("mov_lo", [P, KT, T], F32R)
        raw = sb("raw", [P, RAW_SLOTS, UK * UC], F32)
        w_hi = sb("w_hi", [P, SPLIT_SLOTS, UK * UC], F32R)
        w_lo = sb("w_lo", [P, SPLIT_SLOTS, UK * UC], F32R)
        h_hi = sb("h_hi", [P, 2 * NTOK], F32R)
        h_lo = sb("h_lo", [P, 2 * NTOK], F32R)
        work = sb("work", [P, W_ALL], F32)
        tab = sb("tab", [P, C_ALL], F32)
        ones = sb("ones", [P, P], F32)
        gains = sb("gains", [P, G_ALL], F32)
        rstd = sb("rstd", [P, T], F32)
        lamin = sb("lamin", [HALF, 6], F32)
        lam = sb("lam", [P, 10], F32)
        stat = sb("stat", [P, 2, 20], F32)
        ps = ctx.enter_context(nc.psum_tensor("ps", [P, 8, 512], F32))

        ident = tab[:, C_ID:C_ID + P]

        tab_in = sem("tab_in")
        gains_in = sem("gains_in")
        lam_in = sem("lam_in")
        x_in = [sem(f"x_in{i}") for i in range(3)]
        raw_in = [sem(f"raw_in{i}") for i in range(RAW_SLOTS)]
        ck_in = sem("ck_in")
        cv_in = sem("cv_in")
        cc_in = sem("cc_in")
        hi_done = sem("hi_done")
        lo_done = sem("lo_done")
        unit_used = sem("unit_used")
        drained = sem("drained")
        x_turned = sem("x_turned")
        x_copied = sem("x_copied")
        mov_hi_done = sem("mov_hi_done")
        mov_lo_done = sem("mov_lo_done")
        squared = sem("squared")
        sq_added = sem("sq_added")
        sum_ready = sem("sum_ready")
        mean_ready = sem("mean_ready")
        root_ready = sem("root_ready")
        rstd_ready = sem("rstd_ready")
        silu_done = sem("silu_done")
        gate_scaled = sem("gate_scaled")
        h_hi_done = sem("h_hi_done")
        h_lo_done = sem("h_lo_done")
        job_ready = sem("job_ready")
        job_drained = sem("job_drained")
        scores_ready = sem("scores_ready")
        biased = sem("biased")
        max_ready = sem("max_ready")
        exp_done = sem("exp_done")
        diag_ready = sem("diag_ready")
        at_ready = sem("at_ready")
        at_copied = sem("at_copied")
        o_ready = sem("o_ready")
        o_copied = sem("o_copied")
        o_hi_done = sem("o_hi_done")
        o_lo_done = sem("o_lo_done")
        lam_sq = sem("lam_sq")
        lam_sum = sem("lam_sum")
        lam_exp = sem("lam_exp")
        lam_ready = sem("lam_ready")
        n_sq = sem("n_sq")
        n_sum = sem("n_sum")
        n_mean = sem("n_mean")
        n_root = sem("n_root")
        n_out = sem("n_out")
        n_hi = sem("n_hi")
        n_lo = sem("n_lo")
        swap_ready = sem("swap_ready")
        roped = sem("roped")
        c_ready = sem("c_ready")
        stored = sem("stored")
        ctok_stored = sem("ctok_stored")
        y_stored = sem("y_stored")
        y_scaled = sem("y_scaled")
        ones_set = sem("ones_set")
        dve_chain = sem("dve_chain")
        act_chain = sem("act_chain")

        def wk(at, n, rows=slice(0, P)):
            return work[rows, at:at + n]

        def wk3(at, a, b, rows=slice(0, P)):
            return work[rows, at:at + a * b].rearrange("p (a b) -> p a b", a=a)

        def bank4(g):
            h = 4 * (g % 2)
            return ps[:, h:h + 4, 0:T]

        def over(ap, n):
            return ap.unsqueeze(1).to_broadcast([ap.shape[0], n, ap.shape[1]])

        def raw_value(n, i=0):
            more = sum(u <= n and u % RAW_SLOTS == n % RAW_SLOTS for u in range(U_UQ, U_UKV))
            return 16 * (n // RAW_SLOTS + 1 + 3 * more) + (12 // RAW_SLOTS) * 16 * i

        R4 = over(rstd[:, :], 4)

        def unit_cols(buf, slot, at, width):
            return buf[:, slot, :].rearrange("p (k c) -> p k c", k=UK)[:, :, at:at + width]

        def latents(buf):
            return buf[:, :].rearrange("p (k t) -> p k t", k=2)

        def score_seg(at, width):
            if at >= 768:
                return ps[:, 2:4, :].rearrange("p a b -> p (a b)")[:, at - 768:at - 768 + width]
            return ps[:, at // PH, at % PH:at % PH + width]

        def block_of(w, r0, c0, width=UC):
            return w[0, bass.ds(r0, UK * P), bass.ds(c0, width)].rearrange("(k p) c -> p k c", p=P)

        block = ctx.enter_context(nc.Block())

        @block.sync
        def _(sp):
            def load(n, i, src, width=UC):
                if n >= RAW_SLOTS:
                    sp.wait_ge(lo_done, n - RAW_SLOTS + 1 + 12 * i)
                dst = raw[:, n % RAW_SLOTS, :].rearrange("p (k c) -> p k c", k=UK)[:, :, 0:width]
                sp.dma_start(dst, src).then_inc(raw_in[n % RAW_SLOTS], 16)

            sp.dma_start(tab[:, :], table).then_inc(tab_in, 16)
            for t, (r0, rows) in enumerate(TOK):
                src = x_prompt[0, r0:r0 + rows, :] if t < 2 else x_sample[0]
                sp.dma_start(wk(X_TOK + t * D, D, slice(0, rows)), src).then_inc(x_in[t], 16)

            def ffn_loads(u0, gate, up, down):
                for q in range(4):
                    load(u0 + q, 0, block_of(gate, UC * q, 0))
                for q in range(4):
                    load(u0 + 4 + q, 0, block_of(up, UC * q, 0))
                with sp.Fori(0, PARTS - 1) as i:
                    for q in range(4):
                        load(u0 + 8 + q, i, block_of(gate, UC * q, i * UC + UC))
                    for q in range(4):
                        load(u0 + 12 + q, i, block_of(down, i * UC, UC * q))
                    for q in range(4):
                        load(u0 + 16 + q, i, block_of(up, UC * q, i * UC + UC))
                for q in range(4):
                    load(u0 + FFN_UNITS - 4 + q, 0, block_of(down, (PARTS - 1) * UC, UC * q))

            ffn_loads(0, ffn1_gate, ffn1_up, ffn1_down)

            def z_loads(z):
                for q in range(4):
                    load(U_Z + 4 * z + q, 0, block_of(w_in, UC * q, Z_COLS[z], Z_WIDTH[z]), Z_WIDTH[z])

            for z in range(8):
                z_loads(z)

            uq = w_uq[0].rearrange("(k p) (h c) -> p k h c", p=P, c=QKH)
            for j in range(3):
                n = U_UQ + j
                sp.wait_ge(lo_done, n - RAW_SLOTS + 1)
                for k in range(UK):
                    dst = raw[:, n % RAW_SLOTS, UC * k:UC * k + UC]
                    if j < 2:
                        dst = dst.rearrange("p (h c) -> p h c", c=DH)
                        src = uq[:, k, HB * j:HB * j + HB, 0:DH]
                    else:
                        dst = dst.rearrange("p (h c) -> p h c", c=ROPE)
                        src = uq[:, k, :, DH:QKH]
                    sp.dma_start(dst, src).then_inc(raw_in[n % RAW_SLOTS], 16)
            for hb in range(2):
                n = U_UKV + hb
                sp.wait_ge(lo_done, n - RAW_SLOTS + 1)
                sp.dma_start(raw[:, n % RAW_SLOTS, :].rearrange("p (k c) -> p k c", k=2),
                             w_ukv[0, :, 1024 * hb:1024 * hb + 1024].rearrange("(k p) c -> p k c", p=P)
                             ).then_inc(raw_in[n % RAW_SLOTS], 16)
            for n in range(4):
                for q in range(4):
                    m = U_OUT + 4 * n + q
                    sp.wait_ge(lo_done, m - RAW_SLOTS + 1)
                    sp.dma_start(raw[:, m % RAW_SLOTS, :].rearrange("p (k c) -> p k c", k=UK),
                                 block_of(w_out, UC * q, UC * n)).then_inc(raw_in[m % RAW_SLOTS], 16)
            ffn_loads(U_F2, ffn2_gate, ffn2_up, ffn2_down)
            for j in range(4):
                for t, (r0, rows) in enumerate(TOK):
                    sp.wait_ge(job_drained, JOB_Y + 3 * j + t + 1)
                    dst = (y_prompt[0, r0:r0 + rows, UC * j:UC * j + UC] if t < 2
                           else y_sample[0, :, UC * j:UC * j + UC])
                    sp.dma_start(dst, wk(Y_TOK + t * D + UC * j, UC, slice(0, rows))).then_inc(y_stored, 16)
            sp.wait_ge(y_stored, 16 * 12)
            sp.wait_ge(stored, 16 * 12)
            sp.wait_ge(ctok_stored, 16 * 6)

        @block.gpsimd
        def _(pool):
            for col, g, n in ((G_F1, ffn1_norm[0], KT), (G_MIX, mix_norm[0], KT), (G_F2, ffn2_norm[0], KT),
                              (G_FIN, final_norm, KT), (G_SUB, da_subln[0], 1), (G_Q, q_norm[0], 4),
                              (G_KV, kv_norm[0], 2)):
                pool.dma_start(gains[:, col:col + n], g.rearrange("(j p) -> p j", p=P),
                               allow_slow_non_contiguous=True).then_inc(gains_in, 16)
            for c, v in enumerate((lq1, lq2, lk1, lk2)):
                pool.dma_start(lamin[:, c:c + 1], v[0].rearrange("(p a) -> p a", a=1)).then_inc(lam_in, 16)
            pool.memset(ones[:, :], 1.0).then_inc(ones_set, 1)

            def add_squares(e):
                for q in range(1, 4):
                    pool.wait_ge(squared, 4 * e + q + 1)
                    if 3 * e + q - 1 > 0:
                        pool.wait_ge(sq_added, 3 * e + q - 1)
                    pool.tensor_tensor(wk(F_ACC, 4 * T), wk(F_ACC, 4 * T), wk(F_SQ, 4 * T),
                                       ALU.add).then_inc(sq_added, 1)

            def scale_gate(f, i):
                pool.wait_ge(silu_done, PARTS * f + 1 + i)
                pool.tensor_tensor(wk3(F_GS, 4, T), wk3(F_GS, 4, T), R4, ALU.mult).then_inc(gate_scaled, 1)

            def store_tokens(at, width, col, dst_prompt, dst_sample):
                for t, (r0, rows) in enumerate(TOK):
                    dst = (dst_prompt[r0:r0 + rows, col:col + width] if t < 2
                           else dst_sample[:, col:col + width])
                    pool.dma_start(dst, wk(at[t], width, slice(0, rows))).then_inc(stored, 16)

            kp = k_prompt[0, 0].rearrange("s h d -> s (h d)")
            ks = k_sample[0, 0].rearrange("s h d -> s (h d)")
            vp = v_prompt[0, 0].rearrange("s h d -> s (h d)")
            vs = v_sample[0, 0].rearrange("s h d -> s (h d)")
            ck = cache_k[0, 0].rearrange("s h d -> s (h d)").rearrange("(k p) c -> p k c", p=P)
            cv = cache_v[0, 0].rearrange("s h d -> s (h d)").rearrange("(k p) c -> p k c", p=P)

            def mix_traffic():
                for hf in range(2):
                    cols = slice(UC * hf, UC * hf + UC)
                    if hf == 0:
                        pool.wait_ge(mov_lo_done, 8)
                    else:
                        pool.wait_ge(n_out, 1)
                    pool.dma_start(wk3(D_CST, 4, UC), ck[:, :, cols]).then_inc(ck_in, 16)
                    pool.dma_start(wk3(D_CV, 4, UC), cv[:, :, cols]).then_inc(cv_in, 16)
                    pool.wait_ge(job_drained, 10 * hf + 3)
                    store_tokens([D_VTOK + UC * t for t in range(3)], UC, UC * hf, vp, vs)
                    pool.wait_ge(job_drained, 10 * hf + 6)
                    store_tokens([D_KTOK + UC * t for t in range(3)], UC, UC * hf, kp, ks)
                pool.wait_ge(o_copied, 8)
                pool.dma_start(wk3(M_CCKV, 4, KVL),
                             cache_ckv[0, 0].rearrange("(k p) c -> p k c", p=P)).then_inc(cc_in, 16)
                kr_src = cache_kr[0, 0].rearrange("(k p) c -> p k c", p=P)
                for half in range(2):
                    pool.dma_start(wk3(M_CKR, 4, P)[:, :, ROPE * half:ROPE * half + ROPE],
                                 kr_src).then_inc(cc_in, 16)

            add_squares(0)
            for f in range(2):
                scale_gate(f, 0)
                with pool.Fori(0, PARTS - 1) as i:
                    scale_gate(f, i + 1)
                add_squares(2 * f + 1)
                if f == 0:
                    mix_traffic()
                    add_squares(2)

        @block.scalar
        def _(act):
            def hi(n, i=0, cols=None):
                act.wait_ge(raw_in[n % RAW_SLOTS], raw_value(n, i))
                if n >= SPLIT_SLOTS:
                    act.wait_ge(unit_used, n - SPLIT_SLOTS + 1 + 12 * i)
                if cols is None:
                    act.copy(w_hi[:, n % SPLIT_SLOTS, :], raw[:, n % RAW_SLOTS, :]).then_inc(hi_done, 1)
                else:
                    for c, (to, at, w) in enumerate(cols):
                        last = act.copy(unit_cols(w_hi, n % SPLIT_SLOTS, to, w),
                                        unit_cols(raw, n % RAW_SLOTS, at, w))
                    last.then_inc(hi_done, 1)

            def next_hi(s, i=0):
                if s + 1 < U_END:
                    hi(s + 1, i, KV_COLS if U_Z + 28 <= s + 1 < U_Z + 32 else None)

            def moving_hi(e, q, col):
                for j in range(4 * q, 4 * q + 4):
                    last = act.activation(mov_hi[:, j, :], xT[:, j, :], ACT.Copy, scale=gains[:, col + j:col + j + 1])
                last.then_inc(mov_hi_done, 1)

            def square(e, q):
                if q >= 2:
                    act.wait_ge(sq_added, 3 * e + q - 1)
                act.activation(wk(F_ACC if q == 0 else F_SQ, 4 * T),
                               xT[:, 4 * q:4 * q + 4, :].rearrange("p a b -> p (a b)"),
                               ACT.Square).then_inc(squared, 1)

            def root(e):
                act.wait_ge(mean_ready, e + 1)
                act.activation(wk(F_T, T), wk(F_V, T), ACT.Sqrt).then_inc(root_ready, 1)

            def ffn(f, u0, g0):
                def silu(i):
                    act.wait_ge(drained, (g0 + 3 + 6 * (i - 1)) if not isinstance(i, int) else (g0 + 1))
                    act.activation(wk(F_GS, 4 * T), wk(F_GS, 4 * T), ACT.Silu).then_inc(silu_done, 1)

                def split_h(g, i):
                    act.wait_ge(drained, g + 1 + 6 * i)
                    act.copy(h_hi[:, 0:4 * T], wk(F_H, 4 * T)).then_inc(h_hi_done, 1)

                for j in range(8):
                    next_hi(u0 + j)
                    if j == 1:
                        root(2 * f)
                    if j == 3:
                        silu(0)
                split_h(g0 + 1, 0)
                with act.Fori(0, PARTS - 1) as i:
                    for j in range(12):
                        next_hi(u0 + 8 + j, i)
                        if j == 3:
                            silu(i + 1)
                    split_h(g0 + 7, i)
                for q in range(4):
                    next_hi(u0 + FFN_UNITS - 4 + q)
                    act.wait_ge(drained, g0 + FFN_GROUPS - 4 + q + 1)
                    if f == 0:
                        moving_hi(1, q, G_MIX)
                    square(2 * f + 1, q)

            act.wait_ge(gains_in, 16 * 7)
            for q in range(4):
                act.wait_ge(x_copied, 4 * q + 4)
                moving_hi(0, q, G_F1)
                square(0, q)
                if q == 1:
                    hi(0)
            ffn(0, 0, 0)

            def z_steps(z):
                for j in range(4):
                    next_hi(U_Z + 4 * z + j)
                    if z == 0 and j == 1:
                        root(1)

            def drain_job(n, dst, src):
                act.wait_ge(job_ready, n + 1)
                act.copy(dst, src).then_inc(job_drained, 1)

            def exps(c, src, p, scale):
                act.wait_ge(max_ready, c + 1)
                st = stat[:, c % 2, :]
                for k, (a, w) in enumerate(SEGS):
                    last = act.activation(wk(p + a, w), src(a, w), ACT.Exp, bias=st[:, 5 + k:6 + k],
                                          scale=scale, accum_out=st[:, 10 + k:11 + k])
                last.then_inc(exp_done, 1)

            def norm_root(k, v, y, n):
                act.wait_ge(n_mean, k)
                act.activation(wk(y, n), wk(v, n), ACT.Sqrt).then_inc(n_root, 1)

            for hf in range(2):
                for z in range(3 * hf, 3 * hf + 3):
                    z_steps(z)
                if hf == 0:
                    act.wait_ge(lam_sum, 1)
                    act.activation(lam[:, 0:2], ps[:, 7, 0:2], ACT.Exp).then_inc(lam_exp, 1)
                else:
                    act.wait_ge(stored, 16 * 6)
                for kind, at in ((0, D_VTOK), (3, D_KTOK)):
                    for t, (r0, rows) in enumerate(TOK):
                        n = 10 * hf + kind + t
                        drain_job(n, wk(at + UC * t, UC, slice(0, rows)), ps[0:rows, n % 8, :])
                for hh in range(HB):
                    n = 10 * hf + 6 + hh
                    drain_job(n, wk(D_CKT + PAST * hh, PAST), ps[:, n % 8, :])

                def da_exps(h):
                    p = D_P + PW * (h % 2)
                    exps(h, lambda a, w: wk(p + a, w), p, DA_SCALE)

                def da_copy(h):
                    act.wait_ge(at_ready, h + 1)
                    act.copy(wk(D_AT, 384), ps[:, 4, 0:384])
                    act.copy(wk(D_AT + 384, 256), ps[:, 5, 0:256])
                    act.copy(wk(D_AT + 640, 64, slice(0, 64)), ps[0:64, 5, 256:320]).then_inc(at_copied, 1)

                h0 = HB * hf
                da_exps(h0)
                for h in range(h0, h0 + HB):
                    if h + 1 < h0 + HB:
                        da_exps(h + 1)
                    da_copy(h)
                act.wait_ge(o_copied, h0 + HB)
                act.activation(wk(D_KT, 4 * T), wk(D_QT, 4 * T), ACT.Square).then_inc(n_sq, 1)
                norm_root(hf + 1, D_CKT, D_CV, 4 * T)
            z_steps(6)
            z_steps(7)
            act.wait_ge(unit_used, U_UQ)
            for hf, at in ((0, D_O0), (1, D_O1)):
                act.wait_ge(n_out, hf + 1)
                act.copy(mov_hi[:, 4 * hf:4 * hf + 4, :].rearrange("p a b -> p (a b)"),
                         wk(at, 4 * T)).then_inc(o_hi_done, 1)
            act.wait_ge(drained, GR_Z + 8)
            act.activation(wk(M_SQ, 4 * T), wk(M_CQ, 4 * T), ACT.Square).then_inc(n_sq, 1)
            act.activation(wk(M_SQ2, 2 * T), wk(M_CKV, 2 * T), ACT.Square).then_inc(n_sq, 1)
            act.wait_ge(o_lo_done, 2)
            drain_job(JOB_CC, wk(M_CCT, PAST), ps[:, JOB_CC % 8, :])
            drain_job(JOB_CC + 1, wk(M_CCT + PAST, PAST), ps[:, (JOB_CC + 1) % 8, :])
            drain_job(JOB_CC + 2, wk(M_KR + T, PAST), ps[:, (JOB_CC + 2) % 8, :])
            norm_root(3, M_V, M_Y, T)
            act.wait_ge(n_out, 3)
            act.copy(h_hi[:, 0:4 * T], wk(M_CQ, 4 * T)).then_inc(n_hi, 1)
            norm_root(4, M_V, M_Y, T)
            for t, (r0, rows) in enumerate(TOK):
                n = JOB_CTOK + t
                drain_job(n, wk(M_CTOK + T * t, T, slice(0, rows)), ps[0:rows, n % 8, 0:T])
            act.wait_ge(job_drained, JOB_CTOK + 3)
            for t, (r0, rows) in enumerate(TOK):
                dc = ckv_prompt[0, 0, r0:r0 + rows, :] if t < 2 else ckv_sample[0, 0]
                dk = kr_prompt[0, 0, r0:r0 + rows, :] if t < 2 else kr_sample[0, 0]
                at = M_CTOK + T * t
                act.dma_start(dc, wk(at, KVL, slice(0, rows))).then_inc(ctok_stored, 16)
                act.dma_start(dk, wk(at + KVL, ROPE, slice(0, rows))).then_inc(ctok_stored, 16)
            for j in range(3):
                next_hi(U_UQ + j)
            act.wait_ge(unit_used, U_UKV)
            act.copy(latents(h_hi)[:, :, 0:T], wk3(M_CKV, 2, T))
            act.copy(latents(h_hi)[:, :, T:NTOK], wk3(M_CCT, 2, PAST)).then_inc(n_hi, 1)

            for hb in range(2):
                next_hi(U_UKV + hb)
                jk = JOB_KV + 15 * hb
                for hh in range(HB):
                    for part, (t0, w) in enumerate(((0, T), (T, PAST))):
                        n = jk + 2 * hh + part
                        drain_job(n, wk(M_KN + NTOK * hh + t0, w), ps[:, n % 8, 0:w])
                act.wait_ge(ctok_stored, 16 * 6)
                for t in range(7):
                    n = jk + 8 + t
                    drain_job(n, wk(M_VM + UC * t, UC), ps[:, n % 8, :])

                def mla_exps(c):
                    act.wait_ge(at_ready, c)
                    exps(c, score_seg, M_P, MLA_SCALE)

                c0 = HEADS + 2 * hb
                mla_exps(c0)
                for c in (c0, c0 + 1):
                    if c == c0:
                        mla_exps(c + 1)
                    act.wait_ge(at_ready, c + 1)
                    act.copy(wk3(M_AT, 2, 384), ps[:, 4:6, 0:384])
                    act.copy(wk(M_AT + 768, 512), ps[:, 6, :])
                    act.copy(wk(M_AT + 1280, P, slice(0, 64)), ps[0:64, 7, 0:P]).then_inc(at_copied, 1)
                    act.wait_ge(o_ready, c + 1)
                    j = 2 * c - HEADS
                    act.copy(mov_hi[:, j:j + 2, :], ps[:, 4:6, 0:T]).then_inc(o_hi_done, 1)

            for n in range(4):
                for q in range(4):
                    next_hi(U_OUT + 4 * n + q)
                act.wait_ge(drained, GR_OUT + n + 1)
                square(2, n)
            act.wait_ge(unit_used, U_F2)
            for q in range(4):
                moving_hi(2, q, G_F2)
            ffn(1, U_F2, GR_F2)
            root(3)
            for j in range(4):
                for t, (r0, rows) in enumerate(TOK):
                    n = JOB_Y + 3 * j + t
                    drain_job(n, wk(Y_TOK + t * D + UC * j, UC, slice(0, rows)), ps[0:rows, n % 8, :])

        @block.vector
        def _(dve):
            chain = [0]

            def link(ins):
                chain[0] += 1
                ins.then_inc(dve_chain, 1)
                dve.wait_ge(dve_chain, chain[0])

            def lo(n, i=0, cols=None):
                dve.wait_ge(hi_done, n + 1 + 12 * i)
                if cols is None:
                    dve.tensor_tensor(w_lo[:, n % SPLIT_SLOTS, :], raw[:, n % RAW_SLOTS, :],
                                      w_hi[:, n % SPLIT_SLOTS, :].bitcast(F32), ALU.subtract).then_inc(lo_done, 1)
                else:
                    for to, at, w in cols:
                        last = dve.tensor_tensor(unit_cols(w_lo, n % SPLIT_SLOTS, to, w),
                                                 unit_cols(raw, n % RAW_SLOTS, at, w),
                                                 unit_cols(w_hi, n % SPLIT_SLOTS, to, w).bitcast(F32), ALU.subtract)
                    last.then_inc(lo_done, 1)

            def next_lo(s, i=0):
                if s + 1 < U_END:
                    lo(s + 1, i, KV_COLS if U_Z + 28 <= s + 1 < U_Z + 32 else None)

            def moving_lo(e, q, col):
                dve.wait_ge(mov_hi_done, 4 * e + q + 1)
                for j in range(4 * q, 4 * q + 4):
                    last = dve.scalar_tensor_tensor(mov_lo[:, j, :], xT[:, j, :], gains[:, col + j:col + j + 1],
                                                    mov_hi[:, j, :].bitcast(F32), ALU.mult, ALU.subtract)
                last.then_inc(mov_lo_done, 1)

            def newton(v, y, a, n):
                v, y, a = wk(v, n), wk(y, n), wk(a, n)
                link(dve.reciprocal(y, y))
                link(dve.tensor_tensor(a, y, y, ALU.mult))
                link(dve.tensor_tensor(a, a, v, ALU.mult))
                link(dve.tensor_scalar(a, a, -0.5, 1.5, ALU.mult, ALU.add))
                return y, a

            def norm(e, bank):
                dve.wait_ge(sum_ready, e + 1)
                dve.tensor_scalar(wk(F_V, T), ps[:, bank, 0:T], 1.0 / D, EPS, ALU.mult, ALU.add).then_inc(mean_ready, 1)
                dve.wait_ge(root_ready, e + 1)
                y, a = newton(F_V, F_T, F_SQ, T)
                dve.tensor_tensor(rstd[:, :], y, a, ALU.mult).then_inc(rstd_ready, 1)
                dve.wait_ge(rstd_ready, e + 1)

            def ffn(f, u0, g0):
                def drain_gate(s, i, g):
                    dve.wait_ge(unit_used, s + 1 + 12 * i)
                    dve.tensor_tensor(wk3(F_GS, 4, T), bank4(g), R4, ALU.mult).then_inc(drained, 1)

                def drain_up(s, i, g, part):
                    dve.wait_ge(unit_used, s + 1 + 12 * i)
                    dve.wait_ge(gate_scaled, PARTS * f + 1 + part)
                    dve.tensor_tensor(wk3(F_H, 4, T), bank4(g), wk3(F_GS, 4, T), ALU.mult).then_inc(drained, 1)
                    dve.wait_ge(h_hi_done, PARTS * f + 1 + part)
                    dve.tensor_tensor(h_lo[:, 0:4 * T], wk(F_H, 4 * T), h_hi[:, 0:4 * T].bitcast(F32),
                                      ALU.subtract).then_inc(h_lo_done, 1)

                def drain_down(s, i, g, q):
                    dve.wait_ge(unit_used, s + 1 + 12 * i)
                    dve.scalar_tensor_tensor(xT[:, 4 * q:4 * q + 4, :], bank4(g), 0.5, xT[:, 4 * q:4 * q + 4, :],
                                             ALU.mult, ALU.add).then_inc(drained, 1)

                for j in range(8):
                    next_lo(u0 + j)
                    if j == 1:
                        norm(2 * f, 4 * ((g0 + 1) % 2))
                    if j == 3:
                        drain_gate(u0 + 3, 0, g0)
                drain_up(u0 + 7, 0, g0 + 1, 0)
                with dve.Fori(0, PARTS - 1) as i:
                    for j in range(12):
                        s = u0 + 8 + j
                        next_lo(s, i)
                        if j == 3:
                            drain_gate(s, i, g0 + 2)
                        if 4 <= j < 8:
                            drain_down(s, i, g0 + 3 + j - 4, j - 4)
                    drain_up(u0 + 19, i, g0 + 7, i + 1)
                for q in range(4):
                    s = u0 + FFN_UNITS - 4 + q
                    next_lo(s)
                    drain_down(s, 0, g0 + FFN_GROUPS - 4 + q, q)
                    if f == 0 and q > 0:
                        moving_lo(1, q - 1, G_MIX)
                if f == 0:
                    moving_lo(1, 3, G_MIX)

            for q in range(4):
                for j in range(4 * q, 4 * q + 4):
                    dve.wait_ge(x_turned, j + 1)
                    dve.tensor_copy(xT[:, j, :], ps[:, j % 8, 0:T]).then_inc(x_copied, 1)
                if q > 0:
                    if q == 1:
                        dve.wait_ge(gains_in, 16 * 7)
                    moving_lo(0, q - 1, G_F1)
                if q == 2:
                    lo(0)
            moving_lo(0, 3, G_F1)
            ffn(0, 0, 0)

            def z_steps(z, dst, tiles=4):
                for j in range(4):
                    s = U_Z + 4 * z + j
                    next_lo(s)
                    if z == 0 and j == 1:
                        norm(1, 4 * ((GR_Z + 1) % 2))
                dve.wait_ge(unit_used, s + 1)
                dve.tensor_tensor(wk3(dst, tiles, T), bank4(GR_Z + z)[:, 0:tiles, :], over(rstd[:, :], tiles),
                                  ALU.mult).then_inc(drained, 1)

            def inverse_sums(c):
                dve.wait_ge(exp_done, c + 1)
                st = stat[:, c % 2, :]
                link(dve.reciprocal(st[:, 15:20], st[:, 10:15]))
                return st

            def maxes(c, prompt, sample, scale):
                st = stat[:, c % 2, :]
                dve.tensor_reduce(st[:, 0:2], prompt[:, :, 0:SEQ], AX_X, ALU.max)
                dve.tensor_reduce(st[:, 2:4], prompt[:, :, SEQ:PH], AX_X, ALU.max)
                link(dve.tensor_reduce(st[:, 4:5], sample, AX_X, ALU.max))
                dve.tensor_scalar(st[:, 5:10], st[:, 0:5], -scale, None, ALU.mult).then_inc(max_ready, 1)

            for hf in range(2):
                z_steps(3 * hf, D_QT)
                z_steps(3 * hf + 1, D_KT)
                z_steps(3 * hf + 2, D_VT)
                if hf == 0:
                    dve.wait_ge(lam_in, 16 * 4)
                    dve.tensor_tensor(lamin[:, 4:6], lamin[:, 0:2], lamin[:, 2:4], ALU.mult).then_inc(lam_sq, 1)
                    dve.tensor_scalar(gains[:, G_SUB:G_SUB + 1], gains[:, G_SUB:G_SUB + 1], 1.0 - LAM_INIT, None,
                                      ALU.mult)
                    link(dve.memset(lam[:, 5:10], 1.0))
                    dve.wait_ge(lam_exp, 1)
                    link(dve.scalar_tensor_tensor(lam[:, 6:7], lam[:, 1:2], LAM_INIT, lam[:, 0:1],
                                                  ALU.subtract, ALU.subtract))
                    dve.tensor_copy(lam[:, 8:9], lam[:, 6:7])
                    link(dve.tensor_copy(lam[64:128, 9:10], lam[64:128, 6:7]))

                def bias_and_max(h):
                    p = D_P + PW * (h % 2)
                    s8 = -SLOPES[h] / DA_SCALE
                    dve.wait_ge(scores_ready, h + 1)
                    dve.wait_ge(stored, 16 * 6 * (hf + 1))
                    if h >= 2:
                        dve.wait_ge(at_ready, h - 1)
                    dve.scalar_tensor_tensor(wk3(p, 2, PH), over(tab[:, C_DIST:C_DIST + PH], 2), s8,
                                             ps[:, 0:2, 0:PH], ALU.mult, ALU.add)
                    dve.scalar_tensor_tensor(wk(p + 768, KEYS), tab[:, C_DISTS:C_DISTS + KEYS], s8,
                                             score_seg(768, KEYS), ALU.mult, ALU.add).then_inc(biased, 1)
                    dve.wait_ge(biased, h + 1)
                    maxes(h, wk3(p, 2, PH), wk(p + 2 * PH, KEYS), DA_SCALE)

                def da_diag(h):
                    st = inverse_sums(h)
                    link(dve.tensor_tensor(st[:, 15:20], st[:, 15:20], lam[:, 5:10], ALU.mult))
                    if h >= 1:
                        dve.wait_ge(at_ready, h)
                    for k in range(4):
                        dve.tensor_scalar(wk(D_DG + P * k, P), ident, st[:, 15 + k:16 + k], None, ALU.mult)
                    dve.tensor_scalar(wk(D_DG + 512, 64), tab[:, C_STACK:C_STACK + 64], st[:, 19:20], None,
                                      ALU.mult).then_inc(diag_ready, 1)

                def copy_o(h):
                    dve.wait_ge(o_ready, h + 1)
                    dve.tensor_copy(wk(D_QT + T * (h % HB), T), ps[:, 6 + h % 2, 0:T]).then_inc(o_copied, 1)

                h0 = HB * hf
                bias_and_max(h0)
                for h in range(h0, h0 + HB):
                    if h + 1 < h0 + HB:
                        bias_and_max(h + 1)
                    da_diag(h)
                    if h > h0:
                        copy_o(h - 1)
                copy_o(h0 + HB - 1)
                dve.wait_ge(n_sum, hf + 1)
                dve.tensor_scalar(wk3(D_CKT, 4, T), ps[:, 0:4, 0:T], 1.0 / DH, EPS, ALU.mult,
                                  ALU.add).then_inc(n_mean, 1)
                dve.wait_ge(n_root, hf + 1)
                y, a = newton(D_CKT, D_CV, D_KT, 4 * T)
                link(dve.tensor_tensor(y, y, a, ALU.mult))
                dve.scalar_tensor_tensor(wk(D_O1 if hf else D_O0, 4 * T), wk(D_QT, 4 * T), gains[:, G_SUB:G_SUB + 1],
                                         y, ALU.mult, ALU.mult).then_inc(n_out, 1)
            z_steps(6, M_CQ)
            z_steps(7, M_CKV, 3)
            for hf, at in ((0, D_O0), (1, D_O1)):
                dve.wait_ge(o_hi_done, hf + 1)
                sl = slice(4 * hf, 4 * hf + 4)
                dve.tensor_tensor(mov_lo[:, sl, :].rearrange("p a b -> p (a b)"), wk(at, 4 * T),
                                  mov_hi[:, sl, :].rearrange("p a b -> p (a b)").bitcast(F32),
                                  ALU.subtract).then_inc(o_lo_done, 1)

            def latent_norm(k, bank, at, tiles, col):
                dve.wait_ge(n_sum, k)
                dve.tensor_scalar(wk(M_V, T), ps[:, bank, 0:T], 1.0 / (P * tiles), EPS, ALU.mult,
                                  ALU.add).then_inc(n_mean, 1)
                dve.wait_ge(n_root, k)
                y, a = newton(M_V, M_Y, M_T, T)
                link(dve.tensor_tensor(y, y, a, ALU.mult))
                for j in range(tiles):
                    last = dve.scalar_tensor_tensor(wk(at + T * j, T), wk(at + T * j, T),
                                                    gains[:, col + j:col + j + 1], y, ALU.mult, ALU.mult)
                last.then_inc(n_out, 1)

            latent_norm(3, 0, M_CQ, 4, G_Q)
            dve.wait_ge(n_hi, 1)
            dve.tensor_tensor(h_lo[:, 0:4 * T], wk(M_CQ, 4 * T), h_hi[:, 0:4 * T].bitcast(F32),
                              ALU.subtract).then_inc(n_lo, 1)
            latent_norm(4, 1, M_CKV, 2, G_KV)
            cos, sin = tab[:, C_COS:C_COS + T], tab[:, C_SIN:C_SIN + T]
            dve.wait_ge(swap_ready, 1)
            dve.tensor_tensor(wk(M_RT, T), wk(M_KRAW, T), cos, ALU.mult)
            link(dve.tensor_tensor(wk(M_RT + T, T), ps[:, 2, 0:T], sin, ALU.mult))
            dve.tensor_tensor(wk(M_KR, T), wk(M_RT, T), wk(M_RT + T, T), ALU.add).then_inc(roped, 1)
            for j in range(3):
                next_lo(U_UQ + j)
                dve.wait_ge(unit_used, U_UQ + j + 1)
                dve.tensor_copy(wk3((M_QN, M_QN + 4 * T, M_QR)[j], 4, T), bank4(GR_UQ + j)).then_inc(drained, 1)
            dve.wait_ge(drained, GR_UQ + 3)
            dve.wait_ge(swap_ready, 2)
            dve.tensor_tensor(wk3(M_QR, 4, T), wk3(M_QR, 4, T), over(cos, 4), ALU.mult)
            link(dve.tensor_tensor(wk3(M_RT, 4, T), ps[:, 4:8, 0:T], over(sin, 4), ALU.mult))
            dve.tensor_tensor(wk(M_QR, 4 * T), wk(M_QR, 4 * T), wk(M_RT, 4 * T), ALU.add).then_inc(roped, 1)
            dve.wait_ge(n_hi, 2)
            dve.tensor_tensor(latents(h_lo)[:, :, 0:T], wk3(M_CKV, 2, T), latents(h_hi)[:, :, 0:T].bitcast(F32),
                              ALU.subtract)
            dve.tensor_tensor(latents(h_lo)[:, :, T:NTOK], wk3(M_CCT, 2, PAST),
                              latents(h_hi)[:, :, T:NTOK].bitcast(F32), ALU.subtract).then_inc(n_lo, 1)

            def mask_and_max(c):
                dve.wait_ge(scores_ready, c + 1)
                for end in (SEQ, PH):
                    hidden = ps[0:64, 0:2, end - 64:end]
                    ins = dve.tensor_scalar(hidden, hidden, NEG, None, ALU.add)
                link(ins)
                maxes(c, ps[:, 0:2, 0:PH], score_seg(2 * PH, KEYS), MLA_SCALE)

            def mla_diag(c):
                st = inverse_sums(c)
                dve.wait_ge(at_ready, c)
                for k in range(5):
                    ins = dve.tensor_scalar(wk(M_DG + P * k, P), ident, st[:, 15 + k:16 + k], None, ALU.mult)
                ins.then_inc(diag_ready, 1)

            for hb in range(2):
                next_lo(U_UKV + hb)
                c0 = HEADS + 2 * hb
                mask_and_max(c0)
                for c in (c0, c0 + 1):
                    if c == c0:
                        mask_and_max(c + 1)
                    mla_diag(c)
                    j = 2 * c - HEADS
                    dve.wait_ge(o_hi_done, c - HEADS + 3)
                    dve.tensor_tensor(mov_lo[:, j:j + 2, :], ps[:, 4:6, 0:T], mov_hi[:, j:j + 2, :].bitcast(F32),
                                      ALU.subtract).then_inc(o_lo_done, 1)

            for n in range(4):
                for q in range(4):
                    next_lo(U_OUT + 4 * n + q)
                dve.wait_ge(unit_used, U_OUT + 4 * n + 4)
                dve.tensor_tensor(xT[:, 4 * n:4 * n + 4, :], bank4(GR_OUT + n), xT[:, 4 * n:4 * n + 4, :],
                                  ALU.add).then_inc(drained, 1)
            for q in range(4):
                moving_lo(2, q, G_F2)
            ffn(1, U_F2, GR_F2)
            norm(3, 0)
            for j in range(KT):
                dve.scalar_tensor_tensor(xT[:, j, :], xT[:, j, :], gains[:, G_FIN + j:G_FIN + j + 1], rstd[:, :],
                                         ALU.mult, ALU.mult).then_inc(y_scaled, 1)

        @block.tensor
        def _(pe):
            def triple(out, w, x, first, last):
                pe.matmul(out, w[0], x[0], start=first, stop=False)
                pe.matmul(out, w[0], x[1], start=False, stop=False)
                return pe.matmul(out, w[1], x[0], start=False, stop=last)

            def unit(n, i, g, gi, moving, first, last, tiles=4):
                pe.wait_ge(lo_done, n + 1 + 12 * i)
                if first and g >= 2:
                    pe.wait_ge(drained, g - 1 + gi)
                out = bank4(g)
                for m in range(tiles):
                    for k in range(UK):
                        c = UC * k + P * m
                        w = (w_hi[:, n % SPLIT_SLOTS, c:c + P], w_lo[:, n % SPLIT_SLOTS, c:c + P])
                        ins = triple(out[:, m, :], w, moving(k), first and k == 0, last and k == UK - 1)
                ins.then_inc(unit_used, 1)

            def mov(q):
                return lambda k: (mov_hi[:, 4 * q + k, :], mov_lo[:, 4 * q + k, :])

            def hidden(k):
                return (h_hi[:, T * k:T * k + T], h_lo[:, T * k:T * k + T])

            def add_up(e, bank):
                pe.wait_ge(sq_added, 3 * e + 3)
                for a in range(4):
                    ins = pe.matmul(ps[:, bank, 0:T], ones[:, :], wk(F_ACC + T * a, T), start=(a == 0), stop=(a == 3))
                ins.then_inc(sum_ready, 1)

            def from_x(u, i, g, gi, e=None):
                for q in range(4):
                    if e is not None:
                        pe.wait_ge(mov_lo_done, 4 * e + q + 1)
                        if q == 2:
                            pe.wait_ge(drained, g) if g else None
                            add_up(e if e < 2 else 2, 4 * ((g + 1) % 2))
                    unit(u + q, i, g, gi, mov(q), q == 0, q == 3)

            def ffn(f, u0, g0):
                from_x(u0, 0, g0, 0, 2 * f)
                pe.wait_ge(mean_ready, 2 * f + 1)
                from_x(u0 + 4, 0, g0 + 1, 0)
                with pe.Fori(0, PARTS - 1) as i:
                    from_x(u0 + 8, i, g0 + 2, 6 * i)
                    pe.wait_ge(h_lo_done, PARTS * f + 1 + i)
                    for q in range(4):
                        unit(u0 + 12 + q, i, g0 + 3 + q, 6 * i, hidden, True, True)
                    from_x(u0 + 16, i, g0 + 7, 6 * i)
                pe.wait_ge(h_lo_done, PARTS * f + PARTS)
                for q in range(4):
                    unit(u0 + FFN_UNITS - 4 + q, 0, g0 + FFN_GROUPS - 4 + q, 0, hidden, True, True)

            pe.wait_ge(tab_in, 16)
            for t in range(3):
                pe.wait_ge(x_in[t], 16)
            for j in range(KT):
                if j >= 8:
                    pe.wait_ge(x_copied, j - 7)
                for t, (r0, rows) in enumerate(TOK):
                    ins = pe.transpose(ps[:, j % 8, r0:r0 + rows], wk(X_TOK + t * D + P * j, P, slice(0, rows)),
                                       tab[0:rows, C_ID:C_ID + rows])
                ins.then_inc(x_turned, 1)
            pe.wait_ge(ones_set, 1)
            pe.wait_ge(x_copied, KT)
            ffn(0, 0, 0)

            def z_group(z):
                g = GR_Z + z
                for q in range(4):
                    n = U_Z + 4 * z + q
                    if z == 0:
                        pe.wait_ge(mov_lo_done, 4 + q + 1)
                        if q == 2:
                            pe.wait_ge(drained, g)
                            add_up(1, 4 * ((g + 1) % 2))
                    if z == 1 and q == 0:
                        pe.wait_ge(mean_ready, 2)
                    unit(n, 0, g, 0, mov(q), q == 0, q == 3, 4 if z < 7 else 3)

            for hf in range(2):
                if hf:
                    pe.wait_ge(n_mean, 1)
                for z in range(3 * hf, 3 * hf + 3):
                    z_group(z)
                pe.wait_ge(drained, GR_Z + 3 * hf + 3)
                if hf == 0:
                    pe.wait_ge(lam_sq, 1)
                    pe.matmul(ps[:, 7, 0:2], ones[0:HALF, :], lamin[:, 4:6], start=True, stop=True).then_inc(lam_sum, 1)
                    pe.wait_ge(lam_exp, 1)
                for kind, at in ((0, D_VT), (3, D_KT)):
                    for t, (r0, rows) in enumerate(TOK):
                        n = 10 * hf + kind + t
                        if n >= 8:
                            pe.wait_ge(job_drained, n - 7)
                        for hh in range(HB):
                            ins = pe.transpose(ps[0:rows, n % 8, P * hh:P * hh + P], wk(at + T * hh + r0, rows), ident)
                        ins.then_inc(job_ready, 1)
                pe.wait_ge(ck_in, 16 * (hf + 1))
                for hh in range(HB):
                    n = 10 * hf + 6 + hh
                    if n >= 8:
                        pe.wait_ge(job_drained, n - 7)
                    for kt in range(4):
                        ins = pe.transpose(ps[:, n % 8, P * kt:P * kt + P], wk(D_CST + UC * kt + P * hh, P), ident)
                    ins.then_inc(job_ready, 1)

                def da_scores(h):
                    if h > HB * hf:
                        pe.wait_ge(biased, h)
                    hh = h % HB
                    for half in range(2):
                        d = slice(HALF * half, HALF * half + HALF)
                        q, k = wk(D_QT + T * hh, T, d), wk(D_KT + T * hh, T, d)
                        pe.matmul(ps[:, half, 0:SEQ], q[:, P:SEQ], k[:, 0:SEQ], start=True, stop=True)
                        pe.matmul(ps[:, half, SEQ:PH], q[:, 0:P], k[:, 0:P], start=True, stop=True)
                        pe.matmul(ps[d, 2, :], q[:, SEQ:T], wk(D_CKT + PAST * hh, PAST, d), start=True, stop=True)
                        ins = pe.matmul(ps[d, 3, 0:DEC], q[:, SEQ:T], k[:, SEQ:T], start=True, stop=True)
                    ins.then_inc(scores_ready, 1)

                def da_transpose(h):
                    pe.wait_ge(diag_ready, h + 1)
                    p = D_P + PW * (h % 2)
                    dg = [wk(D_DG + P * k, P) for k in range(4)]
                    for col, at, k in ((0, SEQ, 2), (P, 0, 0), (SEQ, P, 0)):
                        out = ps[:, 4, col:col + P]
                        pe.matmul(out, wk(p + at, P), dg[k], start=True, stop=False)
                        pe.matmul(out, wk(p + at + PH, P), dg[k + 1], start=False, stop=True)
                    for kt in range(5):
                        rows = P if kt < 4 else DEC
                        ins = pe.matmul(ps[0:rows, 5, 64 * kt:64 * kt + 64], wk(p + 768 + P * kt, rows),
                                        wk(D_DG + 512, 64), start=True, stop=True)
                    ins.then_inc(at_ready, 1)

                def da_values(h):
                    pe.wait_ge(at_copied, h + 1)
                    if h == HB * hf:
                        pe.wait_ge(cv_in, 16 * (hf + 1))
                    if h >= 2:
                        pe.wait_ge(o_copied, h - 1)
                    out = ps[:, 6 + h % 2, :]
                    hd = P * (h % HB)
                    pe.matmul(out[:, 0:SEQ], wk(D_VTOK + hd, P), wk(D_AT, SEQ), start=True, stop=False)
                    pe.matmul(out[:, P:SEQ], wk(D_VTOK + UC + hd, P), wk(D_AT + SEQ, P), start=False, stop=True)
                    for kt in range(4):
                        pe.matmul(out[:, SEQ:T], wk(D_CV + UC * kt + hd, P), wk(D_AT + 384 + 64 * kt, 64),
                                  start=(kt == 0), stop=False)
                    new = slice(0, DEC)
                    pe.matmul(out[:, SEQ:T], wk(D_VTOK + 2 * UC + hd, P, new), wk(D_AT + 640, 64, new),
                              start=False, stop=True).then_inc(o_ready, 1)

                h0 = HB * hf
                pe.wait_ge(job_drained, 10 * hf + 10)
                da_scores(h0)
                for h in range(h0, h0 + HB):
                    if h + 1 < h0 + HB:
                        da_scores(h + 1)
                    da_transpose(h)
                    da_values(h)
                pe.wait_ge(n_sq, hf + 1)
                for a in range(4):
                    ins = pe.matmul(ps[:, a, 0:T], ones[:, :], wk(D_KT + T * a, T), start=True, stop=True)
                ins.then_inc(n_sum, 1)
            pe.wait_ge(n_mean, 2)
            z_group(6)
            z_group(7)
            pe.wait_ge(drained, GR_Z + 8)
            pe.wait_ge(cc_in, 16 * 3)
            for a in range(2):
                for kt in range(4):
                    ins = pe.transpose(ps[:, (JOB_CC + a) % 8, P * kt:P * kt + P],
                                       wk(M_CCKV + KVL * kt + P * a, P), ident)
                ins.then_inc(job_ready, 1)
            for kt in range(4):
                ins = pe.transpose(ps[:, (JOB_CC + 2) % 8, P * kt:P * kt + P], wk(M_CKR + P * kt, P), ident)
            ins.then_inc(job_ready, 1)
            swap = tab[:, C_SWAP:C_SWAP + P]
            pe.matmul(ps[:, 2, 0:T], swap, wk(M_KRAW, T), start=True, stop=True).then_inc(swap_ready, 1)
            for bank, at, tiles in ((0, M_SQ, 4), (1, M_SQ2, 2)):
                pe.wait_ge(n_sq, 3 + bank)
                for a in range(tiles):
                    ins = pe.matmul(ps[:, bank, 0:T], ones[:, :], wk(at + T * a, T), start=(a == 0),
                                    stop=(a == tiles - 1))
                ins.then_inc(n_sum, 1)
            pe.wait_ge(n_out, 4)
            pe.wait_ge(roped, 1)
            for t, (r0, rows) in enumerate(TOK):
                b = (JOB_CTOK + t) % 8
                for a in range(2):
                    pe.transpose(ps[0:rows, b, P * a:P * a + P], wk(M_CKV + T * a + r0, rows), ident)
                pe.transpose(ps[0:rows, b, KVL:KVL + ROPE], wk(M_KR + r0, rows, slice(0, ROPE)),
                             tab[0:ROPE, C_ID:C_ID + ROPE]).then_inc(job_ready, 1)
            pe.wait_ge(job_drained, JOB_CTOK + 3)
            pe.wait_ge(n_lo, 1)
            for j in range(3):
                unit(U_UQ + j, 0, GR_UQ + j, 0, hidden, True, True)
            pe.wait_ge(drained, GR_UQ + 3)
            for a in range(4):
                ins = pe.matmul(ps[:, 4 + a, 0:T], swap, wk(M_QR + T * a, T), start=True, stop=True)
            ins.then_inc(swap_ready, 1)
            pe.wait_ge(roped, 2)
            pe.wait_ge(n_lo, 2)

            for hb in range(2):
                n = U_UKV + hb
                jk = JOB_KV + 15 * hb
                pe.wait_ge(lo_done, n + 1)

                def start_job(j):
                    if j - jk >= 8:
                        pe.wait_ge(job_drained, j - 7)

                def wslice(k, hh, v):
                    c = 1024 * k + 256 * hh + P * v
                    return (w_hi[:, n % SPLIT_SLOTS, c:c + P], w_lo[:, n % SPLIT_SLOTS, c:c + P])

                for hh in range(HB):
                    for part, (t0, w) in enumerate(((0, T), (T, PAST))):
                        j = jk + 2 * hh + part
                        start_job(j)
                        for k in range(2):
                            c = (latents(h_hi)[:, k, t0:t0 + w], latents(h_lo)[:, k, t0:t0 + w])
                            ins = triple(ps[:, j % 8, 0:w], wslice(k, hh, 0), c, k == 0, k == 1)
                        ins.then_inc(job_ready, 1)
                for t, t0 in enumerate((0, P, SEQ, T, T + P, T + 2 * P, T + 3 * P)):
                    j = jk + 8 + t
                    start_job(j)
                    for k in range(2):
                        c = (latents(h_hi)[:, k, t0:t0 + P], latents(h_lo)[:, k, t0:t0 + P])
                        wv = [w[:, n % SPLIT_SLOTS, :].rearrange("p (k h v c) -> p k h v c", k=2, h=4, v=2)[:, k, :, 1, :]
                              for w in (w_hi, w_lo)]
                        ins = triple(ps[:, j % 8, :].rearrange("p (h c) -> p h c", h=4), c, wv, k == 0, k == 1)
                    ins.then_inc(job_ready, 1)

                def mla_scores(c):
                    if c > HEADS + 2 * hb:
                        pe.wait_ge(exp_done, c)
                    pr = c - HEADS
                    for half in range(2):
                        d = slice(64 * half, 64 * half + 64)
                        qn = wk(M_QN + T * (2 * pr + half), T)
                        kn = wk(M_KN + NTOK * (2 * (pr % 2) + half), NTOK)
                        qr, kr = wk(M_QR + T * pr, T, d), wk(M_KR, NTOK, d)
                        for out, q, k in ((ps[:, half, 0:SEQ], slice(P, SEQ), slice(0, SEQ)),
                                          (ps[:, half, SEQ:PH], slice(0, P), slice(0, P)),
                                          (ps[d, 2, :], slice(SEQ, T), slice(T, NTOK)),
                                          (ps[d, 3, 0:DEC], slice(SEQ, T), slice(SEQ, T))):
                            ins = pe.matmul(out, qn[:, q], kn[:, k], start=True, stop=False)
                            if c == HEADS + 2 * hb and half == 0 and k.stop == SEQ:
                                ins.then_inc(unit_used, 1)
                            ins = pe.matmul(out, qr[:, q], kr[:, k], start=False, stop=True)
                    ins.then_inc(scores_ready, 1)

                def mla_transpose(c):
                    pe.wait_ge(diag_ready, c + 1)
                    pe.wait_ge(o_lo_done, c - HEADS + 2)
                    dg = [wk(M_DG + P * k, P) for k in range(5)]
                    for half in range(2):
                        for col, at, k in ((0, PH * half + SEQ, 2), (P, PH * half, 0), (SEQ, PH * half + P, 0)):
                            pe.matmul(ps[:, 4 + half, col:col + P], wk(M_P + at, P), dg[k + half], start=True, stop=True)
                    for kt in range(4):
                        pe.matmul(ps[:, 6, P * kt:P * kt + P], wk(M_P + 768 + P * kt, P), dg[4], start=True, stop=True)
                    pe.matmul(ps[0:DEC, 7, 0:P], wk(M_P + 768 + PAST, DEC), dg[4], start=True,
                              stop=True).then_inc(at_ready, 1)

                def mla_values(c):
                    pe.wait_ge(at_copied, c + 1)
                    for half in range(2):
                        out = ps[:, 4 + half, :]
                        hd = P * (2 * ((c - HEADS) % 2) + half)
                        at = M_AT + 384 * half
                        pe.matmul(out[:, 0:SEQ], wk(M_VM + hd, P), wk(at, SEQ), start=True, stop=False)
                        pe.matmul(out[:, P:SEQ], wk(M_VM + UC + hd, P), wk(at + SEQ, P), start=False, stop=True)
                        for kt in range(4):
                            pe.matmul(out[:, SEQ:T], wk(M_VM + UC * (3 + kt) + hd, P),
                                      wk(M_AT + 768 + P * kt + 64 * half, 64), start=(kt == 0), stop=False)
                        new = slice(0, DEC)
                        ins = pe.matmul(out[:, SEQ:T], wk(M_VM + 2 * UC + hd, P, new),
                                        wk(M_AT + 1280 + 64 * half, 64, new), start=False, stop=True)
                    ins.then_inc(o_ready, 1)

                pe.wait_ge(job_drained, jk + 15)
                c0 = HEADS + 2 * hb
                mla_scores(c0)
                for c in (c0, c0 + 1):
                    if c == c0:
                        mla_scores(c + 1)
                    mla_transpose(c)
                    mla_values(c)
                pe.wait_ge(o_lo_done, 2 * hb + 4)

            for n in range(4):
                for q in range(4):
                    unit(U_OUT + 4 * n + q, 0, GR_OUT + n, 0, mov(q), q == 0, q == 3)
            ffn(1, U_F2, GR_F2)
            pe.wait_ge(drained, GR_F2 + FFN_GROUPS)
            add_up(3, 0)
            pe.wait_ge(mean_ready, 4)
            for j in range(4):
                pe.wait_ge(y_scaled, 4 * j + 4)
                for t, (r0, rows) in enumerate(TOK):
                    n = JOB_Y + 3 * j + t
                    if 3 * j + t >= 8:
                        pe.wait_ge(job_drained, n - 7)
                    for a in range(4):
                        ins = pe.transpose(ps[0:rows, n % 8, P * a:P * a + P], xT[:, 4 * j + a, r0:r0 + rows], ident)
                    ins.then_inc(job_ready, 1)


def constants():
    f = np.float32
    p = np.arange(P)
    pos = np.concatenate([np.arange(SEQ), PAST + np.arange(DEC)]).astype(f)
    half = ROPE // 2
    inv = f(ROPE_THETA) ** (-np.arange(half, dtype=f) / f(half))
    ang = pos[None, :] * inv[p % half][:, None]
    sign = np.where(p % ROPE < half, -1.0, 1.0)[:, None]
    q1, k1 = (P + p)[:, None], np.arange(SEQ)[None, :]
    dist = np.where(k1 // CHUNK <= q1 // CHUNK, np.abs(q1 - k1), BIG)
    dists = np.abs(PAST + (p % DEC)[:, None] - np.arange(KEYS)[None, :])
    stack = p[:, None] % HALF == np.arange(HALF)[None, :]
    swap = (p[:, None] ^ half) == p[None, :]
    return np.concatenate([np.eye(P), stack, swap, np.cos(ang), sign * np.sin(ang), dist, dist[:, P:], dists],
                          axis=1).astype(f)


_INS = ["x_prompt", "x_sample", "cache_da_k", "cache_da_v", "cache_mla_ckv", "cache_mla_krope",
        "ffn1_norm", "ffn1_w_gate", "ffn1_w_up", "ffn1_w_down", "mix_norm", "w_in",
        "da_lambda_q1", "da_lambda_k1", "da_lambda_q2", "da_lambda_k2", "da_subln",
        "mla_q_norm", "mla_w_uq", "mla_kv_norm", "mla_w_ukv", "w_out",
        "ffn2_norm", "ffn2_w_gate", "ffn2_w_up", "ffn2_w_down", "final_norm"]
_OUTS = [(1, SEQ, D), (1, DEC, D),
         (1, 1, SEQ, HEADS, DH), (1, 1, SEQ, HEADS, DH), (1, 1, SEQ, KVL), (1, 1, SEQ, ROPE),
         (1, 1, DEC, HEADS, DH), (1, 1, DEC, HEADS, DH), (1, 1, DEC, KVL), (1, 1, DEC, ROPE)]


def kernel(**inputs):
    import concourse.bacc as bacc
    from concourse.bass_utils import run_bass_kernel_spmd

    nc = bacc.Bacc("TRN2", target_bir_lowering=False, num_devices=1)
    arrays = {f"in_{name}": np.ascontiguousarray(inputs[name]) for name in _INS}
    arrays["in_table"] = constants()
    args = [nc.dram_tensor(name, a.shape, F32, kind="ExternalInput").ap() for name, a in arrays.items()]
    args += [nc.dram_tensor(f"out_{i}", shape, F32, kind="ExternalOutput").ap() for i, shape in enumerate(_OUTS)]
    build(nc, *args)
    r = run_bass_kernel_spmd(nc, [arrays], core_ids=[0])
    return tuple(r.results[0][f"out_{i}"] for i in range(len(_OUTS)))
```

```python
from contextlib import ExitStack

import numpy as np

import concourse.bass as bass
from concourse import mybir

F32 = mybir.dt.float32
F32R = mybir.dt.float32r
ALU = mybir.AluOpType
ACT = mybir.ActivationFunctionType
AX_X = mybir.AxisListType.X

P = 128
D = 2048
KT = D // P
SEQ = 256
DEC = 64
T = SEQ + DEC
PAST = 512
CHUNK = 64
KEYS = PAST + DEC
F = 5632
UC = 512
UK = 4
PARTS = F // UC
HEADS = 8
DH = 128
HALF = 64
QL = 512
KVL = 256
ROPE = 64
QKH = DH + ROPE
ROPE_THETA = 10000.0
EPS = 1e-6
LAM_INIT = 0.2
JOB_CC, JOB_CTOK, JOB_KV = 20, 23, 26
DA_SCALE = HALF ** -0.5
MLA_SCALE = QKH ** -0.5
NEG = -1e30
BIG = 1e30
SLOPES = [2.0 ** (-8.0 * (i + 1) / HEADS) for i in range(HEADS)]
HB = 4
RAW_SLOTS = 4
SPLIT_SLOTS = 2
TOK = [(0, P), (P, P), (SEQ, DEC)]
NTOK = T + PAST
Y_JOBS = [(j, t, r0, rows) for j in range(4) for t, (r0, rows) in enumerate(TOK)]

C_ID, C_STACK, C_SWAP = 0, 128, 192
C_COS, C_SIN, C_DIST, C_DISTS, C_ALL = 320, 640, 960, 1344, 1920

G_F1, G_MIX, G_F2, G_FIN, G_SUB, G_Q, G_KV, G_ALL = 0, 16, 32, 48, 64, 65, 69, 71

FFN_UNITS, FFN_GROUPS = 12 * PARTS, 6 * PARTS
U_Z = FFN_UNITS
U_UQ = U_Z + 32
U_UKV = U_UQ + 3
U_OUT = U_UKV + 2
U_F2 = U_OUT + 16
U_END = U_F2 + FFN_UNITS
GR_Z = FFN_GROUPS
H_STEPS = PARTS - 1 + 4
GR_UQ = GR_Z + 8
GR_OUT = GR_UQ + 3
GR_F2 = GR_OUT + 4

Z_COLS = [0, 1024, 2048, 512, 1536, 2560, 3072, 3584]
Z_WIDTH = [UC] * 7 + [KVL + ROPE]

W_ALL = 15488
X_TOK, S_ROWS, S_LROWS = 0, 11904, 12032
F_GS, F_H, F_SQ, F_ACC, F_V, F_T = 6144, 7424, 8704, 9984, 11264, 11584
D_QT, D_KT, D_VTOK, D_CKT, D_CV, D_P, D_AT, D_DG, D_CST, D_O0 = (
    0, 1280, 2560, 4096, 6144, 8192, 10880, 11584, 12160, 14208)
D_VT, D_KTOK, D_O1 = D_AT, D_P, D_P
M_QN, M_QR, M_KN, M_VM, M_KR, M_P, M_AT, M_DG = 0, 2560, 3840, 7168, 10752, 11584, 12928, 14336
M_CQ, M_CKV, M_KRAW, M_SQ, M_V, M_Y, M_T, M_CTOK = 0, 3840, 4480, 4800, 6080, 6400, 6720, 9472
M_SQ2, M_CCT, M_CCKV, M_CKR, M_RT = 7168, 8192, 11584, 12608, 13120
PW = 1344
PH = SEQ + P
SEGS = [(0, SEQ), (PH, SEQ), (SEQ, P), (PH + SEQ, P), (2 * PH, KEYS)]
KV_COLS = [(0, 0, KVL + ROPE), (KVL + ROPE, KVL, ROPE)]
Y_TOK = 0


def build(nc, x_prompt, x_sample, cache_k, cache_v, cache_ckv, cache_kr,
          ffn1_norm, ffn1_gate, ffn1_up, ffn1_down, mix_norm, w_in,
          lq1, lk1, lq2, lk2, da_subln, q_norm, w_uq, kv_norm, w_ukv, w_out,
          ffn2_norm, ffn2_gate, ffn2_up, ffn2_down, final_norm, table,
          y_prompt, y_sample, k_prompt, v_prompt, ckv_prompt, kr_prompt,
          k_sample, v_sample, ckv_sample, kr_sample):
    ctx = ExitStack()
    with ctx:
        def sb(name, shape, dt):
            return ctx.enter_context(nc.sbuf_tensor(name, shape, dt))

        def sem(name):
            return ctx.enter_context(nc.semaphore(name))

        xT = sb("xT", [P, KT, T], F32)
        mov_hi = sb("mov_hi", [P, KT, T], F32R)
        mov_lo = sb("mov_lo", [P, KT, T], F32R)
        raw = sb("raw", [P, RAW_SLOTS, UK * UC], F32)
        w_hi = sb("w_hi", [P, SPLIT_SLOTS, UK * UC], F32R)
        w_lo = sb("w_lo", [P, SPLIT_SLOTS, UK * UC], F32R)
        h_hi = sb("h_hi", [P, 2 * NTOK], F32R)
        h_lo = sb("h_lo", [P, 2 * NTOK], F32R)
        work = sb("work", [P, W_ALL], F32)
        tab = sb("tab", [P, C_ALL], F32)
        ones = sb("ones", [P, P], F32)
        gains = sb("gains", [P, G_ALL], F32)
        rstd = sb("rstd", [P, T], F32)
        lamin = sb("lamin", [HALF, 6], F32)
        lam = sb("lam", [P, 10], F32)
        tok = sb("tok", [P, 12], F32)
        stat = sb("stat", [P, 2, 20], F32)
        ps = ctx.enter_context(nc.psum_tensor("ps", [P, 8, 512], F32))

        ident = tab[:, C_ID:C_ID + P]

        id_in = sem("id_in")
        tab_in = sem("tab_in")
        gains_in = sem("gains_in")
        gains_turned = sem("gains_turned")
        gains_set = sem("gains_set")
        lam_in = sem("lam_in")
        x_in = [sem(f"x_in{i}") for i in range(3)]
        raw_in = [sem(f"raw_in{i}") for i in range(RAW_SLOTS)]
        ck_in = sem("ck_in")
        cv_in = sem("cv_in")
        cc_in = sem("cc_in")
        hi_done = sem("hi_done")
        lo_done = sem("lo_done")
        unit_used = sem("unit_used")
        drained = sem("drained")
        x_turned = sem("x_turned")
        x_copied = sem("x_copied")
        mov_hi_done = sem("mov_hi_done")
        mov_lo_done = sem("mov_lo_done")
        squared = sem("squared")
        sq_added = sem("sq_added")
        sum_ready = sem("sum_ready")
        mean_ready = sem("mean_ready")
        root_ready = sem("root_ready")
        rstd_ready = sem("rstd_ready")
        silu_done = sem("silu_done")
        gate_scaled = sem("gate_scaled")
        h_tile = sem("h_tile")
        h_hi_done = sem("h_hi_done")
        h_lo_done = sem("h_lo_done")
        job_ready = sem("job_ready")
        job_drained = sem("job_drained")
        scores_ready = sem("scores_ready")
        biased = sem("biased")
        max_ready = sem("max_ready")
        exp_done = sem("exp_done")
        diag_ready = sem("diag_ready")
        at_ready = sem("at_ready")
        at_copied = sem("at_copied")
        o_ready = sem("o_ready")
        o_copied = sem("o_copied")
        o_hi_done = sem("o_hi_done")
        o_lo_done = sem("o_lo_done")
        lam_sq = sem("lam_sq")
        lam_sum = sem("lam_sum")
        lam_exp = sem("lam_exp")
        lam_ready = sem("lam_ready")
        n_sq = sem("n_sq")
        n_sum = sem("n_sum")
        n_mean = sem("n_mean")
        n_root = sem("n_root")
        n_out = sem("n_out")
        n_hi = sem("n_hi")
        n_lo = sem("n_lo")
        swap_ready = sem("swap_ready")
        roped = sem("roped")
        c_ready = sem("c_ready")
        stored = sem("stored")
        ctok_stored = sem("ctok_stored")
        y_stored = sem("y_stored")
        y_scaled = sem("y_scaled")
        tok_set = sem("tok_set")
        tok_sum = sem("tok_sum")
        tok_mean = sem("tok_mean")
        tok_root = sem("tok_root")
        tok_rstd = sem("tok_rstd")
        y_turned = sem("y_turned")
        y_even = sem("y_even")
        y_odd = sem("y_odd")
        ones_set = sem("ones_set")
        dve_chain = sem("dve_chain")
        act_chain = sem("act_chain")

        def wk(at, n, rows=slice(0, P)):
            return work[rows, at:at + n]

        def wk3(at, a, b, rows=slice(0, P)):
            return work[rows, at:at + a * b].rearrange("p (a b) -> p a b", a=a)

        def x_bank(j):
            return j if j < 4 else 4 + j % 4

        def y_bank(n):
            return (4, 5, 6, 0, 1, 2, 3)[n % 7]

        def bank4(g):
            h = 4 * (g % 2)
            return ps[:, h:h + 4, 0:T]

        def over(ap, n):
            return ap.unsqueeze(1).to_broadcast([ap.shape[0], n, ap.shape[1]])

        def raw_value(n, i=0):
            more = sum(u <= n and u % RAW_SLOTS == n % RAW_SLOTS for u in range(U_UQ, U_UKV))
            return 16 * (n // RAW_SLOTS + 1 + 3 * more) + (12 // RAW_SLOTS) * 16 * i

        R4 = over(rstd[:, :], 4)

        def unit_cols(buf, slot, at, width):
            return buf[:, slot, :].rearrange("p (k c) -> p k c", k=UK)[:, :, at:at + width]

        def latents(buf):
            return buf[:, :].rearrange("p (k t) -> p k t", k=2)

        def score_seg(at, width):
            if at >= 768:
                return ps[:, 2:4, :].rearrange("p a b -> p (a b)")[:, at - 768:at - 768 + width]
            return ps[:, at // PH, at % PH:at % PH + width]

        def block_of(w, r0, c0, width=UC):
            return w[0, bass.ds(r0, UK * P), bass.ds(c0, width)].rearrange("(k p) c -> p k c", p=P)

        block = ctx.enter_context(nc.Block())

        @block.sync
        def _(sp):
            def load(n, i, src, width=UC):
                if n >= RAW_SLOTS:
                    sp.wait_ge(lo_done, n - RAW_SLOTS + 1 + 12 * i)
                dst = raw[:, n % RAW_SLOTS, :].rearrange("p (k c) -> p k c", k=UK)[:, :, 0:width]
                sp.dma_start(dst, src).then_inc(raw_in[n % RAW_SLOTS], 16)

            sp.dma_start(tab[:, 0:C_STACK], table[:, 0:C_STACK]).then_inc(id_in, 16)
            for t, (r0, rows) in enumerate(TOK):
                src = x_prompt[0, r0:r0 + rows, :] if t < 2 else x_sample[0]
                sp.dma_start(wk(X_TOK + t * D, D, slice(0, rows)), src).then_inc(x_in[t], 16)
            for col, g, n in ((G_F1, ffn1_norm[0], KT), (G_MIX, mix_norm[0], KT), (G_F2, ffn2_norm[0], KT),
                              (G_FIN, final_norm, KT), (G_SUB, da_subln[0], 1), (G_Q, q_norm[0], 4),
                              (G_KV, kv_norm[0], 2)):
                sp.dma_start(wk(S_ROWS, P, slice(col, col + n)),
                              g.rearrange("(j p) -> j p", p=P)).then_inc(gains_in, 16)
            for c, v in enumerate((lq1, lq2, lk1, lk2)):
                sp.dma_start(wk(S_LROWS, HALF, slice(c, c + 1)), v).then_inc(lam_in, 16)

            def ffn_loads(u0, gate, up, down):
                for q in range(4):
                    load(u0 + q, 0, block_of(gate, UC * q, 0))
                if u0 == 0:
                    sp.dma_start(tab[:, C_STACK:C_ALL], table[:, C_STACK:C_ALL]).then_inc(tab_in, 16)
                for q in range(4):
                    load(u0 + 4 + q, 0, block_of(up, UC * q, 0))
                with sp.Fori(0, PARTS - 1) as i:
                    for q in range(4):
                        load(u0 + 8 + q, i, block_of(gate, UC * q, i * UC + UC))
                    for q in range(4):
                        load(u0 + 12 + q, i, block_of(down, i * UC, UC * q))
                    for q in range(4):
                        load(u0 + 16 + q, i, block_of(up, UC * q, i * UC + UC))
                for q in range(4):
                    load(u0 + FFN_UNITS - 4 + q, 0, block_of(down, (PARTS - 1) * UC, UC * q))

            ffn_loads(0, ffn1_gate, ffn1_up, ffn1_down)

            def z_loads(z):
                for q in range(4):
                    load(U_Z + 4 * z + q, 0, block_of(w_in, UC * q, Z_COLS[z], Z_WIDTH[z]), Z_WIDTH[z])

            for z in range(8):
                z_loads(z)

            uq = w_uq[0].rearrange("(k p) (h c) -> p k h c", p=P, c=QKH)
            for j in range(3):
                n = U_UQ + j
                sp.wait_ge(lo_done, n - RAW_SLOTS + 1)
                for k in range(UK):
                    dst = raw[:, n % RAW_SLOTS, UC * k:UC * k + UC]
                    if j < 2:
                        dst = dst.rearrange("p (h c) -> p h c", c=DH)
                        src = uq[:, k, HB * j:HB * j + HB, 0:DH]
                    else:
                        dst = dst.rearrange("p (h c) -> p h c", c=ROPE)
                        src = uq[:, k, :, DH:QKH]
                    sp.dma_start(dst, src).then_inc(raw_in[n % RAW_SLOTS], 16)
            for hb in range(2):
                n = U_UKV + hb
                sp.wait_ge(lo_done, n - RAW_SLOTS + 1)
                sp.dma_start(raw[:, n % RAW_SLOTS, :].rearrange("p (k c) -> p k c", k=2),
                             w_ukv[0, :, 1024 * hb:1024 * hb + 1024].rearrange("(k p) c -> p k c", p=P)
                             ).then_inc(raw_in[n % RAW_SLOTS], 16)
            for n in range(4):
                for q in range(4):
                    m = U_OUT + 4 * n + q
                    sp.wait_ge(lo_done, m - RAW_SLOTS + 1)
                    sp.dma_start(raw[:, m % RAW_SLOTS, :].rearrange("p (k c) -> p k c", k=UK),
                                 block_of(w_out, UC * q, UC * n)).then_inc(raw_in[m % RAW_SLOTS], 16)
            ffn_loads(U_F2, ffn2_gate, ffn2_up, ffn2_down)
            for n, (j, t, r0, rows) in enumerate(Y_JOBS):
                sp.wait_ge(y_odd if n % 2 else y_even, n // 2 + 1)
                dst = (y_prompt[0, r0:r0 + rows, UC * j:UC * j + UC] if t < 2
                       else y_sample[0, :, UC * j:UC * j + UC])
                sp.dma_start(dst, wk(Y_TOK + t * D + UC * j, UC, slice(0, rows))).then_inc(y_stored, 16)
            sp.wait_ge(y_stored, 16 * 12)
            sp.wait_ge(stored, 16 * 12)
            sp.wait_ge(ctok_stored, 16 * 6)

        @block.gpsimd
        def _(pool):
            pool.memset(ones[:, :], 1.0).then_inc(ones_set, 1)

            def add_squares(e):
                for q in range(1, 4 if e < 3 else 3):
                    pool.wait_ge(squared, 4 * e + q + 1)
                    if 3 * e + q - 1 > 0:
                        pool.wait_ge(sq_added, 3 * e + q - 1)
                    pool.tensor_tensor(wk(F_ACC, 4 * T), wk(F_ACC, 4 * T), wk(F_SQ, 4 * T),
                                       ALU.add).then_inc(sq_added, 1)

            def scale_gate(f, i):
                pool.wait_ge(silu_done, PARTS * f + 1 + i)
                pool.tensor_tensor(wk3(F_GS, 4, T), wk3(F_GS, 4, T), R4, ALU.mult).then_inc(gate_scaled, 1)

            def store_tokens(at, width, col, dst_prompt, dst_sample):
                for t, (r0, rows) in enumerate(TOK):
                    dst = (dst_prompt[r0:r0 + rows, col:col + width] if t < 2
                           else dst_sample[:, col:col + width])
                    pool.dma_start(dst, wk(at[t], width, slice(0, rows))).then_inc(stored, 16)

            kp = k_prompt[0, 0].rearrange("s h d -> s (h d)")
            ks = k_sample[0, 0].rearrange("s h d -> s (h d)")
            vp = v_prompt[0, 0].rearrange("s h d -> s (h d)")
            vs = v_sample[0, 0].rearrange("s h d -> s (h d)")
            ck = cache_k[0, 0].rearrange("s h d -> s (h d)").rearrange("(k p) c -> p k c", p=P)
            cv = cache_v[0, 0].rearrange("s h d -> s (h d)").rearrange("(k p) c -> p k c", p=P)

            def mix_traffic():
                for hf in range(2):
                    cols = slice(UC * hf, UC * hf + UC)
                    if hf == 0:
                        pool.wait_ge(mov_lo_done, 8)
                    else:
                        pool.wait_ge(n_out, 1)
                    pool.dma_start(wk3(D_CST, 4, UC), ck[:, :, cols]).then_inc(ck_in, 16)
                    pool.dma_start(wk3(D_CV, 4, UC), cv[:, :, cols]).then_inc(cv_in, 16)
                    pool.wait_ge(job_drained, 10 * hf + 3)
                    store_tokens([D_VTOK + UC * t for t in range(3)], UC, UC * hf, vp, vs)
                    pool.wait_ge(job_drained, 10 * hf + 6)
                    store_tokens([D_KTOK + UC * t for t in range(3)], UC, UC * hf, kp, ks)
                pool.wait_ge(o_copied, 8)
                pool.dma_start(wk3(M_CCKV, 4, KVL),
                             cache_ckv[0, 0].rearrange("(k p) c -> p k c", p=P)).then_inc(cc_in, 16)
                kr_src = cache_kr[0, 0].rearrange("(k p) c -> p k c", p=P)
                for half in range(2):
                    pool.dma_start(wk3(M_CKR, 4, P)[:, :, ROPE * half:ROPE * half + ROPE],
                                 kr_src).then_inc(cc_in, 16)

            pool.wait_ge(x_copied, 4)
            pool.tensor_tensor(wk3(F_ACC, 4, T), xT[:, 0:4, :], xT[:, 0:4, :], ALU.mult).then_inc(squared, 1)
            pool.wait_ge(x_copied, 8)
            pool.tensor_tensor(wk3(F_SQ, 4, T), xT[:, 4:8, :], xT[:, 4:8, :], ALU.mult).then_inc(squared, 1)
            add_squares(0)
            for f in range(2):
                scale_gate(f, 0)
                with pool.Fori(0, PARTS - 1) as i:
                    scale_gate(f, i + 1)
                add_squares(2 * f + 1)
                if f == 0:
                    mix_traffic()
                    add_squares(2)

        @block.scalar
        def _(act):
            def hi(n, i=0, cols=None):
                act.wait_ge(raw_in[n % RAW_SLOTS], raw_value(n, i))
                if n >= SPLIT_SLOTS:
                    act.wait_ge(unit_used, n - SPLIT_SLOTS + 1 + 12 * i)
                if cols is None:
                    act.copy(w_hi[:, n % SPLIT_SLOTS, :], raw[:, n % RAW_SLOTS, :]).then_inc(hi_done, 1)
                else:
                    for c, (to, at, w) in enumerate(cols):
                        last = act.copy(unit_cols(w_hi, n % SPLIT_SLOTS, to, w),
                                        unit_cols(raw, n % RAW_SLOTS, at, w))
                    last.then_inc(hi_done, 1)

            def next_hi(s, i=0):
                if s + 1 < U_END:
                    hi(s + 1, i, KV_COLS if U_Z + 28 <= s + 1 < U_Z + 32 else None)

            def moving_hi(e, q, col):
                for j in range(4 * q, 4 * q + 4):
                    last = act.activation(mov_hi[:, j, :], xT[:, j, :], ACT.Copy, scale=gains[:, col + j:col + j + 1])
                last.then_inc(mov_hi_done, 1)

            def square(e, q):
                if q >= 2:
                    act.wait_ge(sq_added, 3 * e + q - 1)
                act.activation(wk(F_ACC if q == 0 else F_SQ, 4 * T),
                               xT[:, 4 * q:4 * q + 4, :].rearrange("p a b -> p (a b)"),
                               ACT.Square).then_inc(squared, 1)

            def root(e):
                act.wait_ge(mean_ready, e + 1)
                act.activation(wk(F_T, T), wk(F_V, T), ACT.Sqrt).then_inc(root_ready, 1)

            def ffn(f, u0, g0):
                def silu(i):
                    act.wait_ge(drained, (g0 + 3 + 6 * (i - 1)) if not isinstance(i, int) else (g0 + 1))
                    act.activation(wk(F_GS, 4 * T), wk(F_GS, 4 * T), ACT.Silu).then_inc(silu_done, 1)

                def split_h(g, i):
                    act.wait_ge(drained, g + 1 + 6 * i)
                    act.copy(h_hi[:, 0:4 * T], wk(F_H, 4 * T)).then_inc(h_hi_done, 1)

                for j in range(8):
                    next_hi(u0 + j)
                    if f == 0 and j == 0:
                        first_moving_hi(2)
                        square(0, 2)
                        first_moving_hi(3)
                        square(0, 3)
                    if j == 2:
                        root(2 * f)
                    if j == 4:
                        silu(0)
                with act.Fori(0, PARTS - 1) as i:
                    for j in range(12):
                        next_hi(u0 + 8 + j, i)
                        if j == 0:
                            split_h(g0 + 1, i)
                        if j == 4:
                            silu(i + 1)
                for k in range(4):
                    if k < 3:
                        act.wait_ge(h_tile, 3 * (PARTS * (f + 1) - 1) + k + 1)
                    else:
                        act.wait_ge(drained, g0 + FFN_GROUPS - 4)
                    act.copy(h_hi[:, T * k:T * k + T], wk(F_H + T * k, T)).then_inc(h_hi_done, 1)
                for q in range(4):
                    next_hi(u0 + FFN_UNITS - 4 + q)
                    act.wait_ge(drained, g0 + FFN_GROUPS - 4 + q + 1)
                    if f == 0:
                        moving_hi(1, q, G_MIX)
                    if f == 1 and q == 0:
                        act.wait_ge(tok_set, 1)
                        act.activation(tok[:, 11:12], tok[:, 10:11], ACT.Sqrt)
                    square(2 * f + 1, q)

            act.wait_ge(gains_set, 1)
            def first_moving_hi(q):
                act.wait_ge(x_copied, 4 * q + 4)
                moving_hi(0, q, G_F1)

            first_moving_hi(0)
            hi(0)
            first_moving_hi(1)
            ffn(0, 0, 0)

            def z_steps(z):
                for j in range(4):
                    next_hi(U_Z + 4 * z + j)
                    if z == 0 and j == 2:
                        root(1)

            def drain_job(n, dst, src):
                act.wait_ge(job_ready, n + 1)
                act.copy(dst, src).then_inc(job_drained, 1)

            def exps(c, src, p, scale):
                act.wait_ge(max_ready, c + 1)
                st = stat[:, c % 2, :]
                for k, (a, w) in enumerate(SEGS):
                    last = act.activation(wk(p + a, w), src(a, w), ACT.Exp, bias=st[:, 5 + k:6 + k],
                                          scale=scale, accum_out=st[:, 10 + k:11 + k])
                last.then_inc(exp_done, 1)

            def norm_root(k, v, y, n):
                act.wait_ge(n_mean, k)
                act.activation(wk(y, n), wk(v, n), ACT.Sqrt).then_inc(n_root, 1)

            for hf in range(2):
                for z in range(3 * hf, 3 * hf + 3):
                    z_steps(z)
                if hf == 0:
                    act.wait_ge(lam_sum, 1)
                    act.activation(lam[:, 0:2], ps[:, 7, 0:2], ACT.Exp).then_inc(lam_exp, 1)
                else:
                    act.wait_ge(stored, 16 * 6)
                for kind, at in ((0, D_VTOK), (3, D_KTOK)):
                    for t, (r0, rows) in enumerate(TOK):
                        n = 10 * hf + kind + t
                        drain_job(n, wk(at + UC * t, UC, slice(0, rows)), ps[0:rows, n % 8, :])
                for hh in range(HB):
                    n = 10 * hf + 6 + hh
                    drain_job(n, wk(D_CKT + PAST * hh, PAST), ps[:, n % 8, :])

                def da_exps(h):
                    p = D_P + PW * (h % 2)
                    exps(h, lambda a, w: wk(p + a, w), p, DA_SCALE)

                def da_copy(h):
                    act.wait_ge(at_ready, h + 1)
                    act.copy(wk(D_AT, 384), ps[:, 4, 0:384])
                    act.copy(wk(D_AT + 384, 256), ps[:, 5, 0:256])
                    act.copy(wk(D_AT + 640, 64, slice(0, 64)), ps[0:64, 5, 256:320]).then_inc(at_copied, 1)

                h0 = HB * hf
                da_exps(h0)
                for h in range(h0, h0 + HB):
                    if h + 1 < h0 + HB:
                        da_exps(h + 1)
                    da_copy(h)
                act.wait_ge(o_copied, h0 + HB)
                act.activation(wk(D_KT, 4 * T), wk(D_QT, 4 * T), ACT.Square).then_inc(n_sq, 1)
                norm_root(hf + 1, D_CKT, D_CV, 4 * T)
            z_steps(6)
            z_steps(7)
            act.wait_ge(unit_used, U_UQ)
            for hf, at in ((0, D_O0), (1, D_O1)):
                act.wait_ge(n_out, hf + 1)
                act.copy(mov_hi[:, 4 * hf:4 * hf + 4, :].rearrange("p a b -> p (a b)"),
                         wk(at, 4 * T)).then_inc(o_hi_done, 1)
            act.wait_ge(drained, GR_Z + 8)
            act.activation(wk(M_SQ, 4 * T), wk(M_CQ, 4 * T), ACT.Square).then_inc(n_sq, 1)
            act.activation(wk(M_SQ2, 2 * T), wk(M_CKV, 2 * T), ACT.Square).then_inc(n_sq, 1)
            act.wait_ge(o_lo_done, 2)
            drain_job(JOB_CC, wk(M_CCT, PAST), ps[:, JOB_CC % 8, :])
            drain_job(JOB_CC + 1, wk(M_CCT + PAST, PAST), ps[:, (JOB_CC + 1) % 8, :])
            drain_job(JOB_CC + 2, wk(M_KR + T, PAST), ps[:, (JOB_CC + 2) % 8, :])
            norm_root(3, M_V, M_Y, T)
            act.wait_ge(n_out, 3)
            act.copy(h_hi[:, 0:4 * T], wk(M_CQ, 4 * T)).then_inc(n_hi, 1)
            norm_root(4, M_V, M_Y, T)
            for t, (r0, rows) in enumerate(TOK):
                n = JOB_CTOK + t
                drain_job(n, wk(M_CTOK + T * t, T, slice(0, rows)), ps[0:rows, n % 8, 0:T])
            act.wait_ge(job_drained, JOB_CTOK + 3)
            for t, (r0, rows) in enumerate(TOK):
                dc = ckv_prompt[0, 0, r0:r0 + rows, :] if t < 2 else ckv_sample[0, 0]
                dk = kr_prompt[0, 0, r0:r0 + rows, :] if t < 2 else kr_sample[0, 0]
                at = M_CTOK + T * t
                act.dma_start(dc, wk(at, KVL, slice(0, rows))).then_inc(ctok_stored, 16)
                act.dma_start(dk, wk(at + KVL, ROPE, slice(0, rows))).then_inc(ctok_stored, 16)
            for j in range(3):
                next_hi(U_UQ + j)
            act.wait_ge(unit_used, U_UKV)
            act.copy(latents(h_hi)[:, :, 0:T], wk3(M_CKV, 2, T))
            act.copy(latents(h_hi)[:, :, T:NTOK], wk3(M_CCT, 2, PAST)).then_inc(n_hi, 1)

            for hb in range(2):
                next_hi(U_UKV + hb)
                jk = JOB_KV + 15 * hb
                for hh in range(HB):
                    for part, (t0, w) in enumerate(((0, T), (T, PAST))):
                        n = jk + 2 * hh + part
                        drain_job(n, wk(M_KN + NTOK * hh + t0, w), ps[:, n % 8, 0:w])
                act.wait_ge(ctok_stored, 16 * 6)
                for t in range(7):
                    n = jk + 8 + t
                    drain_job(n, wk(M_VM + UC * t, UC), ps[:, n % 8, :])

                def mla_exps(c):
                    act.wait_ge(at_ready, c)
                    exps(c, score_seg, M_P, MLA_SCALE)

                c0 = HEADS + 2 * hb
                mla_exps(c0)
                for c in (c0, c0 + 1):
                    if c == c0:
                        mla_exps(c + 1)
                    act.wait_ge(at_ready, c + 1)
                    act.copy(wk3(M_AT, 2, 384), ps[:, 4:6, 0:384])
                    act.copy(wk(M_AT + 768, 512), ps[:, 6, :])
                    act.copy(wk(M_AT + 1280, P, slice(0, 64)), ps[0:64, 7, 0:P]).then_inc(at_copied, 1)
                    act.wait_ge(o_ready, c + 1)
                    j = 2 * c - HEADS
                    act.copy(mov_hi[:, j:j + 2, :], ps[:, 4:6, 0:T]).then_inc(o_hi_done, 1)

            for n in range(4):
                for q in range(4):
                    next_hi(U_OUT + 4 * n + q)
                act.wait_ge(drained, GR_OUT + n + 1)
                square(2, n)
            act.wait_ge(unit_used, U_F2)
            for q in range(4):
                moving_hi(2, q, G_F2)
            ffn(1, U_F2, GR_F2)
            act.wait_ge(tok_mean, 1)
            act.activation(tok[:, 3:6], tok[:, 0:3], ACT.Sqrt).then_inc(tok_root, 1)
            act.wait_ge(tok_rstd, 1)
            for n, (j, t, r0, rows) in enumerate(Y_JOBS):
                if n % 2 == 0:
                    act.wait_ge(y_turned, n + 1)
                    act.activation(wk(Y_TOK + t * D + UC * j, UC, slice(0, rows)), ps[0:rows, y_bank(n), :], ACT.Copy,
                                   scale=tok[0:rows, 6 + t:7 + t]).then_inc(y_even, 1)

        @block.vector
        def _(dve):
            chain = [0]

            def link(ins):
                chain[0] += 1
                ins.then_inc(dve_chain, 1)
                dve.wait_ge(dve_chain, chain[0])

            def lo(n, i=0, cols=None):
                dve.wait_ge(hi_done, n + 1 + 12 * i)
                if cols is None:
                    dve.tensor_tensor(w_lo[:, n % SPLIT_SLOTS, :], raw[:, n % RAW_SLOTS, :],
                                      w_hi[:, n % SPLIT_SLOTS, :].bitcast(F32), ALU.subtract).then_inc(lo_done, 1)
                else:
                    for to, at, w in cols:
                        last = dve.tensor_tensor(unit_cols(w_lo, n % SPLIT_SLOTS, to, w),
                                                 unit_cols(raw, n % RAW_SLOTS, at, w),
                                                 unit_cols(w_hi, n % SPLIT_SLOTS, to, w).bitcast(F32), ALU.subtract)
                    last.then_inc(lo_done, 1)

            def next_lo(s, i=0):
                if s + 1 < U_END:
                    lo(s + 1, i, KV_COLS if U_Z + 28 <= s + 1 < U_Z + 32 else None)

            def moving_lo(e, q, col):
                dve.wait_ge(mov_hi_done, 4 * e + q + 1)
                for j in range(4 * q, 4 * q + 4):
                    last = dve.scalar_tensor_tensor(mov_lo[:, j, :], xT[:, j, :], gains[:, col + j:col + j + 1],
                                                    mov_hi[:, j, :].bitcast(F32), ALU.mult, ALU.subtract)
                last.then_inc(mov_lo_done, 1)

            def newton(v, y, a, n):
                v, y, a = wk(v, n), wk(y, n), wk(a, n)
                link(dve.reciprocal(y, y))
                link(dve.tensor_tensor(a, y, y, ALU.mult))
                link(dve.tensor_tensor(a, a, v, ALU.mult))
                link(dve.tensor_scalar(a, a, -0.5, 1.5, ALU.mult, ALU.add))
                return y, a

            def norm(e, bank):
                dve.wait_ge(sum_ready, e + 1)
                dve.tensor_scalar(wk(F_V, T), ps[:, bank, 0:T], 1.0 / D, EPS, ALU.mult, ALU.add).then_inc(mean_ready, 1)
                dve.wait_ge(root_ready, e + 1)
                y, a = newton(F_V, F_T, F_SQ, T)
                dve.tensor_tensor(rstd[:, :], y, a, ALU.mult).then_inc(rstd_ready, 1)
                dve.wait_ge(rstd_ready, e + 1)

            def ffn(f, u0, g0):
                def drain_gate(s, i, g):
                    dve.wait_ge(unit_used, s + 1 + 12 * i)
                    dve.tensor_tensor(wk3(F_GS, 4, T), bank4(g), R4, ALU.mult).then_inc(drained, 1)

                def drain_up(s, i, g, part):
                    dve.wait_ge(unit_used, s + 1 + 12 * i)
                    dve.wait_ge(gate_scaled, PARTS * f + 1 + part)
                    for k in range(4):
                        dve.tensor_tensor(wk(F_H + T * k, T), bank4(g)[:, k, :], wk(F_GS + T * k, T),
                                          ALU.mult).then_inc(h_tile if k < 3 else drained, 1)

                def h_lows(i):
                    dve.wait_ge(h_hi_done, H_STEPS * f + 1 + i)
                    dve.tensor_tensor(h_lo[:, 0:4 * T], wk(F_H, 4 * T), h_hi[:, 0:4 * T].bitcast(F32),
                                      ALU.subtract).then_inc(h_lo_done, 1)

                def drain_down(s, i, g, q):
                    dve.wait_ge(unit_used, s + 1 + 12 * i)
                    dve.scalar_tensor_tensor(xT[:, 4 * q:4 * q + 4, :], bank4(g), 0.5, xT[:, 4 * q:4 * q + 4, :],
                                             ALU.mult, ALU.add).then_inc(drained, 1)

                for j in range(8):
                    next_lo(u0 + j)
                    if f == 0 and j == 0:
                        moving_lo(0, 2, G_F1)
                        copy_x(3)
                        moving_lo(0, 3, G_F1)
                    if j == 2:
                        norm(2 * f, 4 * ((g0 + 1) % 2))
                    if j == 3:
                        drain_gate(u0 + 3, 0, g0)
                drain_up(u0 + 7, 0, g0 + 1, 0)
                with dve.Fori(0, PARTS - 1) as i:
                    for j in range(12):
                        s = u0 + 8 + j
                        next_lo(s, i)
                        if j == 0:
                            h_lows(i)
                        if j == 3:
                            drain_gate(s, i, g0 + 2)
                        if 4 <= j < 8:
                            drain_down(s, i, g0 + 3 + j - 4, j - 4)
                    drain_up(u0 + 19, i, g0 + 7, i + 1)
                for k in range(4):
                    sl = slice(T * k, T * k + T)
                    dve.wait_ge(h_hi_done, H_STEPS * f + PARTS + k)
                    dve.tensor_tensor(h_lo[:, sl], wk(F_H + T * k, T), h_hi[:, sl].bitcast(F32),
                                      ALU.subtract).then_inc(h_lo_done, 1)
                for q in range(4):
                    s = u0 + FFN_UNITS - 4 + q
                    next_lo(s)
                    drain_down(s, 0, g0 + FFN_GROUPS - 4 + q, q)
                    if f == 1:
                        dve.wait_ge(squared, 4 * 3 + q + 1)
                        for j in range(4 * q, 4 * q + 4):
                            last = dve.tensor_scalar(xT[:, j, :], xT[:, j, :], gains[:, G_FIN + j:G_FIN + j + 1],
                                                     None, ALU.mult)
                        last.then_inc(y_scaled, 1)
                    if f == 0 and q > 0:
                        moving_lo(1, q - 1, G_MIX)
                if f == 0:
                    moving_lo(1, 3, G_MIX)

            dve.memset(tok[:, :], 1.0).then_inc(tok_set, 1)
            def copy_x(q):
                for j in range(4 * q, 4 * q + 4):
                    dve.wait_ge(x_turned, j + 1)
                    dve.tensor_copy(xT[:, j, :], ps[:, x_bank(j), 0:T]).then_inc(x_copied, 1)

            copy_x(0)
            dve.wait_ge(gains_turned, 1)
            dve.tensor_copy(gains[:, :], ps[:, 7, 0:G_ALL]).then_inc(gains_set, 1)
            dve.tensor_copy(lamin[:, 0:4], ps[0:HALF, 7, 128:132]).then_inc(gains_set, 1)
            copy_x(1)
            lo(0)
            moving_lo(0, 0, G_F1)
            copy_x(2)
            moving_lo(0, 1, G_F1)
            ffn(0, 0, 0)

            def z_steps(z, dst, tiles=4):
                for j in range(4):
                    s = U_Z + 4 * z + j
                    next_lo(s)
                    if z == 0 and j == 2:
                        norm(1, 4 * ((GR_Z + 1) % 2))
                dve.wait_ge(unit_used, s + 1)
                dve.tensor_tensor(wk3(dst, tiles, T), bank4(GR_Z + z)[:, 0:tiles, :], over(rstd[:, :], tiles),
                                  ALU.mult).then_inc(drained, 1)

            def inverse_sums(c):
                dve.wait_ge(exp_done, c + 1)
                st = stat[:, c % 2, :]
                link(dve.reciprocal(st[:, 15:20], st[:, 10:15]))
                return st

            def maxes(c, prompt, sample, scale):
                st = stat[:, c % 2, :]
                dve.tensor_reduce(st[:, 0:2], prompt[:, :, 0:SEQ], AX_X, ALU.max)
                dve.tensor_reduce(st[:, 2:4], prompt[:, :, SEQ:PH], AX_X, ALU.max)
                link(dve.tensor_reduce(st[:, 4:5], sample, AX_X, ALU.max))
                dve.tensor_scalar(st[:, 5:10], st[:, 0:5], -scale, None, ALU.mult).then_inc(max_ready, 1)

            for hf in range(2):
                z_steps(3 * hf, D_QT)
                z_steps(3 * hf + 1, D_KT)
                z_steps(3 * hf + 2, D_VT)
                if hf == 0:
                    dve.tensor_tensor(lamin[:, 4:6], lamin[:, 0:2], lamin[:, 2:4], ALU.mult).then_inc(lam_sq, 1)
                    dve.tensor_scalar(gains[:, G_SUB:G_SUB + 1], gains[:, G_SUB:G_SUB + 1], 1.0 - LAM_INIT, None,
                                      ALU.mult)
                    link(dve.memset(lam[:, 5:10], 1.0))
                    dve.wait_ge(lam_exp, 1)
                    link(dve.scalar_tensor_tensor(lam[:, 6:7], lam[:, 1:2], LAM_INIT, lam[:, 0:1],
                                                  ALU.subtract, ALU.subtract))
                    dve.tensor_copy(lam[:, 8:9], lam[:, 6:7])
                    link(dve.tensor_copy(lam[64:128, 9:10], lam[64:128, 6:7]))

                def bias_and_max(h):
                    if h == 0:
                        dve.wait_ge(tab_in, 16)
                    if h == 0:
                        dve.wait_ge(tab_in, 16)
                    p = D_P + PW * (h % 2)
                    s8 = -SLOPES[h] / DA_SCALE
                    dve.wait_ge(scores_ready, h + 1)
                    dve.wait_ge(stored, 16 * 6 * (hf + 1))
                    if h >= 2:
                        dve.wait_ge(at_ready, h - 1)
                    dve.scalar_tensor_tensor(wk3(p, 2, PH), over(tab[:, C_DIST:C_DIST + PH], 2), s8,
                                             ps[:, 0:2, 0:PH], ALU.mult, ALU.add)
                    dve.scalar_tensor_tensor(wk(p + 768, KEYS), tab[:, C_DISTS:C_DISTS + KEYS], s8,
                                             score_seg(768, KEYS), ALU.mult, ALU.add).then_inc(biased, 1)
                    dve.wait_ge(biased, h + 1)
                    maxes(h, wk3(p, 2, PH), wk(p + 2 * PH, KEYS), DA_SCALE)

                def da_diag(h):
                    st = inverse_sums(h)
                    link(dve.tensor_tensor(st[:, 15:20], st[:, 15:20], lam[:, 5:10], ALU.mult))
                    if h >= 1:
                        dve.wait_ge(at_ready, h)
                    for k in range(4):
                        dve.tensor_scalar(wk(D_DG + P * k, P), ident, st[:, 15 + k:16 + k], None, ALU.mult)
                    dve.tensor_scalar(wk(D_DG + 512, 64), tab[:, C_STACK:C_STACK + 64], st[:, 19:20], None,
                                      ALU.mult).then_inc(diag_ready, 1)

                def copy_o(h):
                    dve.wait_ge(o_ready, h + 1)
                    dve.tensor_copy(wk(D_QT + T * (h % HB), T), ps[:, 6 + h % 2, 0:T]).then_inc(o_copied, 1)

                h0 = HB * hf
                bias_and_max(h0)
                for h in range(h0, h0 + HB):
                    if h + 1 < h0 + HB:
                        bias_and_max(h + 1)
                    da_diag(h)
                    if h > h0:
                        copy_o(h - 1)
                copy_o(h0 + HB - 1)
                dve.wait_ge(n_sum, hf + 1)
                dve.tensor_scalar(wk3(D_CKT, 4, T), ps[:, 0:4, 0:T], 1.0 / DH, EPS, ALU.mult,
                                  ALU.add).then_inc(n_mean, 1)
                dve.wait_ge(n_root, hf + 1)
                y, a = newton(D_CKT, D_CV, D_KT, 4 * T)
                link(dve.tensor_tensor(y, y, a, ALU.mult))
                dve.scalar_tensor_tensor(wk(D_O1 if hf else D_O0, 4 * T), wk(D_QT, 4 * T), gains[:, G_SUB:G_SUB + 1],
                                         y, ALU.mult, ALU.mult).then_inc(n_out, 1)
            z_steps(6, M_CQ)
            z_steps(7, M_CKV, 3)
            for hf, at in ((0, D_O0), (1, D_O1)):
                dve.wait_ge(o_hi_done, hf + 1)
                sl = slice(4 * hf, 4 * hf + 4)
                dve.tensor_tensor(mov_lo[:, sl, :].rearrange("p a b -> p (a b)"), wk(at, 4 * T),
                                  mov_hi[:, sl, :].rearrange("p a b -> p (a b)").bitcast(F32),
                                  ALU.subtract).then_inc(o_lo_done, 1)

            def latent_norm(k, bank, at, tiles, col):
                dve.wait_ge(n_sum, k)
                dve.tensor_scalar(wk(M_V, T), ps[:, bank, 0:T], 1.0 / (P * tiles), EPS, ALU.mult,
                                  ALU.add).then_inc(n_mean, 1)
                dve.wait_ge(n_root, k)
                y, a = newton(M_V, M_Y, M_T, T)
                link(dve.tensor_tensor(y, y, a, ALU.mult))
                for j in range(tiles):
                    last = dve.scalar_tensor_tensor(wk(at + T * j, T), wk(at + T * j, T),
                                                    gains[:, col + j:col + j + 1], y, ALU.mult, ALU.mult)
                last.then_inc(n_out, 1)

            latent_norm(3, 0, M_CQ, 4, G_Q)
            dve.wait_ge(n_hi, 1)
            dve.tensor_tensor(h_lo[:, 0:4 * T], wk(M_CQ, 4 * T), h_hi[:, 0:4 * T].bitcast(F32),
                              ALU.subtract).then_inc(n_lo, 1)
            latent_norm(4, 1, M_CKV, 2, G_KV)
            cos, sin = tab[:, C_COS:C_COS + T], tab[:, C_SIN:C_SIN + T]
            dve.wait_ge(swap_ready, 1)
            dve.tensor_tensor(wk(M_RT, T), wk(M_KRAW, T), cos, ALU.mult)
            link(dve.tensor_tensor(wk(M_RT + T, T), ps[:, 2, 0:T], sin, ALU.mult))
            dve.tensor_tensor(wk(M_KR, T), wk(M_RT, T), wk(M_RT + T, T), ALU.add).then_inc(roped, 1)
            for j in range(3):
                next_lo(U_UQ + j)
                dve.wait_ge(unit_used, U_UQ + j + 1)
                dve.tensor_copy(wk3((M_QN, M_QN + 4 * T, M_QR)[j], 4, T), bank4(GR_UQ + j)).then_inc(drained, 1)
            dve.wait_ge(drained, GR_UQ + 3)
            dve.wait_ge(swap_ready, 2)
            dve.tensor_tensor(wk3(M_QR, 4, T), wk3(M_QR, 4, T), over(cos, 4), ALU.mult)
            link(dve.tensor_tensor(wk3(M_RT, 4, T), ps[:, 4:8, 0:T], over(sin, 4), ALU.mult))
            dve.tensor_tensor(wk(M_QR, 4 * T), wk(M_QR, 4 * T), wk(M_RT, 4 * T), ALU.add).then_inc(roped, 1)
            dve.wait_ge(n_hi, 2)
            dve.tensor_tensor(latents(h_lo)[:, :, 0:T], wk3(M_CKV, 2, T), latents(h_hi)[:, :, 0:T].bitcast(F32),
                              ALU.subtract)
            dve.tensor_tensor(latents(h_lo)[:, :, T:NTOK], wk3(M_CCT, 2, PAST),
                              latents(h_hi)[:, :, T:NTOK].bitcast(F32), ALU.subtract).then_inc(n_lo, 1)

            def mask_and_max(c):
                dve.wait_ge(scores_ready, c + 1)
                for end in (SEQ, PH):
                    hidden = ps[0:64, 0:2, end - 64:end]
                    ins = dve.tensor_scalar(hidden, hidden, NEG, None, ALU.add)
                link(ins)
                maxes(c, ps[:, 0:2, 0:PH], score_seg(2 * PH, KEYS), MLA_SCALE)

            def mla_diag(c):
                st = inverse_sums(c)
                dve.wait_ge(at_ready, c)
                for k in range(5):
                    ins = dve.tensor_scalar(wk(M_DG + P * k, P), ident, st[:, 15 + k:16 + k], None, ALU.mult)
                ins.then_inc(diag_ready, 1)

            for hb in range(2):
                next_lo(U_UKV + hb)
                c0 = HEADS + 2 * hb
                mask_and_max(c0)
                for c in (c0, c0 + 1):
                    if c == c0:
                        mask_and_max(c + 1)
                    mla_diag(c)
                    j = 2 * c - HEADS
                    dve.wait_ge(o_hi_done, c - HEADS + 3)
                    dve.tensor_tensor(mov_lo[:, j:j + 2, :], ps[:, 4:6, 0:T], mov_hi[:, j:j + 2, :].bitcast(F32),
                                      ALU.subtract).then_inc(o_lo_done, 1)

            for n in range(4):
                for q in range(4):
                    next_lo(U_OUT + 4 * n + q)
                dve.wait_ge(unit_used, U_OUT + 4 * n + 4)
                dve.tensor_tensor(xT[:, 4 * n:4 * n + 4, :], bank4(GR_OUT + n), xT[:, 4 * n:4 * n + 4, :],
                                  ALU.add).then_inc(drained, 1)
            for q in range(4):
                moving_lo(2, q, G_F2)
            ffn(1, U_F2, GR_F2)
            dve.wait_ge(tok_sum, 1)
            link(dve.tensor_scalar(tok[:, 0:2], ps[:, 7, 0:2], 1.0 / D, EPS, ALU.mult, ALU.add))
            dve.tensor_scalar(tok[0:DEC, 2:3], ps[0:DEC, 7, 2:3], 1.0 / D, EPS, ALU.mult, ALU.add).then_inc(tok_mean, 1)
            dve.wait_ge(tok_root, 1)
            y, a, v = tok[:, 3:6], tok[:, 6:9], tok[:, 0:3]
            link(dve.reciprocal(y, y))
            link(dve.tensor_tensor(a, y, y, ALU.mult))
            link(dve.tensor_tensor(a, a, v, ALU.mult))
            link(dve.tensor_scalar(a, a, -0.5, 1.5, ALU.mult, ALU.add))
            dve.tensor_tensor(a, a, y, ALU.mult).then_inc(tok_rstd, 1)
            dve.wait_ge(tok_rstd, 1)
            for n, (j, t, r0, rows) in enumerate(Y_JOBS):
                if n % 2 == 1:
                    dve.wait_ge(y_turned, n + 1)
                    dve.tensor_scalar(wk(Y_TOK + t * D + UC * j, UC, slice(0, rows)), ps[0:rows, y_bank(n), :],
                                      tok[0:rows, 6 + t:7 + t], None, ALU.mult).then_inc(y_odd, 1)

        @block.tensor
        def _(pe):
            def triple(out, w, x, first, last):
                pe.matmul(out, w[0], x[0], start=first, stop=False)
                pe.matmul(out, w[0], x[1], start=False, stop=False)
                return pe.matmul(out, w[1], x[0], start=False, stop=last)

            def unit(n, i, g, gi, moving, first, last, tiles=4, tile_ready=None):
                pe.wait_ge(lo_done, n + 1 + 12 * i)
                if first and g >= 2:
                    pe.wait_ge(drained, g - 1 + gi)
                out = bank4(g)
                order = ([(m, k) for m in range(tiles) for k in range(UK)] if tile_ready is None else
                         [(m, k) for k in range(UK) for m in range(tiles)])
                for m, k in order:
                    if tile_ready is not None and m == 0:
                        tile_ready(k)
                    c = UC * k + P * m
                    w = (w_hi[:, n % SPLIT_SLOTS, c:c + P], w_lo[:, n % SPLIT_SLOTS, c:c + P])
                    ins = triple(out[:, m, :], w, moving(k), first and k == 0, last and k == UK - 1)
                ins.then_inc(unit_used, 1)

            def mov(q):
                return lambda k: (mov_hi[:, 4 * q + k, :], mov_lo[:, 4 * q + k, :])

            def hidden(k):
                return (h_hi[:, T * k:T * k + T], h_lo[:, T * k:T * k + T])

            def add_up(e, bank):
                pe.wait_ge(sq_added, 3 * e + 3)
                for a in range(4):
                    ins = pe.matmul(ps[:, bank, 0:T], ones[:, :], wk(F_ACC + T * a, T), start=(a == 0), stop=(a == 3))
                ins.then_inc(sum_ready, 1)

            def from_x(u, i, g, gi, e=None):
                for q in range(4):
                    if e is not None:
                        pe.wait_ge(mov_lo_done, 4 * e + q + 1)
                        if g == 0 and q == 1:
                            turn_x(3)
                        if q == 3:
                            if g:
                                pe.wait_ge(drained, g)
                            else:
                                pe.wait_ge(x_copied, KT)
                            add_up(e if e < 2 else 2, 4 * ((g + 1) % 2))
                    unit(u + q, i, g, gi, mov(q), q == 0, q == 3)

            def ffn(f, u0, g0):
                from_x(u0, 0, g0, 0, 2 * f)
                pe.wait_ge(mean_ready, 2 * f + 1)
                from_x(u0 + 4, 0, g0 + 1, 0)
                with pe.Fori(0, PARTS - 1) as i:
                    from_x(u0 + 8, i, g0 + 2, 6 * i)
                    pe.wait_ge(h_lo_done, H_STEPS * f + 1 + i)
                    for q in range(4):
                        unit(u0 + 12 + q, i, g0 + 3 + q, 6 * i, hidden, True, True)
                    from_x(u0 + 16, i, g0 + 7, 6 * i)
                for q in range(4):
                    unit(u0 + FFN_UNITS - 4 + q, 0, g0 + FFN_GROUPS - 4 + q, 0, hidden, True, True,
                         tile_ready=(lambda k: pe.wait_ge(h_lo_done, H_STEPS * f + PARTS + k)) if q == 0 else None)

            def turn_x(q):
                for j in range(4 * q, 4 * q + 4):
                    if j >= 8:
                        pe.wait_ge(x_copied, j - 3)
                    for t, (r0, rows) in enumerate(TOK):
                        ins = pe.transpose(ps[:, x_bank(j), r0:r0 + rows],
                                           wk(X_TOK + t * D + P * j, P, slice(0, rows)), tab[0:rows, C_ID:C_ID + rows])
                    ins.then_inc(x_turned, 1)

            pe.wait_ge(id_in, 16)
            for t in range(3):
                pe.wait_ge(x_in[t], 16)
            turn_x(0)
            pe.wait_ge(gains_in, 16 * 7)
            pe.wait_ge(lam_in, 16 * 4)
            pe.transpose(ps[:, 7, 0:G_ALL], wk(S_ROWS, P, slice(0, G_ALL)), tab[0:G_ALL, 0:G_ALL])
            pe.transpose(ps[0:HALF, 7, 128:132], wk(S_LROWS, HALF, slice(0, 4)), tab[0:4, 0:4]).then_inc(gains_turned, 1)
            pe.wait_ge(gains_set, 2)
            turn_x(1)
            turn_x(2)
            pe.wait_ge(ones_set, 1)
            pe.wait_ge(x_copied, 4)
            ffn(0, 0, 0)

            def z_group(z):
                g = GR_Z + z
                for q in range(4):
                    n = U_Z + 4 * z + q
                    if z == 0:
                        pe.wait_ge(mov_lo_done, 4 + q + 1)
                        if q == 3:
                            pe.wait_ge(drained, g)
                            add_up(1, 4 * ((g + 1) % 2))
                    if z == 1 and q == 0:
                        pe.wait_ge(mean_ready, 2)
                    unit(n, 0, g, 0, mov(q), q == 0, q == 3, 4 if z < 7 else 3)

            for hf in range(2):
                if hf:
                    pe.wait_ge(n_mean, 1)
                for z in range(3 * hf, 3 * hf + 3):
                    z_group(z)
                pe.wait_ge(drained, GR_Z + 3 * hf + 3)
                if hf == 0:
                    pe.wait_ge(lam_sq, 1)
                    pe.matmul(ps[:, 7, 0:2], ones[0:HALF, :], lamin[:, 4:6], start=True, stop=True).then_inc(lam_sum, 1)
                    pe.wait_ge(lam_exp, 1)
                for kind, at in ((0, D_VT), (3, D_KT)):
                    for t, (r0, rows) in enumerate(TOK):
                        n = 10 * hf + kind + t
                        if n >= 8:
                            pe.wait_ge(job_drained, n - 7)
                        for hh in range(HB):
                            ins = pe.transpose(ps[0:rows, n % 8, P * hh:P * hh + P], wk(at + T * hh + r0, rows), ident)
                        ins.then_inc(job_ready, 1)
                pe.wait_ge(ck_in, 16 * (hf + 1))
                for hh in range(HB):
                    n = 10 * hf + 6 + hh
                    if n >= 8:
                        pe.wait_ge(job_drained, n - 7)
                    for kt in range(4):
                        ins = pe.transpose(ps[:, n % 8, P * kt:P * kt + P], wk(D_CST + UC * kt + P * hh, P), ident)
                    ins.then_inc(job_ready, 1)

                def da_scores(h):
                    if h > HB * hf:
                        pe.wait_ge(biased, h)
                    hh = h % HB
                    for half in range(2):
                        d = slice(HALF * half, HALF * half + HALF)
                        q, k = wk(D_QT + T * hh, T, d), wk(D_KT + T * hh, T, d)
                        pe.matmul(ps[:, half, 0:SEQ], q[:, P:SEQ], k[:, 0:SEQ], start=True, stop=True)
                        pe.matmul(ps[:, half, SEQ:PH], q[:, 0:P], k[:, 0:P], start=True, stop=True)
                        pe.matmul(ps[d, 2, :], q[:, SEQ:T], wk(D_CKT + PAST * hh, PAST, d), start=True, stop=True)
                        ins = pe.matmul(ps[d, 3, 0:DEC], q[:, SEQ:T], k[:, SEQ:T], start=True, stop=True)
                    ins.then_inc(scores_ready, 1)

                def da_transpose(h):
                    pe.wait_ge(diag_ready, h + 1)
                    p = D_P + PW * (h % 2)
                    dg = [wk(D_DG + P * k, P) for k in range(4)]
                    for col, at, k in ((0, SEQ, 2), (P, 0, 0), (SEQ, P, 0)):
                        out = ps[:, 4, col:col + P]
                        pe.matmul(out, wk(p + at, P), dg[k], start=True, stop=False)
                        pe.matmul(out, wk(p + at + PH, P), dg[k + 1], start=False, stop=True)
                    for kt in range(5):
                        rows = P if kt < 4 else DEC
                        ins = pe.matmul(ps[0:rows, 5, 64 * kt:64 * kt + 64], wk(p + 768 + P * kt, rows),
                                        wk(D_DG + 512, 64), start=True, stop=True)
                    ins.then_inc(at_ready, 1)

                def da_values(h):
                    pe.wait_ge(at_copied, h + 1)
                    if h == HB * hf:
                        pe.wait_ge(cv_in, 16 * (hf + 1))
                    if h >= 2:
                        pe.wait_ge(o_copied, h - 1)
                    out = ps[:, 6 + h % 2, :]
                    hd = P * (h % HB)
                    pe.matmul(out[:, 0:SEQ], wk(D_VTOK + hd, P), wk(D_AT, SEQ), start=True, stop=False)
                    pe.matmul(out[:, P:SEQ], wk(D_VTOK + UC + hd, P), wk(D_AT + SEQ, P), start=False, stop=True)
                    for kt in range(4):
                        pe.matmul(out[:, SEQ:T], wk(D_CV + UC * kt + hd, P), wk(D_AT + 384 + 64 * kt, 64),
                                  start=(kt == 0), stop=False)
                    new = slice(0, DEC)
                    pe.matmul(out[:, SEQ:T], wk(D_VTOK + 2 * UC + hd, P, new), wk(D_AT + 640, 64, new),
                              start=False, stop=True).then_inc(o_ready, 1)

                h0 = HB * hf
                pe.wait_ge(job_drained, 10 * hf + 10)
                da_scores(h0)
                for h in range(h0, h0 + HB):
                    if h + 1 < h0 + HB:
                        da_scores(h + 1)
                    da_transpose(h)
                    da_values(h)
                pe.wait_ge(n_sq, hf + 1)
                for a in range(4):
                    ins = pe.matmul(ps[:, a, 0:T], ones[:, :], wk(D_KT + T * a, T), start=True, stop=True)
                ins.then_inc(n_sum, 1)
            pe.wait_ge(n_mean, 2)
            z_group(6)
            z_group(7)
            pe.wait_ge(drained, GR_Z + 8)
            pe.wait_ge(cc_in, 16 * 3)
            for a in range(2):
                for kt in range(4):
                    ins = pe.transpose(ps[:, (JOB_CC + a) % 8, P * kt:P * kt + P],
                                       wk(M_CCKV + KVL * kt + P * a, P), ident)
                ins.then_inc(job_ready, 1)
            for kt in range(4):
                ins = pe.transpose(ps[:, (JOB_CC + 2) % 8, P * kt:P * kt + P], wk(M_CKR + P * kt, P), ident)
            ins.then_inc(job_ready, 1)
            pe.wait_ge(tab_in, 16)
            swap = tab[:, C_SWAP:C_SWAP + P]
            pe.matmul(ps[:, 2, 0:T], swap, wk(M_KRAW, T), start=True, stop=True).then_inc(swap_ready, 1)
            for bank, at, tiles in ((0, M_SQ, 4), (1, M_SQ2, 2)):
                pe.wait_ge(n_sq, 3 + bank)
                for a in range(tiles):
                    ins = pe.matmul(ps[:, bank, 0:T], ones[:, :], wk(at + T * a, T), start=(a == 0),
                                    stop=(a == tiles - 1))
                ins.then_inc(n_sum, 1)
            pe.wait_ge(n_out, 4)
            pe.wait_ge(roped, 1)
            for t, (r0, rows) in enumerate(TOK):
                b = (JOB_CTOK + t) % 8
                for a in range(2):
                    pe.transpose(ps[0:rows, b, P * a:P * a + P], wk(M_CKV + T * a + r0, rows), ident)
                pe.transpose(ps[0:rows, b, KVL:KVL + ROPE], wk(M_KR + r0, rows, slice(0, ROPE)),
                             tab[0:ROPE, C_ID:C_ID + ROPE]).then_inc(job_ready, 1)
            pe.wait_ge(job_drained, JOB_CTOK + 3)
            pe.wait_ge(n_lo, 1)
            for j in range(3):
                unit(U_UQ + j, 0, GR_UQ + j, 0, hidden, True, True)
            pe.wait_ge(drained, GR_UQ + 3)
            for a in range(4):
                ins = pe.matmul(ps[:, 4 + a, 0:T], swap, wk(M_QR + T * a, T), start=True, stop=True)
            ins.then_inc(swap_ready, 1)
            pe.wait_ge(roped, 2)
            pe.wait_ge(n_lo, 2)

            for hb in range(2):
                n = U_UKV + hb
                jk = JOB_KV + 15 * hb
                pe.wait_ge(lo_done, n + 1)

                def start_job(j):
                    if j - jk >= 8:
                        pe.wait_ge(job_drained, j - 7)

                def wslice(k, hh, v):
                    c = 1024 * k + 256 * hh + P * v
                    return (w_hi[:, n % SPLIT_SLOTS, c:c + P], w_lo[:, n % SPLIT_SLOTS, c:c + P])

                for hh in range(HB):
                    for part, (t0, w) in enumerate(((0, T), (T, PAST))):
                        j = jk + 2 * hh + part
                        start_job(j)
                        for k in range(2):
                            c = (latents(h_hi)[:, k, t0:t0 + w], latents(h_lo)[:, k, t0:t0 + w])
                            ins = triple(ps[:, j % 8, 0:w], wslice(k, hh, 0), c, k == 0, k == 1)
                        ins.then_inc(job_ready, 1)
                for t, t0 in enumerate((0, P, SEQ, T, T + P, T + 2 * P, T + 3 * P)):
                    j = jk + 8 + t
                    start_job(j)
                    for k in range(2):
                        c = (latents(h_hi)[:, k, t0:t0 + P], latents(h_lo)[:, k, t0:t0 + P])
                        wv = [w[:, n % SPLIT_SLOTS, :].rearrange("p (k h v c) -> p k h v c", k=2, h=4, v=2)[:, k, :, 1, :]
                              for w in (w_hi, w_lo)]
                        ins = triple(ps[:, j % 8, :].rearrange("p (h c) -> p h c", h=4), c, wv, k == 0, k == 1)
                    ins.then_inc(job_ready, 1)

                def mla_scores(c):
                    if c > HEADS + 2 * hb:
                        pe.wait_ge(exp_done, c)
                    pr = c - HEADS
                    for half in range(2):
                        d = slice(64 * half, 64 * half + 64)
                        qn = wk(M_QN + T * (2 * pr + half), T)
                        kn = wk(M_KN + NTOK * (2 * (pr % 2) + half), NTOK)
                        qr, kr = wk(M_QR + T * pr, T, d), wk(M_KR, NTOK, d)
                        for out, q, k in ((ps[:, half, 0:SEQ], slice(P, SEQ), slice(0, SEQ)),
                                          (ps[:, half, SEQ:PH], slice(0, P), slice(0, P)),
                                          (ps[d, 2, :], slice(SEQ, T), slice(T, NTOK)),
                                          (ps[d, 3, 0:DEC], slice(SEQ, T), slice(SEQ, T))):
                            ins = pe.matmul(out, qn[:, q], kn[:, k], start=True, stop=False)
                            if c == HEADS + 2 * hb and half == 0 and k.stop == SEQ:
                                ins.then_inc(unit_used, 1)
                            ins = pe.matmul(out, qr[:, q], kr[:, k], start=False, stop=True)
                    ins.then_inc(scores_ready, 1)

                def mla_transpose(c):
                    pe.wait_ge(diag_ready, c + 1)
                    pe.wait_ge(o_lo_done, c - HEADS + 2)
                    dg = [wk(M_DG + P * k, P) for k in range(5)]
                    for half in range(2):
                        for col, at, k in ((0, PH * half + SEQ, 2), (P, PH * half, 0), (SEQ, PH * half + P, 0)):
                            pe.matmul(ps[:, 4 + half, col:col + P], wk(M_P + at, P), dg[k + half], start=True, stop=True)
                    for kt in range(4):
                        pe.matmul(ps[:, 6, P * kt:P * kt + P], wk(M_P + 768 + P * kt, P), dg[4], start=True, stop=True)
                    pe.matmul(ps[0:DEC, 7, 0:P], wk(M_P + 768 + PAST, DEC), dg[4], start=True,
                              stop=True).then_inc(at_ready, 1)

                def mla_values(c):
                    pe.wait_ge(at_copied, c + 1)
                    for half in range(2):
                        out = ps[:, 4 + half, :]
                        hd = P * (2 * ((c - HEADS) % 2) + half)
                        at = M_AT + 384 * half
                        pe.matmul(out[:, 0:SEQ], wk(M_VM + hd, P), wk(at, SEQ), start=True, stop=False)
                        pe.matmul(out[:, P:SEQ], wk(M_VM + UC + hd, P), wk(at + SEQ, P), start=False, stop=True)
                        for kt in range(4):
                            pe.matmul(out[:, SEQ:T], wk(M_VM + UC * (3 + kt) + hd, P),
                                      wk(M_AT + 768 + P * kt + 64 * half, 64), start=(kt == 0), stop=False)
                        new = slice(0, DEC)
                        ins = pe.matmul(out[:, SEQ:T], wk(M_VM + 2 * UC + hd, P, new),
                                        wk(M_AT + 1280 + 64 * half, 64, new), start=False, stop=True)
                    ins.then_inc(o_ready, 1)

                pe.wait_ge(job_drained, jk + 15)
                c0 = HEADS + 2 * hb
                mla_scores(c0)
                for c in (c0, c0 + 1):
                    if c == c0:
                        mla_scores(c + 1)
                    mla_transpose(c)
                    mla_values(c)
                pe.wait_ge(o_lo_done, 2 * hb + 4)

            for n in range(4):
                for q in range(4):
                    unit(U_OUT + 4 * n + q, 0, GR_OUT + n, 0, mov(q), q == 0, q == 3)
            ffn(1, U_F2, GR_F2)
            def y_job(n):
                j, t, r0, rows = Y_JOBS[n]
                if n >= 7:
                    pe.wait_ge(y_odd if n % 2 == 0 else y_even, (n - 7) // 2 + 1)
                for a in range(4):
                    ins = pe.transpose(ps[0:rows, y_bank(n), P * a:P * a + P], xT[:, 4 * j + a, r0:r0 + rows], ident)
                ins.then_inc(y_turned, 1)

            pe.wait_ge(sq_added, 11)
            for step, at in enumerate((F_ACC, F_SQ)):
                if step:
                    pe.wait_ge(y_scaled, 2)
                    for n in range(3):
                        y_job(n)
                    pe.wait_ge(squared, 16)
                for t, (r0, rows) in enumerate(TOK):
                    for a in range(4):
                        ins = pe.matmul(ps[0:rows, 7, t:t + 1], wk(at + T * a + r0, rows), ones[:, 0:1],
                                        start=(step == 0 and t == 0 and a == 0), stop=(step == 1 and a == 3),
                                        skip_group_check=True)
            ins.then_inc(tok_sum, 1)
            pe.wait_ge(drained, GR_F2 + FFN_GROUPS)
            for n in range(3, 12):
                if n % 3 == 0:
                    pe.wait_ge(y_scaled, n // 3 + 1)
                y_job(n)


def constants():
    f = np.float32
    p = np.arange(P)
    pos = np.concatenate([np.arange(SEQ), PAST + np.arange(DEC)]).astype(f)
    half = ROPE // 2
    inv = (ROPE_THETA ** (-np.arange(half) / half)).astype(f)
    ang = pos[None, :] * inv[p % half][:, None]
    sign = np.where(p % ROPE < half, -1.0, 1.0)[:, None]
    q1, k1 = (P + p)[:, None], np.arange(SEQ)[None, :]
    dist = np.where(k1 // CHUNK <= q1 // CHUNK, np.abs(q1 - k1), BIG)
    dists = np.abs(PAST + (p % DEC)[:, None] - np.arange(KEYS)[None, :])
    stack = p[:, None] % HALF == np.arange(HALF)[None, :]
    swap = (p[:, None] ^ half) == p[None, :]
    return np.concatenate([np.eye(P), stack, swap, np.cos(ang), sign * np.sin(ang), dist, dist[:, P:], dists],
                          axis=1).astype(f)


_INS = ["x_prompt", "x_sample", "cache_da_k", "cache_da_v", "cache_mla_ckv", "cache_mla_krope",
        "ffn1_norm", "ffn1_w_gate", "ffn1_w_up", "ffn1_w_down", "mix_norm", "w_in",
        "da_lambda_q1", "da_lambda_k1", "da_lambda_q2", "da_lambda_k2", "da_subln",
        "mla_q_norm", "mla_w_uq", "mla_kv_norm", "mla_w_ukv", "w_out",
        "ffn2_norm", "ffn2_w_gate", "ffn2_w_up", "ffn2_w_down", "final_norm"]
_OUTS = [(1, SEQ, D), (1, DEC, D),
         (1, 1, SEQ, HEADS, DH), (1, 1, SEQ, HEADS, DH), (1, 1, SEQ, KVL), (1, 1, SEQ, ROPE),
         (1, 1, DEC, HEADS, DH), (1, 1, DEC, HEADS, DH), (1, 1, DEC, KVL), (1, 1, DEC, ROPE)]


def kernel(**inputs):
    import concourse.bacc as bacc
    from concourse.bass_utils import run_bass_kernel_spmd

    nc = bacc.Bacc("TRN2", target_bir_lowering=False, num_devices=1)
    arrays = {f"in_{name}": np.ascontiguousarray(inputs[name]) for name in _INS}
    arrays["in_table"] = constants()
    args = [nc.dram_tensor(name, a.shape, F32, kind="ExternalInput").ap() for name, a in arrays.items()]
    args += [nc.dram_tensor(f"out_{i}", shape, F32, kind="ExternalOutput").ap() for i, shape in enumerate(_OUTS)]
    build(nc, *args)
    r = run_bass_kernel_spmd(nc, [arrays], core_ids=[0])
    return tuple(r.results[0][f"out_{i}"] for i in range(len(_OUTS)))
```

```python
from contextlib import ExitStack

import numpy as np

import concourse.bass as bass
from concourse import mybir

F32 = mybir.dt.float32
F32R = mybir.dt.float32r
ALU = mybir.AluOpType
ACT = mybir.ActivationFunctionType
AX_X = mybir.AxisListType.X

P = 128
D = 2048
KT = D // P
SEQ = 256
DEC = 64
T = SEQ + DEC
PAST = 512
CHUNK = 64
KEYS = PAST + DEC
F = 5632
UC = 512
UK = 4
PARTS = F // UC
HEADS = 8
DH = 128
HALF = 64
QL = 512
KVL = 256
ROPE = 64
QKH = DH + ROPE
ROPE_THETA = 10000.0
EPS = 1e-6
LAM_INIT = 0.2
JOB_CC, JOB_CTOK, JOB_KV = 20, 23, 26
DA_SCALE = HALF ** -0.5
MLA_SCALE = QKH ** -0.5
NEG = -1e30
BIG = 1e30
SLOPES = [2.0 ** (-8.0 * (i + 1) / HEADS) for i in range(HEADS)]
HB = 4
RAW_SLOTS = 4
SPLIT_SLOTS = 2
TOK = [(0, P), (P, P), (SEQ, DEC)]
NTOK = T + PAST
Y_JOBS = [(j, t, r0, rows) for j in range(4) for t, (r0, rows) in enumerate(TOK)]

C_ID, C_STACK, C_SWAP = 0, 128, 192
C_COS, C_SIN, C_DIST, C_DISTS, C_ALL = 320, 640, 960, 1344, 1920

G_F1, G_MIX, G_F2, G_FIN, G_SUB, G_Q, G_KV, G_ALL = 0, 16, 32, 48, 64, 65, 69, 71

FFN_UNITS, FFN_GROUPS = 12 * PARTS, 6 * PARTS
U_Z = FFN_UNITS
U_OA = U_Z + 32
U_UQ = U_OA + 4
U_OA2 = U_UQ + 3
U_UKV = (U_OA2 + 2, U_OA2 + 5)
U_OA3 = U_OA2 + 3
U_OB = U_OA2 + 6
U_F2 = U_OB + 8
U_END = U_F2 + FFN_UNITS
GR_Z = FFN_GROUPS
GR_OA = GR_Z + 8
GR_UQ = GR_OA + 2
GR_ROPE = GR_UQ + 3
GR_OA2 = GR_ROPE + 1
GR_OA3 = GR_OA2 + 1
GR_OB = GR_OA3 + 1
GR_F2 = GR_OB + 8
H_STEPS = PARTS - 1 + 4

Z_COLS = [0, 1024, 2048, 512, 1536, 2560, 3072, 3584]
Z_WIDTH = [UC] * 7 + [KVL + ROPE]

W_ALL = 15488
X_TOK, S_ROWS, S_LROWS = 0, 11904, 12032
F_GS, F_H, F_SQ, F_ACC, F_V, F_T = 6144, 7424, 8704, 9984, 11264, 11584
D_QT, D_KT, D_VTOK, D_CKT, D_CV, D_P, D_AT, D_DG, D_CST, D_O0 = (
    0, 1280, 2560, 4096, 6144, 8192, 10880, 11584, 12160, 14208)
D_VT, D_KTOK, D_O1 = D_CST, D_P, D_P
M_QN, M_QR, M_KN, M_VM, M_KR, M_P, M_AT, M_DG = 0, 2560, 3840, 7168, 10752, 11584, 12928, 14336
M_CQ, M_CKV, M_KRAW, M_SQ, M_V, M_Y, M_T, M_CTOK = 0, 3840, 4480, 4800, 6080, 6400, 6720, 9472
M_SQ2, M_CCT, M_CCKV, M_CKR, M_RT = 7168, 8192, 11584, 12608, 13120
PW = 1344
PH = SEQ + P
SEGS = [(0, SEQ), (PH, SEQ), (SEQ, P), (PH + SEQ, P), (2 * PH, KEYS)]
KV_COLS = [(0, 0, KVL + ROPE), (KVL + ROPE, KVL, ROPE)]
Y_TOK = 0


def build(nc, x_prompt, x_sample, cache_k, cache_v, cache_ckv, cache_kr,
          ffn1_norm, ffn1_gate, ffn1_up, ffn1_down, mix_norm, w_in,
          lq1, lk1, lq2, lk2, da_subln, q_norm, w_uq, kv_norm, w_ukv, w_out,
          ffn2_norm, ffn2_gate, ffn2_up, ffn2_down, final_norm, table,
          y_prompt, y_sample, k_prompt, v_prompt, ckv_prompt, kr_prompt,
          k_sample, v_sample, ckv_sample, kr_sample):
    ctx = ExitStack()
    with ctx:
        def sb(name, shape, dt):
            return ctx.enter_context(nc.sbuf_tensor(name, shape, dt))

        def sem(name):
            return ctx.enter_context(nc.semaphore(name))

        xT = sb("xT", [P, KT, T], F32)
        mov_hi = sb("mov_hi", [P, KT, T], F32R)
        mov_lo = sb("mov_lo", [P, KT, T], F32R)
        raw = sb("raw", [P, RAW_SLOTS, UK * UC], F32)
        w_hi = sb("w_hi", [P, SPLIT_SLOTS, UK * UC], F32R)
        w_lo = sb("w_lo", [P, SPLIT_SLOTS, UK * UC], F32R)
        h_hi = sb("h_hi", [P, 2 * NTOK], F32R)
        h_lo = sb("h_lo", [P, 2 * NTOK], F32R)
        work = sb("work", [P, W_ALL], F32)
        tab = sb("tab", [P, C_ALL], F32)
        ones = sb("ones", [P, P], F32)
        gains = sb("gains", [P, G_ALL], F32)
        rstd = sb("rstd", [P, T], F32)
        lamin = sb("lamin", [HALF, 6], F32)
        lam = sb("lam", [P, 10], F32)
        tok = sb("tok", [P, 12], F32)
        stat = sb("stat", [P, 2, 20], F32)
        ps = ctx.enter_context(nc.psum_tensor("ps", [P, 8, 512], F32))

        ident = tab[:, C_ID:C_ID + P]

        id_in = sem("id_in")
        tab_in = sem("tab_in")
        gains_in = sem("gains_in")
        gains_turned = sem("gains_turned")
        gains_set = sem("gains_set")
        lam_in = sem("lam_in")
        x_in = [sem(f"x_in{i}") for i in range(3)]
        raw_in = [sem(f"raw_in{i}") for i in range(RAW_SLOTS)]
        ck_in = sem("ck_in")
        cv_in = sem("cv_in")
        cc_in = sem("cc_in")
        hi_done = sem("hi_done")
        lo_done = sem("lo_done")
        unit_used = sem("unit_used")
        drained = sem("drained")
        x_turned = sem("x_turned")
        x_copied = sem("x_copied")
        mov_hi_done = sem("mov_hi_done")
        mov_lo_done = sem("mov_lo_done")
        squared = sem("squared")
        sq_added = sem("sq_added")
        sum_ready = sem("sum_ready")
        mean_ready = sem("mean_ready")
        root_ready = sem("root_ready")
        rstd_ready = sem("rstd_ready")
        silu_done = sem("silu_done")
        gate_scaled = sem("gate_scaled")
        h_tile = sem("h_tile")
        h_hi_done = sem("h_hi_done")
        h_lo_done = sem("h_lo_done")
        job_ready = sem("job_ready")
        job_drained = sem("job_drained")
        scores_ready = sem("scores_ready")
        biased = sem("biased")
        max_ready = sem("max_ready")
        exp_done = sem("exp_done")
        diag_ready = sem("diag_ready")
        at_ready = sem("at_ready")
        at_copied = sem("at_copied")
        o_ready = sem("o_ready")
        o_copied = sem("o_copied")
        o_hi_done = sem("o_hi_done")
        o_lo_done = sem("o_lo_done")
        lam_sq = sem("lam_sq")
        lam_sum = sem("lam_sum")
        lam_exp = sem("lam_exp")
        lam_ready = sem("lam_ready")
        n_sq = sem("n_sq")
        n_sum = sem("n_sum")
        n_mean = sem("n_mean")
        n_root = sem("n_root")
        n_out = sem("n_out")
        n_hi = sem("n_hi")
        n_lo = sem("n_lo")
        swap_ready = sem("swap_ready")
        roped = sem("roped")
        c_ready = sem("c_ready")
        k_stored = sem("k_stored")
        v_stored = sem("v_stored")
        ctok_stored = sem("ctok_stored")
        y_stored = sem("y_stored")
        y_scaled = sem("y_scaled")
        tok_set = sem("tok_set")
        tok_sum = sem("tok_sum")
        tok_mean = sem("tok_mean")
        tok_root = sem("tok_root")
        tok_rstd = sem("tok_rstd")
        y_turned = sem("y_turned")
        y_even = sem("y_even")
        y_odd = sem("y_odd")
        ones_set = sem("ones_set")
        dve_chain = sem("dve_chain")
        act_chain = sem("act_chain")

        def wk(at, n, rows=slice(0, P)):
            return work[rows, at:at + n]

        def wk3(at, a, b, rows=slice(0, P)):
            return work[rows, at:at + a * b].rearrange("p (a b) -> p a b", a=a)

        def x_bank(j):
            return j if j < 4 else 4 + j % 4

        def y_bank(n):
            return (0, 1, 2, 4, 5, 6, 7)[n % 7]

        def bank4(g):
            h = 4 if g == GR_OB else 4 * (g % 2)
            return ps[:, h:h + 4, 0:T]

        def half_free(g):
            return g if g in (GR_OB, GR_OB + 1) else g - 1

        def scores_half(hf):
            return 4 * (1 - hf)

        def job_bank(n):
            if n < JOB_CC:
                hf, m = n // 10, n % 10
                return scores_half(hf) + m % 4 if m < 7 else 4 * hf + (2, 3, 2)[m - 7]
            if n < JOB_CTOK:
                return (1, 4, 5)[n - JOB_CC]
            if n < JOB_KV:
                return n - JOB_CTOK
            return (n - JOB_KV + 4) % 8 if n < JOB_KV + 15 else (n - JOB_KV - 15) % 8

        def over(ap, n):
            return ap.unsqueeze(1).to_broadcast([ap.shape[0], n, ap.shape[1]])

        def raw_value(n, i=0):
            more = sum(u <= n and u % RAW_SLOTS == n % RAW_SLOTS for u in range(U_UQ, U_UQ + 3))
            return 16 * (n // RAW_SLOTS + 1 + 3 * more) + (12 // RAW_SLOTS) * 16 * i

        R4 = over(rstd[:, :], 4)

        def unit_cols(buf, slot, at, width):
            return buf[:, slot, :].rearrange("p (k c) -> p k c", k=UK)[:, :, at:at + width]

        def diagonal(k):
            return wk(D_DG + P * k, P if k < 4 else 64)

        def latents(buf):
            return buf[:, :].rearrange("p (k t) -> p k t", k=2)

        def score_seg(at, width, b=0):
            if at >= 768:
                return ps[:, b + 2:b + 4, :].rearrange("p a b -> p (a b)")[:, at - 768:at - 768 + width]
            return ps[:, at // PH, at % PH:at % PH + width]

        def block_of(w, r0, c0, width=UC):
            return w[0, bass.ds(r0, UK * P), bass.ds(c0, width)].rearrange("(k p) c -> p k c", p=P)

        block = ctx.enter_context(nc.Block())

        @block.sync
        def _(sp):
            def load(n, i, src, width=UC):
                if n >= RAW_SLOTS:
                    sp.wait_ge(lo_done, n - RAW_SLOTS + 1 + 12 * i)
                dst = raw[:, n % RAW_SLOTS, :].rearrange("p (k c) -> p k c", k=UK)[:, :, 0:width]
                sp.dma_start(dst, src).then_inc(raw_in[n % RAW_SLOTS], 16)

            sp.dma_start(tab[:, 0:C_STACK], table[:, 0:C_STACK]).then_inc(id_in, 16)
            for t, (r0, rows) in enumerate(TOK):
                src = x_prompt[0, r0:r0 + rows, :] if t < 2 else x_sample[0]
                sp.dma_start(wk(X_TOK + t * D, D, slice(0, rows)), src).then_inc(x_in[t], 16)
            for col, g, n in ((G_F1, ffn1_norm[0], KT), (G_MIX, mix_norm[0], KT), (G_F2, ffn2_norm[0], KT),
                              (G_FIN, final_norm, KT), (G_SUB, da_subln[0], 1), (G_Q, q_norm[0], 4),
                              (G_KV, kv_norm[0], 2)):
                sp.dma_start(wk(S_ROWS, P, slice(col, col + n)),
                              g.rearrange("(j p) -> j p", p=P)).then_inc(gains_in, 16)
            for c, v in enumerate((lq1, lq2, lk1, lk2)):
                sp.dma_start(wk(S_LROWS, HALF, slice(c, c + 1)), v).then_inc(lam_in, 16)

            def ffn_loads(u0, gate, up, down):
                for q in range(4):
                    load(u0 + q, 0, block_of(gate, UC * q, 0))
                if u0 == 0:
                    sp.dma_start(tab[:, C_STACK:C_ALL], table[:, C_STACK:C_ALL]).then_inc(tab_in, 16)
                for q in range(4):
                    load(u0 + 4 + q, 0, block_of(up, UC * q, 0))
                with sp.Fori(0, PARTS - 1) as i:
                    for q in range(4):
                        load(u0 + 8 + q, i, block_of(gate, UC * q, i * UC + UC))
                    for q in range(4):
                        load(u0 + 12 + q, i, block_of(down, i * UC, UC * q))
                    for q in range(4):
                        load(u0 + 16 + q, i, block_of(up, UC * q, i * UC + UC))
                for q in range(4):
                    load(u0 + FFN_UNITS - 4 + q, 0, block_of(down, (PARTS - 1) * UC, UC * q))

            ffn_loads(0, ffn1_gate, ffn1_up, ffn1_down)

            def z_loads(z):
                for q in range(4):
                    load(U_Z + 4 * z + q, 0, block_of(w_in, UC * q, Z_COLS[z], Z_WIDTH[z]), Z_WIDTH[z])

            for z in range(8):
                z_loads(z)

            def out_load(n, rows, cols):
                load(n, 0, block_of(w_out, UC * rows, UC * cols))

            def ukv_load(hb):
                n = U_UKV[hb]
                sp.wait_ge(lo_done, n - RAW_SLOTS + 1)
                sp.dma_start(raw[:, n % RAW_SLOTS, :].rearrange("p (k c) -> p k c", k=2),
                             w_ukv[0, :, 1024 * hb:1024 * hb + 1024].rearrange("(k p) c -> p k c", p=P)
                             ).then_inc(raw_in[n % RAW_SLOTS], 16)

            for c in range(2):
                for q in range(2):
                    out_load(U_OA + 2 * c + q, q, c)
            uq = w_uq[0].rearrange("(k p) (h c) -> p k h c", p=P, c=QKH)
            for j in range(3):
                n = U_UQ + j
                sp.wait_ge(lo_done, n - RAW_SLOTS + 1)
                for k in range(UK):
                    dst = raw[:, n % RAW_SLOTS, UC * k:UC * k + UC]
                    if j == 0:
                        dst = dst.rearrange("p (h c) -> p h c", c=ROPE)
                        src = uq[:, k, :, DH:QKH]
                    else:
                        dst = dst.rearrange("p (h c) -> p h c", c=DH)
                        src = uq[:, k, HB * (j - 1):HB * j, 0:DH]
                    sp.dma_start(dst, src).then_inc(raw_in[n % RAW_SLOTS], 16)
            for q in range(2):
                out_load(U_OA2 + q, q, 2)
            ukv_load(0)
            for q in range(2):
                out_load(U_OA3 + q, q, 3)
            ukv_load(1)
            for q in range(2):
                for c in range(4):
                    out_load(U_OB + 4 * q + c, 2 + q, c)
            ffn_loads(U_F2, ffn2_gate, ffn2_up, ffn2_down)
            for n, (j, t, r0, rows) in enumerate(Y_JOBS):
                sp.wait_ge(y_odd if n % 2 else y_even, n // 2 + 1)
                dst = (y_prompt[0, r0:r0 + rows, UC * j:UC * j + UC] if t < 2
                       else y_sample[0, :, UC * j:UC * j + UC])
                sp.dma_start(dst, wk(Y_TOK + t * D + UC * j, UC, slice(0, rows))).then_inc(y_stored, 16)
            sp.wait_ge(y_stored, 16 * 12)
            sp.wait_ge(k_stored, 16 * 6)
            sp.wait_ge(v_stored, 16 * 6)
            sp.wait_ge(ctok_stored, 16 * 6)

        @block.gpsimd
        def _(pool):
            pool.memset(ones[:, :], 1.0).then_inc(ones_set, 1)

            def add_squares(e):
                for q in range(1, 4 if e < 3 else 3):
                    pool.wait_ge(squared, 4 * e + q + 1)
                    if 3 * e + q - 1 > 0:
                        pool.wait_ge(sq_added, 3 * e + q - 1)
                    pool.tensor_tensor(wk(F_ACC, 4 * T), wk(F_ACC, 4 * T), wk(F_SQ, 4 * T),
                                       ALU.add).then_inc(sq_added, 1)

            def scale_gate(f, i):
                pool.wait_ge(silu_done, PARTS * f + 1 + i)
                pool.tensor_tensor(wk3(F_GS, 4, T), wk3(F_GS, 4, T), R4, ALU.mult).then_inc(gate_scaled, 1)

            def store_tokens(at, width, col, dst_prompt, dst_sample, stored):
                for t, (r0, rows) in enumerate(TOK):
                    dst = (dst_prompt[r0:r0 + rows, col:col + width] if t < 2
                           else dst_sample[:, col:col + width])
                    pool.dma_start(dst, wk(at[t], width, slice(0, rows))).then_inc(stored, 16)

            kp = k_prompt[0, 0].rearrange("s h d -> s (h d)")
            ks = k_sample[0, 0].rearrange("s h d -> s (h d)")
            vp = v_prompt[0, 0].rearrange("s h d -> s (h d)")
            vs = v_sample[0, 0].rearrange("s h d -> s (h d)")
            ck = cache_k[0, 0].rearrange("s h d -> s (h d)").rearrange("(k p) c -> p k c", p=P)
            cv = cache_v[0, 0].rearrange("s h d -> s (h d)").rearrange("(k p) c -> p k c", p=P)

            def mix_traffic():
                for hf in range(2):
                    cols = slice(UC * hf, UC * hf + UC)
                    if hf == 0:
                        pool.wait_ge(mov_lo_done, 8)
                    else:
                        pool.wait_ge(n_out, 1)
                    pool.dma_start(wk3(D_CST, 4, UC), ck[:, :, cols]).then_inc(ck_in, 16)
                    pool.dma_start(wk3(D_CV, 4, UC), cv[:, :, cols]).then_inc(cv_in, 16)
                    pool.wait_ge(job_drained, 10 * hf + 3)
                    store_tokens([D_KTOK + UC * t for t in range(3)], UC, UC * hf, kp, ks, k_stored)
                    pool.wait_ge(job_drained, 10 * hf + 10)
                    store_tokens([D_VTOK + UC * t for t in range(3)], UC, UC * hf, vp, vs, v_stored)
                pool.wait_ge(o_copied, 8)
                pool.dma_start(wk3(M_CCKV, 4, KVL),
                             cache_ckv[0, 0].rearrange("(k p) c -> p k c", p=P)).then_inc(cc_in, 16)
                kr_src = cache_kr[0, 0].rearrange("(k p) c -> p k c", p=P)
                for half in range(2):
                    pool.dma_start(wk3(M_CKR, 4, P)[:, :, ROPE * half:ROPE * half + ROPE],
                                 kr_src).then_inc(cc_in, 16)

            pool.wait_ge(x_copied, 4)
            pool.tensor_tensor(wk3(F_ACC, 4, T), xT[:, 0:4, :], xT[:, 0:4, :], ALU.mult).then_inc(squared, 1)
            pool.wait_ge(x_copied, 8)
            pool.tensor_tensor(wk3(F_SQ, 4, T), xT[:, 4:8, :], xT[:, 4:8, :], ALU.mult).then_inc(squared, 1)
            add_squares(0)
            for f in range(2):
                scale_gate(f, 0)
                with pool.Fori(0, PARTS - 1) as i:
                    scale_gate(f, i + 1)
                add_squares(2 * f + 1)
                if f == 0:
                    mix_traffic()
                    add_squares(2)

        @block.scalar
        def _(act):
            def hi(n, i=0, cols=None):
                act.wait_ge(raw_in[n % RAW_SLOTS], raw_value(n, i))
                if n >= SPLIT_SLOTS:
                    act.wait_ge(unit_used, n - SPLIT_SLOTS + 1 + 12 * i)
                if cols is None:
                    act.copy(w_hi[:, n % SPLIT_SLOTS, :], raw[:, n % RAW_SLOTS, :]).then_inc(hi_done, 1)
                else:
                    for c, (to, at, w) in enumerate(cols):
                        last = act.copy(unit_cols(w_hi, n % SPLIT_SLOTS, to, w),
                                        unit_cols(raw, n % RAW_SLOTS, at, w))
                    last.then_inc(hi_done, 1)

            def next_hi(s, i=0):
                if s + 1 < U_END:
                    hi(s + 1, i, KV_COLS if U_Z + 28 <= s + 1 < U_Z + 32 else None)

            def moving_hi(e, q, col):
                for j in range(4 * q, 4 * q + 4):
                    last = act.activation(mov_hi[:, j, :], xT[:, j, :], ACT.Copy, scale=gains[:, col + j:col + j + 1])
                last.then_inc(mov_hi_done, 1)

            def square(e, q):
                if q >= 2:
                    act.wait_ge(sq_added, 3 * e + q - 1)
                act.activation(wk(F_ACC if q == 0 else F_SQ, 4 * T),
                               xT[:, 4 * q:4 * q + 4, :].rearrange("p a b -> p (a b)"),
                               ACT.Square).then_inc(squared, 1)

            def root(e):
                act.wait_ge(mean_ready, e + 1)
                act.activation(wk(F_T, T), wk(F_V, T), ACT.Sqrt).then_inc(root_ready, 1)

            def ffn(f, u0, g0):
                def silu(i):
                    act.wait_ge(drained, (g0 + 3 + 6 * (i - 1)) if not isinstance(i, int) else (g0 + 1))
                    act.activation(wk(F_GS, 4 * T), wk(F_GS, 4 * T), ACT.Silu).then_inc(silu_done, 1)

                def split_h(g, i):
                    act.wait_ge(drained, g + 1 + 6 * i)
                    act.copy(h_hi[:, 0:4 * T], wk(F_H, 4 * T)).then_inc(h_hi_done, 1)

                for j in range(8):
                    next_hi(u0 + j)
                    if f == 1 and j == 0:
                        out_steps(3)
                    if f == 0 and j < 2:
                        first_moving_hi(2 + j)
                        square(0, 2 + j)
                    if j == 2:
                        root(2 * f)
                    if j == 4:
                        silu(0)
                with act.Fori(0, PARTS - 1) as i:
                    for j in range(12):
                        next_hi(u0 + 8 + j, i)
                        if j == 0:
                            split_h(g0 + 1, i)
                        if j == 4:
                            silu(i + 1)
                for k in range(4):
                    if k < 3:
                        act.wait_ge(h_tile, 3 * (PARTS * (f + 1) - 1) + k + 1)
                    else:
                        act.wait_ge(drained, g0 + FFN_GROUPS - 4)
                    act.copy(h_hi[:, T * k:T * k + T], wk(F_H + T * k, T)).then_inc(h_hi_done, 1)
                def last_steps(q):
                    act.wait_ge(drained, g0 + FFN_GROUPS - 4 + q + 1)
                    if f == 0:
                        moving_hi(1, q, G_MIX)
                    square(2 * f + 1, q)

                for q in range(4):
                    next_hi(u0 + FFN_UNITS - 4 + q)
                    if f == 1 and q == 0:
                        act.wait_ge(tok_set, 1)
                        act.activation(tok[:, 11:12], tok[:, 10:11], ACT.Sqrt)
                    if q > 0:
                        last_steps(q - 1)
                if f == 0:
                    next_hi(U_Z)
                last_steps(3)

            def out_steps(q):
                act.wait_ge(drained, GR_OB + 4 + q + 1)
                square(2, q)
                if q == 3:
                    act.wait_ge(unit_used, U_F2)
                moving_hi(2, q, G_F2)

            act.wait_ge(gains_set, 1)
            def first_moving_hi(q):
                act.wait_ge(x_copied, 4 * q + 4)
                moving_hi(0, q, G_F1)

            first_moving_hi(0)
            hi(0)
            first_moving_hi(1)
            ffn(0, 0, 0)

            def z_steps(z):
                for j in range(4):
                    if z % 3 or j:
                        next_hi(U_Z + 4 * z + j)
                    if z == 0 and j == 2:
                        root(1)
                    if z in (3, 6) and j == 2:
                        norm_root(z // 3, D_CKT, D_CV, 4 * T)
                    if z == 1 and j == 2:
                        act.wait_ge(lam_sum, 1)
                        act.activation(lam[:, 0:2], ps[:, 0, 0:2], ACT.Exp).then_inc(lam_exp, 1)
                    if z in (2, 5):
                        job_steps(z // 3, j)
                    if z == 7:
                        latent_steps(j)

            def drain_job(n, dst, src):
                act.wait_ge(job_ready, n + 1)
                act.copy(dst, src).then_inc(job_drained, 1)

            def exps(c, src, p, scale):
                act.wait_ge(max_ready, c + 1)
                st = stat[:, c % 2, :]
                for k, (a, w) in enumerate(SEGS):
                    last = act.activation(wk(p + a, w), src(a, w), ACT.Exp, bias=st[:, 5 + k:6 + k],
                                          scale=scale, accum_out=st[:, 10 + k:11 + k])
                last.then_inc(exp_done, 1)

            def norm_root(k, v, y, n):
                act.wait_ge(n_mean, k)
                act.activation(wk(y, n), wk(v, n), ACT.Sqrt).then_inc(n_root, 1)

            def da_exps(h):
                p = D_P + PW * (h % 2)
                exps(h, lambda a, w: wk(p + a, w), p, DA_SCALE)

            def job_steps(hf, j):
                if j == 1:
                    for t, (r0, rows) in enumerate(TOK):
                        n = 10 * hf + t
                        drain_job(n, wk(D_KTOK + UC * t, UC, slice(0, rows)), ps[0:rows, job_bank(n), :])
                if j == 2:
                    for hh in range(HB):
                        n = 10 * hf + 3 + hh
                        drain_job(n, wk(D_CKT + PAST * hh, PAST), ps[:, job_bank(n), :])
                if j == 3:
                    da_exps(HB * hf)

            for hf in range(2):
                for z in range(3 * hf, 3 * hf + 3):
                    z_steps(z)
                if hf == 1:
                    act.wait_ge(v_stored, 16 * 3)
                for t, (r0, rows) in enumerate(TOK):
                    n = 10 * hf + 7 + t
                    drain_job(n, wk(D_VTOK + UC * t, UC, slice(0, rows)), ps[0:rows, job_bank(n), :])

                def da_copy(h):
                    act.wait_ge(at_ready, h + 1)
                    b = 4 * hf
                    act.copy(wk(D_AT, 384), ps[:, b, 0:384])
                    act.copy(wk(D_AT + 384, 256), ps[:, b + 1, 0:256])
                    act.copy(wk(D_AT + 640, 64, slice(0, 64)), ps[0:64, b + 1, 256:320]).then_inc(at_copied, 1)

                h0 = HB * hf
                for h in range(h0, h0 + HB):
                    if h + 2 < h0 + HB:
                        da_exps(h + 1)
                    da_copy(h)
                    if h + 2 == h0 + HB:
                        da_exps(h + 1)
                    if h == h0:
                        next_hi(U_Z + 4 * (3 * hf + 3))
                act.wait_ge(o_copied, h0 + HB)
                act.activation(wk(D_KT, 4 * T), wk(D_QT, 4 * T), ACT.Square).then_inc(n_sq, 1)

            def o_hi(hf, at):
                act.wait_ge(n_out, hf + 1)
                act.wait_ge(unit_used, U_Z + 28 + hf + 1)
                act.copy(mov_hi[:, 4 * hf:4 * hf + 4, :].rearrange("p a b -> p (a b)"),
                         wk(at, 4 * T)).then_inc(o_hi_done, 1)

            def latent_steps(j):
                if j == 1:
                    o_hi(0, D_O0)
                if j == 2:
                    act.wait_ge(drained, GR_Z + 7)
                    act.activation(wk(M_SQ, 4 * T), wk(M_CQ, 4 * T), ACT.Square).then_inc(n_sq, 1)
                    o_hi(1, D_O1)
                if j == 3:
                    drain_job(JOB_CC, wk(M_KR + T, PAST), ps[:, job_bank(JOB_CC), :])
                    norm_root(3, M_V, M_Y, T)

            z_steps(6)
            z_steps(7)
            next_hi(U_OA)
            act.wait_ge(drained, GR_Z + 8)
            act.activation(wk(M_SQ2, 2 * T), wk(M_CKV, 2 * T), ACT.Square).then_inc(n_sq, 1)
            next_hi(U_OA + 1)
            act.wait_ge(o_lo_done, 2)
            for a in range(2):
                drain_job(JOB_CC + 1 + a, wk(M_CCT + PAST * a, PAST), ps[:, job_bank(JOB_CC + 1 + a), :])
            norm_root(4, M_V, M_Y, T)
            next_hi(U_OA + 2)
            act.wait_ge(n_out, 3)
            act.copy(h_hi[:, 0:4 * T], wk(M_CQ, 4 * T)).then_inc(n_hi, 1)
            next_hi(U_OA + 3)
            for t, (r0, rows) in enumerate(TOK):
                n = JOB_CTOK + t
                drain_job(n, wk(M_CTOK + T * t, T, slice(0, rows)), ps[0:rows, job_bank(n), 0:T])
            act.wait_ge(job_drained, JOB_CTOK + 3)
            for t, (r0, rows) in enumerate(TOK):
                dc = ckv_prompt[0, 0, r0:r0 + rows, :] if t < 2 else ckv_sample[0, 0]
                dk = kr_prompt[0, 0, r0:r0 + rows, :] if t < 2 else kr_sample[0, 0]
                at = M_CTOK + T * t
                act.dma_start(dc, wk(at, KVL, slice(0, rows))).then_inc(ctok_stored, 16)
                act.dma_start(dk, wk(at + KVL, ROPE, slice(0, rows))).then_inc(ctok_stored, 16)
            for j in range(3):
                next_hi(U_UQ + j)
            next_hi(U_OA2)
            act.wait_ge(unit_used, U_UQ + 3)
            act.copy(latents(h_hi)[:, :, 0:T], wk3(M_CKV, 2, T))
            act.copy(latents(h_hi)[:, :, T:NTOK], wk3(M_CCT, 2, PAST)).then_inc(n_hi, 1)
            next_hi(U_OA2 + 1)

            for hb in range(2):
                next_hi(U_UKV[hb])
                jk = JOB_KV + 15 * hb
                for hh in range(HB):
                    for part, (t0, w) in enumerate(((0, T), (T, PAST))):
                        n = jk + 2 * hh + part
                        drain_job(n, wk(M_KN + NTOK * hh + t0, w), ps[:, job_bank(n), 0:w])
                act.wait_ge(ctok_stored, 16 * 6)
                for t in range(7):
                    n = jk + 8 + t
                    drain_job(n, wk(M_VM + UC * t, UC), ps[:, job_bank(n), :])
                for j in range(2):
                    next_hi(U_UKV[hb] + 1 + j)

                def mla_exps(c):
                    act.wait_ge(at_ready, c)
                    exps(c, score_seg, M_P, MLA_SCALE)

                c0 = HEADS + 2 * hb
                mla_exps(c0)
                for c in (c0, c0 + 1):
                    act.wait_ge(at_ready, c + 1)
                    act.copy(wk3(M_AT, 2, 384), ps[:, 4:6, 0:384])
                    act.copy(wk(M_AT + 768, 512), ps[:, 6, :])
                    act.copy(wk(M_AT + 1280, P, slice(0, 64)), ps[0:64, 7, 0:P]).then_inc(at_copied, 1)
                    if c == c0:
                        mla_exps(c + 1)
                    act.wait_ge(o_ready, c + 1)
                    j = 2 * c - HEADS
                    act.copy(mov_hi[:, j:j + 2, :], ps[:, 4:6, 0:T]).then_inc(o_hi_done, 1)

            next_hi(U_OB + 2)
            next_hi(U_OB + 3)
            for q in range(4):
                next_hi(U_OB + 4 + q)
                if q > 0:
                    out_steps(q - 1)
            ffn(1, U_F2, GR_F2)
            act.wait_ge(tok_mean, 1)
            act.activation(tok[:, 3:6], tok[:, 0:3], ACT.Sqrt).then_inc(tok_root, 1)
            act.wait_ge(tok_rstd, 1)
            for n, (j, t, r0, rows) in enumerate(Y_JOBS):
                if n % 2 == 0:
                    act.wait_ge(y_turned, n + 1)
                    act.activation(wk(Y_TOK + t * D + UC * j, UC, slice(0, rows)), ps[0:rows, y_bank(n), :], ACT.Copy,
                                   scale=tok[0:rows, 6 + t:7 + t]).then_inc(y_even, 1)

        @block.vector
        def _(dve):
            chain = [0]

            def link(ins):
                chain[0] += 1
                ins.then_inc(dve_chain, 1)
                dve.wait_ge(dve_chain, chain[0])

            def lo(n, i=0, cols=None):
                dve.wait_ge(hi_done, n + 1 + 12 * i)
                if cols is None:
                    dve.tensor_tensor(w_lo[:, n % SPLIT_SLOTS, :], raw[:, n % RAW_SLOTS, :],
                                      w_hi[:, n % SPLIT_SLOTS, :].bitcast(F32), ALU.subtract).then_inc(lo_done, 1)
                else:
                    for to, at, w in cols:
                        last = dve.tensor_tensor(unit_cols(w_lo, n % SPLIT_SLOTS, to, w),
                                                 unit_cols(raw, n % RAW_SLOTS, at, w),
                                                 unit_cols(w_hi, n % SPLIT_SLOTS, to, w).bitcast(F32), ALU.subtract)
                    last.then_inc(lo_done, 1)

            def next_lo(s, i=0):
                if s + 1 < U_END:
                    lo(s + 1, i, KV_COLS if U_Z + 28 <= s + 1 < U_Z + 32 else None)

            def moving_lo(e, q, col):
                dve.wait_ge(mov_hi_done, 4 * e + q + 1)
                for j in range(4 * q, 4 * q + 4):
                    last = dve.scalar_tensor_tensor(mov_lo[:, j, :], xT[:, j, :], gains[:, col + j:col + j + 1],
                                                    mov_hi[:, j, :].bitcast(F32), ALU.mult, ALU.subtract)
                last.then_inc(mov_lo_done, 1)

            def newton(v, y, a, n):
                v, y, a = wk(v, n), wk(y, n), wk(a, n)
                link(dve.tensor_tensor(a, y, y, ALU.mult))
                link(dve.scalar_tensor_tensor(a, a, -0.5, v, ALU.mult, ALU.mult))
                return y, a

            def norm(e, bank):
                dve.wait_ge(sum_ready, e + 1)
                dve.tensor_scalar(wk(F_V, T), ps[:, bank, 0:T], 1.0 / D, EPS, ALU.mult, ALU.add).then_inc(mean_ready, 1)
                dve.wait_ge(root_ready, e + 1)
                link(dve.reciprocal(wk(F_T, T), wk(F_T, T)))
                y, a = newton(F_V, F_T, F_SQ, T)
                dve.scalar_tensor_tensor(rstd[:, :], a, 1.5, y, ALU.add, ALU.mult).then_inc(rstd_ready, 1)
                dve.wait_ge(rstd_ready, e + 1)

            def ffn(f, u0, g0):
                def drain_gate(s, i, g):
                    dve.wait_ge(unit_used, s + 1 + 12 * i)
                    dve.tensor_tensor(wk3(F_GS, 4, T), bank4(g), R4, ALU.mult).then_inc(drained, 1)

                def drain_up(s, i, g, part):
                    dve.wait_ge(unit_used, s + 1 + 12 * i)
                    dve.wait_ge(gate_scaled, PARTS * f + 1 + part)
                    for k in range(4):
                        dve.tensor_tensor(wk(F_H + T * k, T), bank4(g)[:, k, :], wk(F_GS + T * k, T),
                                          ALU.mult).then_inc(h_tile if k < 3 else drained, 1)

                def h_lows(i):
                    dve.wait_ge(h_hi_done, H_STEPS * f + 1 + i)
                    dve.tensor_tensor(h_lo[:, 0:4 * T], wk(F_H, 4 * T), h_hi[:, 0:4 * T].bitcast(F32),
                                      ALU.subtract).then_inc(h_lo_done, 1)

                def drain_down(s, i, g, q):
                    dve.wait_ge(unit_used, s + 1 + 12 * i)
                    dve.scalar_tensor_tensor(xT[:, 4 * q:4 * q + 4, :], bank4(g), 0.5, xT[:, 4 * q:4 * q + 4, :],
                                             ALU.mult, ALU.add).then_inc(drained, 1)

                for j in range(8):
                    next_lo(u0 + j)
                    if f == 1 and j == 0:
                        moving_lo(2, 2, G_F2)
                        moving_lo(2, 3, G_F2)
                    if f == 0 and j < 2:
                        moving_lo(0, 2 + j, G_F1)
                    if f == 0 and j == 0:
                        copy_x(3)
                    if j == 2:
                        norm(2 * f, 4 * ((g0 + 1) % 2))
                    if j == 3:
                        drain_gate(u0 + 3, 0, g0)
                drain_up(u0 + 7, 0, g0 + 1, 0)
                with dve.Fori(0, PARTS - 1) as i:
                    for j in range(12):
                        s = u0 + 8 + j
                        next_lo(s, i)
                        if j == 0:
                            h_lows(i)
                        if j == 3:
                            drain_gate(s, i, g0 + 2)
                        if 4 <= j < 8:
                            drain_down(s, i, g0 + 3 + j - 4, j - 4)
                    drain_up(u0 + 19, i, g0 + 7, i + 1)
                for k in range(4):
                    sl = slice(T * k, T * k + T)
                    dve.wait_ge(h_hi_done, H_STEPS * f + PARTS + k)
                    dve.tensor_tensor(h_lo[:, sl], wk(F_H + T * k, T), h_hi[:, sl].bitcast(F32),
                                      ALU.subtract).then_inc(h_lo_done, 1)
                for q in range(4):
                    s = u0 + FFN_UNITS - 4 + q
                    next_lo(s)
                    if f == 0 and q > 1:
                        moving_lo(1, q - 2, G_MIX)
                    if f == 1 and q > 0:
                        scale_y(q - 1)
                    drain_down(s, 0, g0 + FFN_GROUPS - 4 + q, q)
                if f == 0:
                    next_lo(U_Z)
                    moving_lo(1, 2, G_MIX)
                    moving_lo(1, 3, G_MIX)
                else:
                    scale_y(3)

            def scale_y(q):
                dve.wait_ge(squared, 4 * 3 + q + 1)
                for j in range(4 * q, 4 * q + 4):
                    last = dve.tensor_scalar(xT[:, j, :], xT[:, j, :], gains[:, G_FIN + j:G_FIN + j + 1],
                                             None, ALU.mult)
                last.then_inc(y_scaled, 1)

            dve.memset(tok[:, :], 1.0).then_inc(tok_set, 1)
            def copy_x(q):
                for j in range(4 * q, 4 * q + 4):
                    dve.wait_ge(x_turned, j + 1)
                    dve.tensor_copy(xT[:, j, :], ps[:, x_bank(j), 0:T]).then_inc(x_copied, 1)

            copy_x(0)
            dve.wait_ge(gains_turned, 1)
            dve.tensor_copy(gains[:, :], ps[:, 7, 0:G_ALL]).then_inc(gains_set, 1)
            dve.tensor_copy(lamin[:, 0:4], ps[0:HALF, 7, 128:132]).then_inc(gains_set, 1)
            copy_x(1)
            moving_lo(0, 0, G_F1)
            lo(0)
            copy_x(2)
            moving_lo(0, 1, G_F1)
            ffn(0, 0, 0)

            def z_drain(z, dst, tiles=4):
                dve.wait_ge(unit_used, U_Z + 4 * z + 4)
                dve.tensor_tensor(wk3(dst, tiles, T), bank4(GR_Z + z)[:, 0:tiles, :], over(rstd[:, :], tiles),
                                  ALU.mult).then_inc(drained, 1)

            def z_steps(z, before=None):
                for j in range(4):
                    if z % 3 or j:
                        next_lo(U_Z + 4 * z + j)
                    if z == 0 and j == 2:
                        norm(1, 4 * ((GR_Z + 1) % 2))
                    if z in (3, 6):
                        da_norm(z // 3 - 1, j)
                    if z in (4, 7):
                        da_norm(z // 3 - 1, 4 + j)
                        if j == 1:
                            dve.wait_ge(n_out, z // 3)
                            z_drain(z - 1, before)
                    if z in (2, 5) and j == 3:
                        bias_and_max(HB * (z // 3))
                    if z == 7:
                        latent_steps(j)

            def inverse_sums(c):
                dve.wait_ge(exp_done, c + 1)
                st = stat[:, c % 2, :]
                link(dve.reciprocal(st[:, 15:20], st[:, 10:15]))
                return st

            def maxes(c, prompt, sample, scale):
                st = stat[:, c % 2, :]
                dve.tensor_reduce(st[:, 0:2], prompt[:, :, 0:SEQ], AX_X, ALU.max)
                dve.tensor_reduce(st[:, 2:4], prompt[:, :, SEQ:PH], AX_X, ALU.max)
                link(dve.tensor_reduce(st[:, 4:5], sample, AX_X, ALU.max))
                dve.tensor_scalar(st[:, 5:10], st[:, 0:5], -scale, None, ALU.mult).then_inc(max_ready, 1)

            def bias_and_max(h):
                if h == 0:
                    dve.wait_ge(tab_in, 16)
                p, b = D_P + PW * (h % 2), scores_half(h // HB)
                s8 = -SLOPES[h] / DA_SCALE
                dve.wait_ge(scores_ready, h + 1)
                dve.wait_ge(k_stored, 16 * 3 * (h // HB + 1))
                if h >= 2:
                    dve.wait_ge(at_ready, h - 1)
                dve.scalar_tensor_tensor(wk3(p, 2, PH), over(tab[:, C_DIST:C_DIST + PH], 2), s8,
                                         ps[:, b:b + 2, 0:PH], ALU.mult, ALU.add)
                dve.scalar_tensor_tensor(wk(p + 768, KEYS), tab[:, C_DISTS:C_DISTS + KEYS], s8,
                                         score_seg(768, KEYS, b), ALU.mult, ALU.add).then_inc(biased, 1)
                dve.wait_ge(biased, h + 1)
                maxes(h, wk3(p, 2, PH), wk(p + 2 * PH, KEYS), DA_SCALE)

            def da_norm(hf, j):
                if j == 1:
                    dve.wait_ge(n_sum, hf + 1)
                    dve.tensor_scalar(wk3(D_CKT, 4, T), ps[:, 4 * hf:4 * hf + 4, 0:T], 1.0 / DH, EPS, ALU.mult,
                                      ALU.add).then_inc(n_mean, 1)
                if j in (2, 3):
                    dve.wait_ge(n_root, hf + 1)
                    y = wk(D_CV + 2 * T * (j - 2), 2 * T)
                    link(dve.reciprocal(y, y))
                if j == 4:
                    newton(D_CKT, D_CV, D_KT, 4 * T)
                if j == 5:
                    y, a = wk(D_CV, 4 * T), wk(D_KT, 4 * T)
                    link(dve.scalar_tensor_tensor(y, a, 1.5, y, ALU.add, ALU.mult))
                    dve.scalar_tensor_tensor(wk(D_O1 if hf else D_O0, 4 * T), wk(D_QT, 4 * T),
                                             gains[:, G_SUB:G_SUB + 1], y, ALU.mult, ALU.mult).then_inc(n_out, 1)

            for hf in range(2):
                z_steps(3 * hf)
                if hf == 0:
                    z_drain(0, D_QT)
                    dve.tensor_tensor(lamin[:, 4:6], lamin[:, 0:2], lamin[:, 2:4], ALU.mult).then_inc(lam_sq, 1)
                    dve.tensor_scalar(gains[:, G_SUB:G_SUB + 1], gains[:, G_SUB:G_SUB + 1], 1.0 - LAM_INIT, None,
                                      ALU.mult)
                    link(dve.memset(lam[:, 5:10], 1.0))
                z_steps(3 * hf + 1, D_QT)
                z_drain(3 * hf + 1, D_KT)
                if hf == 0:
                    dve.wait_ge(lam_exp, 1)
                    link(dve.scalar_tensor_tensor(lam[:, 6:7], lam[:, 1:2], LAM_INIT, lam[:, 0:1],
                                                  ALU.subtract, ALU.subtract))
                    dve.tensor_copy(lam[:, 8:9], lam[:, 6:7])
                    link(dve.tensor_copy(lam[64:128, 9:10], lam[64:128, 6:7]))
                z_steps(3 * hf + 2)
                z_drain(3 * hf + 2, D_VT)
                def da_diag(h):
                    st = inverse_sums(h)
                    link(dve.tensor_tensor(st[:, 15:20], st[:, 15:20], lam[:, 5:10], ALU.mult))
                    if h >= 1:
                        dve.wait_ge(at_ready, h)
                    for k in range(4):
                        dve.tensor_scalar(diagonal(k), ident, st[:, 15 + k:16 + k], None, ALU.mult)
                    dve.tensor_scalar(diagonal(4), tab[:, C_STACK:C_STACK + 64], st[:, 19:20], None,
                                      ALU.mult).then_inc(diag_ready, 1)

                def copy_o(h):
                    dve.wait_ge(o_ready, h + 1)
                    dve.tensor_copy(wk(D_QT + T * (h % HB), T), ps[:, 4 * hf + 2 + h % 2, 0:T]).then_inc(o_copied, 1)

                h0 = HB * hf
                da_diag(h0)
                for h in range(h0 + 1, h0 + HB):
                    bias_and_max(h)
                    if h == h0 + HB - 1:
                        next_lo(U_Z + 4 * (3 * hf + 3))
                    if h > h0 + 1:
                        copy_o(h - 2)
                    da_diag(h)
                copy_o(h0 + HB - 2)
                copy_o(h0 + HB - 1)

            def o_lo(hf, at):
                dve.wait_ge(o_hi_done, hf + 1)
                sl = slice(4 * hf, 4 * hf + 4)
                dve.tensor_tensor(mov_lo[:, sl, :].rearrange("p a b -> p (a b)"), wk(at, 4 * T),
                                  mov_hi[:, sl, :].rearrange("p a b -> p (a b)").bitcast(F32),
                                  ALU.subtract).then_inc(o_lo_done, 1)

            def latent_mean(k, bank, tiles):
                dve.wait_ge(n_sum, k)
                dve.tensor_scalar(wk(M_V, T), ps[:, bank, 0:T], 1.0 / (P * tiles), EPS, ALU.mult,
                                  ALU.add).then_inc(n_mean, 1)

            def latent_norm(k, at, tiles, col):
                dve.wait_ge(n_root, k)
                link(dve.reciprocal(wk(M_Y, T), wk(M_Y, T)))
                y, a = newton(M_V, M_Y, M_T, T)
                link(dve.scalar_tensor_tensor(y, a, 1.5, y, ALU.add, ALU.mult))
                for j in range(tiles):
                    last = dve.scalar_tensor_tensor(wk(at + T * j, T), wk(at + T * j, T),
                                                    gains[:, col + j:col + j + 1], y, ALU.mult, ALU.mult)
                last.then_inc(n_out, 1)

            def latent_steps(j):
                if j == 2:
                    o_lo(0, D_O0)
                    o_lo(1, D_O1)
                    latent_mean(3, 0, 4)
                if j == 3:
                    latent_norm(3, M_CQ, 4, G_Q)

            def drain_out(s, g, c):
                dve.wait_ge(unit_used, s + 1)
                dve.tensor_tensor(xT[:, 4 * c:4 * c + 4, :], bank4(g), xT[:, 4 * c:4 * c + 4, :],
                                  ALU.add).then_inc(drained, 1)

            z_steps(6)
            z_steps(7, M_CQ)
            z_drain(7, M_CKV, 3)
            cos, sin = tab[:, C_COS:C_COS + T], tab[:, C_SIN:C_SIN + T]
            next_lo(U_OA)
            dve.wait_ge(swap_ready, 1)
            dve.tensor_tensor(wk(M_RT, T), wk(M_KRAW, T), cos, ALU.mult)
            link(dve.tensor_tensor(wk(M_RT + T, T), ps[:, 6, 0:T], sin, ALU.mult))
            dve.tensor_tensor(wk(M_KR, T), wk(M_RT, T), wk(M_RT + T, T), ALU.add).then_inc(roped, 1)
            latent_mean(4, 7, 2)
            next_lo(U_OA + 1)
            latent_norm(4, M_CKV, 2, G_KV)
            drain_out(U_OA + 1, GR_OA, 0)
            next_lo(U_OA + 2)
            dve.wait_ge(n_hi, 1)
            dve.tensor_tensor(h_lo[:, 0:4 * T], wk(M_CQ, 4 * T), h_hi[:, 0:4 * T].bitcast(F32),
                              ALU.subtract).then_inc(n_lo, 1)
            next_lo(U_OA + 3)
            drain_out(U_OA + 3, GR_OA + 1, 1)
            for j in range(3):
                next_lo(U_UQ + j)
                dve.wait_ge(unit_used, U_UQ + j + 1)
                dve.tensor_copy(wk3((M_QR, M_QN, M_QN + 4 * T)[j], 4, T), bank4(GR_UQ + j)).then_inc(drained, 1)
            next_lo(U_OA2)
            dve.wait_ge(swap_ready, 2)
            dve.tensor_tensor(wk3(M_RT, 4, T), bank4(GR_ROPE), over(sin, 4), ALU.mult).then_inc(drained, 1)
            link(dve.tensor_tensor(wk3(M_QR, 4, T), wk3(M_QR, 4, T), over(cos, 4), ALU.mult))
            dve.wait_ge(drained, GR_ROPE + 1)
            dve.tensor_tensor(wk(M_QR, 4 * T), wk(M_QR, 4 * T), wk(M_RT, 4 * T), ALU.add).then_inc(roped, 1)
            dve.wait_ge(n_hi, 2)
            dve.tensor_tensor(latents(h_lo)[:, :, 0:T], wk3(M_CKV, 2, T), latents(h_hi)[:, :, 0:T].bitcast(F32),
                              ALU.subtract)
            dve.tensor_tensor(latents(h_lo)[:, :, T:NTOK], wk3(M_CCT, 2, PAST),
                              latents(h_hi)[:, :, T:NTOK].bitcast(F32), ALU.subtract).then_inc(n_lo, 1)
            next_lo(U_OA2 + 1)
            drain_out(U_OA2 + 1, GR_OA2, 2)

            def mask_and_max(c):
                dve.wait_ge(scores_ready, c + 1)
                for end in (SEQ, PH):
                    hidden = ps[0:64, 0:2, end - 64:end]
                    ins = dve.tensor_scalar(hidden, hidden, NEG, None, ALU.add)
                link(ins)
                maxes(c, ps[:, 0:2, 0:PH], score_seg(2 * PH, KEYS), MLA_SCALE)

            def mla_diag(c):
                st = inverse_sums(c)
                dve.wait_ge(at_ready, c)
                for k in range(5):
                    ins = dve.tensor_scalar(wk(M_DG + P * k, P), ident, st[:, 15 + k:16 + k], None, ALU.mult)
                ins.then_inc(diag_ready, 1)

            for hb in range(2):
                for j in range(3):
                    next_lo(U_UKV[hb] + j)
                    if hb == 1 and j == 1:
                        drain_out(U_OB, GR_OB, 0)
                c0 = HEADS + 2 * hb
                mask_and_max(c0)
                for c in (c0, c0 + 1):
                    mla_diag(c)
                    if c == c0:
                        if hb == 0:
                            drain_out(U_OA3 + 1, GR_OA3, 3)
                        else:
                            drain_out(U_OB + 1, GR_OB + 1, 1)
                        mask_and_max(c + 1)
                    j = 2 * c - HEADS
                    dve.wait_ge(o_hi_done, c - HEADS + 3)
                    dve.tensor_tensor(mov_lo[:, j:j + 2, :], ps[:, 4:6, 0:T], mov_hi[:, j:j + 2, :].bitcast(F32),
                                      ALU.subtract).then_inc(o_lo_done, 1)

            for j in range(2, 8):
                next_lo(U_OB + j)
                if j >= 6:
                    moving_lo(2, j - 6, G_F2)
                drain_out(U_OB + j, GR_OB + j, j % 4)
            ffn(1, U_F2, GR_F2)
            dve.wait_ge(tok_sum, 1)
            link(dve.tensor_scalar(tok[:, 0:2], ps[:, 3, 0:2], 1.0 / D, EPS, ALU.mult, ALU.add))
            dve.tensor_scalar(tok[0:DEC, 2:3], ps[0:DEC, 3, 2:3], 1.0 / D, EPS, ALU.mult, ALU.add).then_inc(tok_mean, 1)
            dve.wait_ge(tok_root, 1)
            y, a, v = tok[:, 3:6], tok[:, 6:9], tok[:, 0:3]
            link(dve.reciprocal(y, y))
            link(dve.tensor_tensor(a, y, y, ALU.mult))
            link(dve.tensor_tensor(a, a, v, ALU.mult))
            link(dve.tensor_scalar(a, a, -0.5, 1.5, ALU.mult, ALU.add))
            dve.tensor_tensor(a, a, y, ALU.mult).then_inc(tok_rstd, 1)
            dve.wait_ge(tok_rstd, 1)
            for n, (j, t, r0, rows) in enumerate(Y_JOBS):
                if n % 2 == 1:
                    dve.wait_ge(y_turned, n + 1)
                    dve.tensor_scalar(wk(Y_TOK + t * D + UC * j, UC, slice(0, rows)), ps[0:rows, y_bank(n), :],
                                      tok[0:rows, 6 + t:7 + t], None, ALU.mult).then_inc(y_odd, 1)

        @block.tensor
        def _(pe):
            def triple(out, w, x, first, last):
                pe.matmul(out, w[0], x[0], start=first, stop=False)
                pe.matmul(out, w[0], x[1], start=False, stop=False)
                return pe.matmul(out, w[1], x[0], start=False, stop=last)

            def unit(n, i, g, gi, moving, first, last, tiles=4, tile_ready=None, frees=False):
                pe.wait_ge(lo_done, n + 1 + 12 * i)
                if first and g >= 2:
                    pe.wait_ge(drained, half_free(g) + gi)
                out = bank4(g)
                order = ([(m, k) for m in range(tiles) for k in range(UK)] if tile_ready is None else
                         [(m, k) for k in range(UK) for m in range(tiles)])
                for m, k in order:
                    if tile_ready is not None and m == 0:
                        tile_ready(k)
                    c = UC * k + P * m
                    w = (w_hi[:, n % SPLIT_SLOTS, c:c + P], w_lo[:, n % SPLIT_SLOTS, c:c + P])
                    ins = triple(out[:, m, :], w, moving(k), first and k == 0, last and k == UK - 1)
                    if frees and m == 0 and k == 0:
                        ins.then_inc(unit_used, 1)
                ins.then_inc(unit_used, 1)

            def mov(q):
                return lambda k: (mov_hi[:, 4 * q + k, :], mov_lo[:, 4 * q + k, :])

            def hidden(k):
                return (h_hi[:, T * k:T * k + T], h_lo[:, T * k:T * k + T])

            def add_up(e, bank):
                pe.wait_ge(sq_added, 3 * e + 3)
                for a in range(4):
                    ins = pe.matmul(ps[:, bank, 0:T], ones[:, :], wk(F_ACC + T * a, T), start=(a == 0), stop=(a == 3))
                ins.then_inc(sum_ready, 1)

            def from_x(u, i, g, gi, e=None):
                for q in range(4):
                    if e is not None:
                        pe.wait_ge(mov_lo_done, 4 * e + q + 1)
                        if g == 0 and q == 1:
                            turn_x(3)
                        if q == 3:
                            if g:
                                pe.wait_ge(drained, g)
                            else:
                                pe.wait_ge(x_copied, KT)
                            add_up(e if e < 2 else 2, 4 * ((g + 1) % 2))
                    unit(u + q, i, g, gi, mov(q), q == 0, q == 3)

            def ffn(f, u0, g0):
                from_x(u0, 0, g0, 0, 2 * f)
                pe.wait_ge(mean_ready, 2 * f + 1)
                from_x(u0 + 4, 0, g0 + 1, 0)
                with pe.Fori(0, PARTS - 1) as i:
                    from_x(u0 + 8, i, g0 + 2, 6 * i)
                    pe.wait_ge(h_lo_done, H_STEPS * f + 1 + i)
                    for q in range(4):
                        unit(u0 + 12 + q, i, g0 + 3 + q, 6 * i, hidden, True, True)
                    from_x(u0 + 16, i, g0 + 7, 6 * i)
                for q in range(4):
                    unit(u0 + FFN_UNITS - 4 + q, 0, g0 + FFN_GROUPS - 4 + q, 0, hidden, True, True,
                         tile_ready=(lambda k: pe.wait_ge(h_lo_done, H_STEPS * f + PARTS + k)) if q == 0 else None)

            def turn_x(q):
                for j in range(4 * q, 4 * q + 4):
                    if j >= 8:
                        pe.wait_ge(x_copied, j - 3)
                    for t, (r0, rows) in enumerate(TOK):
                        ins = pe.transpose(ps[:, x_bank(j), r0:r0 + rows],
                                           wk(X_TOK + t * D + P * j, P, slice(0, rows)), tab[0:rows, C_ID:C_ID + rows])
                    ins.then_inc(x_turned, 1)

            pe.wait_ge(id_in, 16)
            for t in range(3):
                pe.wait_ge(x_in[t], 16)
            turn_x(0)
            pe.wait_ge(gains_in, 16 * 7)
            pe.wait_ge(lam_in, 16 * 4)
            pe.transpose(ps[:, 7, 0:G_ALL], wk(S_ROWS, P, slice(0, G_ALL)), tab[0:G_ALL, 0:G_ALL])
            pe.transpose(ps[0:HALF, 7, 128:132], wk(S_LROWS, HALF, slice(0, 4)), tab[0:4, 0:4]).then_inc(gains_turned, 1)
            pe.wait_ge(gains_set, 2)
            turn_x(1)
            turn_x(2)
            pe.wait_ge(ones_set, 1)
            pe.wait_ge(x_copied, 4)
            ffn(0, 0, 0)

            def z_unit(z, q):
                g = GR_Z + z
                if z == 0:
                    pe.wait_ge(mov_lo_done, 4 + q + 1)
                    if q == 3:
                        pe.wait_ge(drained, g)
                        add_up(1, 4 * ((g + 1) % 2))
                if z == 1 and q == 0:
                    pe.wait_ge(mean_ready, 2)
                if z == 2 and q == 0:
                    pe.wait_ge(lam_exp, 1)
                if z in (4, 7) and q == 0:
                    pe.wait_ge(n_mean, z // 3)
                unit(U_Z + 4 * z + q, 0, g, 0, mov(q), q == 0, q == 3, 4 if z < 7 else 3)
                if z == 1 and q == 0:
                    pe.wait_ge(drained, GR_Z + 1)
                    pe.wait_ge(lam_sq, 1)
                    pe.matmul(ps[:, 0, 0:2], ones[0:HALF, :], lamin[:, 4:6], start=True, stop=True).then_inc(lam_sum, 1)
                if z in (3, 6) and q == 1:
                    pe.wait_ge(n_sq, z // 3)
                    for a in range(4):
                        ins = pe.matmul(ps[:, 4 * (z // 3 - 1) + a, 0:T], ones[:, :], wk(D_KT + T * a, T),
                                        start=True, stop=True)
                    ins.then_inc(n_sum, 1)
                if z == 7 and q == 2:
                    pe.wait_ge(drained, GR_Z + 7)
                    pe.wait_ge(cc_in, 16 * 3)
                    latent_sum(3, 0, M_SQ, 4)
                    for kt in range(4):
                        ins = pe.transpose(ps[:, job_bank(JOB_CC), P * kt:P * kt + P], wk(M_CKR + P * kt, P), ident)
                    ins.then_inc(job_ready, 1)

            def z_group(z, q0=0):
                for q in range(q0, 4):
                    z_unit(z, q)

            def latent_sum(k, bank, at, tiles):
                pe.wait_ge(n_sq, k)
                for a in range(tiles):
                    ins = pe.matmul(ps[:, bank, 0:T], ones[:, :], wk(at + T * a, T), start=(a == 0),
                                    stop=(a == tiles - 1))
                ins.then_inc(n_sum, 1)

            for hf in range(2):
                z_group(3 * hf, 1 if hf else 0)
                z_group(3 * hf + 1)

                def turn_tokens(n0, at):
                    for t, (r0, rows) in enumerate(TOK):
                        if n0 % 10 and t == 2:
                            pe.wait_ge(job_drained, n0 + 1)
                        for hh in range(HB):
                            ins = pe.transpose(ps[0:rows, job_bank(n0 + t), P * hh:P * hh + P],
                                               wk(at + T * hh + r0, rows), ident)
                        ins.then_inc(job_ready, 1)

                def turn_cache(hh):
                    n = 10 * hf + 3 + hh
                    if hh:
                        pe.wait_ge(job_drained, n - 3)
                    for kt in range(4):
                        ins = pe.transpose(ps[:, job_bank(n), P * kt:P * kt + P], wk(D_CST + UC * kt + P * hh, P), ident)
                    ins.then_inc(job_ready, 1)

                def da_scores(h):
                    if h > HB * hf:
                        pe.wait_ge(biased, h)
                    hh, b = h % HB, scores_half(hf)
                    for half in range(2):
                        d = slice(HALF * half, HALF * half + HALF)
                        q, k = wk(D_QT + T * hh, T, d), wk(D_KT + T * hh, T, d)
                        pe.matmul(ps[:, b + half, 0:SEQ], q[:, P:SEQ], k[:, 0:SEQ], start=True, stop=True)
                        pe.matmul(ps[:, b + half, SEQ:PH], q[:, 0:P], k[:, 0:P], start=True, stop=True)
                        pe.matmul(ps[d, b + 2, :], q[:, SEQ:T], wk(D_CKT + PAST * hh, PAST, d), start=True, stop=True)
                        ins = pe.matmul(ps[d, b + 3, 0:DEC], q[:, SEQ:T], k[:, SEQ:T], start=True, stop=True)
                    ins.then_inc(scores_ready, 1)

                z_unit(3 * hf + 2, 0)
                pe.wait_ge(drained, GR_Z + 3 * hf + 2)
                turn_tokens(10 * hf, D_KT)
                z_unit(3 * hf + 2, 1)
                pe.wait_ge(ck_in, 16 * (hf + 1))
                for hh in range(HB):
                    turn_cache(hh)
                z_unit(3 * hf + 2, 2)
                pe.wait_ge(job_drained, 10 * hf + 7)
                da_scores(HB * hf)
                z_unit(3 * hf + 2, 3)

                def da_transpose(h):
                    pe.wait_ge(diag_ready, h + 1)
                    p = D_P + PW * (h % 2)
                    dg = [diagonal(k) for k in range(4)]
                    for col, at, k in ((0, SEQ, 2), (P, 0, 0), (SEQ, P, 0)):
                        out = ps[:, 4 * hf, col:col + P]
                        pe.matmul(out, wk(p + at, P), dg[k], start=True, stop=False)
                        pe.matmul(out, wk(p + at + PH, P), dg[k + 1], start=False, stop=True)
                    for kt in range(5):
                        rows = P if kt < 4 else DEC
                        ins = pe.matmul(ps[0:rows, 4 * hf + 1, 64 * kt:64 * kt + 64], wk(p + 768 + P * kt, rows),
                                        diagonal(4), start=True, stop=True)
                    ins.then_inc(at_ready, 1)

                def da_values(h):
                    pe.wait_ge(at_copied, h + 1)
                    if h == HB * hf:
                        pe.wait_ge(job_drained, 10 * hf + 10)
                        pe.wait_ge(cv_in, 16 * (hf + 1))
                    if h >= 2:
                        pe.wait_ge(o_copied, h - 1)
                    out = ps[:, 4 * hf + 2 + h % 2, :]
                    hd = P * (h % HB)
                    pe.matmul(out[:, 0:SEQ], wk(D_VTOK + hd, P), wk(D_AT, SEQ), start=True, stop=False)
                    pe.matmul(out[:, P:SEQ], wk(D_VTOK + UC + hd, P), wk(D_AT + SEQ, P), start=False, stop=True)
                    for kt in range(4):
                        pe.matmul(out[:, SEQ:T], wk(D_CV + UC * kt + hd, P), wk(D_AT + 384 + 64 * kt, 64),
                                  start=(kt == 0), stop=False)
                    new = slice(0, DEC)
                    pe.matmul(out[:, SEQ:T], wk(D_VTOK + 2 * UC + hd, P, new), wk(D_AT + 640, 64, new),
                              start=False, stop=True).then_inc(o_ready, 1)

                h0 = HB * hf
                da_scores(h0 + 1)
                pe.wait_ge(drained, GR_Z + 3 * hf + 3)
                turn_tokens(10 * hf + 7, D_VT)
                for h in range(h0, h0 + HB):
                    if h == h0 + HB - 1:
                        pe.wait_ge(biased, h + 1)
                        z_unit(3 * hf + 3, 0)
                    da_transpose(h)
                    if h + 2 < h0 + HB:
                        da_scores(h + 2)
                    da_values(h)
            z_group(6, 1)
            z_group(7)

            def out_unit(n, g, q, first=True, last=True, frees=False):
                unit(n, 0, g, 0, mov(q), first, last, frees=frees)

            swap = tab[:, C_SWAP:C_SWAP + P]
            pe.wait_ge(n_mean, 3)
            pe.wait_ge(job_drained, JOB_CC + 1)
            pe.wait_ge(o_lo_done, 2)
            out_unit(U_OA, GR_OA, 0, last=False)
            pe.wait_ge(drained, GR_Z + 8)
            pe.matmul(ps[:, 6, 0:T], swap, wk(M_KRAW, T), start=True, stop=True).then_inc(swap_ready, 1)
            latent_sum(4, 7, M_SQ2, 2)
            for a in range(2):
                for kt in range(4):
                    ins = pe.transpose(ps[:, job_bank(JOB_CC + 1 + a), P * kt:P * kt + P],
                                       wk(M_CCKV + KVL * kt + P * a, P), ident)
                ins.then_inc(job_ready, 1)
            out_unit(U_OA + 1, GR_OA, 1, first=False)
            pe.wait_ge(n_mean, 4)
            pe.wait_ge(roped, 1)
            pe.wait_ge(job_drained, JOB_CTOK)
            out_unit(U_OA + 2, GR_OA + 1, 0, last=False)
            pe.wait_ge(drained, GR_OA + 1)
            pe.wait_ge(n_out, 4)
            for t, (r0, rows) in enumerate(TOK):
                b = job_bank(JOB_CTOK + t)
                for a in range(2):
                    pe.transpose(ps[0:rows, b, P * a:P * a + P], wk(M_CKV + T * a + r0, rows), ident)
                pe.transpose(ps[0:rows, b, KVL:KVL + ROPE], wk(M_KR + r0, rows, slice(0, ROPE)),
                             tab[0:ROPE, C_ID:C_ID + ROPE]).then_inc(job_ready, 1)
            out_unit(U_OA + 3, GR_OA + 1, 1, first=False)
            pe.wait_ge(job_drained, JOB_CTOK + 3)
            pe.wait_ge(n_lo, 1)
            for j in range(3):
                unit(U_UQ + j, 0, GR_UQ + j, 0, hidden, True, True)
            pe.wait_ge(drained, GR_UQ + 2)
            for a in range(4):
                ins = pe.matmul(bank4(GR_ROPE)[:, a, :], swap, wk(M_QR + T * a, T), start=True, stop=True)
            ins.then_inc(swap_ready, 1)
            for q in range(2):
                out_unit(U_OA2 + q, GR_OA2, q, q == 0, q == 1)
            pe.wait_ge(roped, 2)
            pe.wait_ge(n_lo, 2)

            for hb in range(2):
                n = U_UKV[hb]
                jk = JOB_KV + 15 * hb
                pe.wait_ge(lo_done, n + 1)
                if hb == 0:
                    pe.wait_ge(drained, GR_ROPE + 1)

                def start_job(j):
                    if hb == 0 and j - jk == 4:
                        pe.wait_ge(drained, GR_OA2 + 1)
                    if hb == 1 and j - jk == 4:
                        pe.wait_ge(o_lo_done, 4)
                    if j - jk >= 8:
                        pe.wait_ge(job_drained, j - 7)

                def wslice(k, hh, v):
                    c = 1024 * k + 256 * hh + P * v
                    return (w_hi[:, n % SPLIT_SLOTS, c:c + P], w_lo[:, n % SPLIT_SLOTS, c:c + P])

                for hh in range(HB):
                    for part, (t0, w) in enumerate(((0, T), (T, PAST))):
                        j = jk + 2 * hh + part
                        start_job(j)
                        for k in range(2):
                            c = (latents(h_hi)[:, k, t0:t0 + w], latents(h_lo)[:, k, t0:t0 + w])
                            ins = triple(ps[:, job_bank(j), 0:w], wslice(k, hh, 0), c, k == 0, k == 1)
                        ins.then_inc(job_ready, 1)
                for t, t0 in enumerate((0, P, SEQ, T, T + P, T + 2 * P, T + 3 * P)):
                    j = jk + 8 + t
                    start_job(j)
                    for k in range(2):
                        c = (latents(h_hi)[:, k, t0:t0 + P], latents(h_lo)[:, k, t0:t0 + P])
                        wv = [w[:, n % SPLIT_SLOTS, :].rearrange("p (k h v c) -> p k h v c", k=2, h=4, v=2)[:, k, :, 1, :]
                              for w in (w_hi, w_lo)]
                        ins = triple(ps[:, job_bank(j), :].rearrange("p (h c) -> p h c", h=4), c, wv, k == 0, k == 1)
                    ins.then_inc(job_ready, 1)

                def mla_scores(c):
                    if c > HEADS + 2 * hb:
                        pe.wait_ge(exp_done, c)
                    pr = c - HEADS
                    for half in range(2):
                        d = slice(64 * half, 64 * half + 64)
                        qn = wk(M_QN + T * (2 * pr + half), T)
                        kn = wk(M_KN + NTOK * (2 * (pr % 2) + half), NTOK)
                        qr, kr = wk(M_QR + T * pr, T, d), wk(M_KR, NTOK, d)
                        for out, q, k in ((ps[:, half, 0:SEQ], slice(P, SEQ), slice(0, SEQ)),
                                          (ps[:, half, SEQ:PH], slice(0, P), slice(0, P)),
                                          (ps[d, 2, :], slice(SEQ, T), slice(T, NTOK)),
                                          (ps[d, 3, 0:DEC], slice(SEQ, T), slice(SEQ, T))):
                            pe.matmul(out, qn[:, q], kn[:, k], start=True, stop=False)
                            ins = pe.matmul(out, qr[:, q], kr[:, k], start=False, stop=True)
                    ins.then_inc(scores_ready, 1)

                def mla_transpose(c):
                    pe.wait_ge(diag_ready, c + 1)
                    pe.wait_ge(o_lo_done, c - HEADS + 2)
                    dg = [wk(M_DG + P * k, P) for k in range(5)]
                    for half in range(2):
                        for col, at, k in ((0, PH * half + SEQ, 2), (P, PH * half, 0), (SEQ, PH * half + P, 0)):
                            pe.matmul(ps[:, 4 + half, col:col + P], wk(M_P + at, P), dg[k + half], start=True, stop=True)
                    for kt in range(4):
                        pe.matmul(ps[:, 6, P * kt:P * kt + P], wk(M_P + 768 + P * kt, P), dg[4], start=True, stop=True)
                    pe.matmul(ps[0:DEC, 7, 0:P], wk(M_P + 768 + PAST, DEC), dg[4], start=True,
                              stop=True).then_inc(at_ready, 1)

                def mla_values(c):
                    pe.wait_ge(at_copied, c + 1)
                    for half in range(2):
                        out = ps[:, 4 + half, :]
                        hd = P * (2 * ((c - HEADS) % 2) + half)
                        at = M_AT + 384 * half
                        pe.matmul(out[:, 0:SEQ], wk(M_VM + hd, P), wk(at, SEQ), start=True, stop=False)
                        pe.matmul(out[:, P:SEQ], wk(M_VM + UC + hd, P), wk(at + SEQ, P), start=False, stop=True)
                        for kt in range(4):
                            pe.matmul(out[:, SEQ:T], wk(M_VM + UC * (3 + kt) + hd, P),
                                      wk(M_AT + 768 + P * kt + 64 * half, 64), start=(kt == 0), stop=False)
                        new = slice(0, DEC)
                        ins = pe.matmul(out[:, SEQ:T], wk(M_VM + 2 * UC + hd, P, new),
                                        wk(M_AT + 1280 + 64 * half, 64, new), start=False, stop=True)
                    ins.then_inc(o_ready, 1)

                c0 = HEADS + 2 * hb
                if hb == 0:
                    pe.wait_ge(job_drained, jk + 12)
                    out_unit(U_OA3, GR_OA3, 0, last=False, frees=True)
                    pe.wait_ge(job_drained, jk + 15)
                    mla_scores(c0)
                    out_unit(U_OA3 + 1, GR_OA3, 1, first=False)
                    mla_scores(c0 + 1)
                    pe.wait_ge(drained, GR_OA3 + 1)
                else:
                    pe.wait_ge(job_drained, jk + 15)
                    out_unit(U_OB, GR_OB, 2, frees=True)
                    mla_scores(c0)
                    out_unit(U_OB + 1, GR_OB + 1, 2)
                    mla_scores(c0 + 1)
                    pe.wait_ge(drained, GR_OB + 2)
                for c in (c0, c0 + 1):
                    mla_transpose(c)
                    mla_values(c)

            out_unit(U_OB + 2, GR_OB + 2, 2)
            pe.wait_ge(o_lo_done, 6)
            for j in range(3, 8):
                out_unit(U_OB + j, GR_OB + j, 2 + j // 4)
            ffn(1, U_F2, GR_F2)
            def y_job(n):
                j, t, r0, rows = Y_JOBS[n]
                if n >= 7:
                    pe.wait_ge(y_odd if n % 2 == 0 else y_even, (n - 7) // 2 + 1)
                for a in range(4):
                    ins = pe.transpose(ps[0:rows, y_bank(n), P * a:P * a + P], xT[:, 4 * j + a, r0:r0 + rows], ident)
                ins.then_inc(y_turned, 1)

            pe.wait_ge(sq_added, 11)
            for step, at in enumerate((F_ACC, F_SQ)):
                if step:
                    pe.wait_ge(y_scaled, 2)
                    for n in range(3):
                        y_job(n)
                    pe.wait_ge(squared, 16)
                for t, (r0, rows) in enumerate(TOK):
                    for a in range(4):
                        ins = pe.matmul(ps[0:rows, 3, t:t + 1], wk(at + T * a + r0, rows), ones[:, 0:1],
                                        start=(step == 0 and t == 0 and a == 0), stop=(step == 1 and a == 3),
                                        skip_group_check=True)
            ins.then_inc(tok_sum, 1)
            pe.wait_ge(drained, GR_F2 + FFN_GROUPS)
            for n in range(3, 12):
                if n % 3 == 0:
                    pe.wait_ge(y_scaled, n // 3 + 1)
                y_job(n)


def constants():
    f = np.float32
    p = np.arange(P)
    pos = np.concatenate([np.arange(SEQ), PAST + np.arange(DEC)]).astype(f)
    half = ROPE // 2
    inv = (ROPE_THETA ** (-np.arange(half) / half)).astype(f)
    ang = pos[None, :] * inv[p % half][:, None]
    sign = np.where(p % ROPE < half, -1.0, 1.0)[:, None]
    q1, k1 = (P + p)[:, None], np.arange(SEQ)[None, :]
    dist = np.where(k1 // CHUNK <= q1 // CHUNK, np.abs(q1 - k1), BIG)
    dists = np.abs(PAST + (p % DEC)[:, None] - np.arange(KEYS)[None, :])
    stack = p[:, None] % HALF == np.arange(HALF)[None, :]
    swap = (p[:, None] ^ half) == p[None, :]
    return np.concatenate([np.eye(P), stack, swap, np.cos(ang), sign * np.sin(ang), dist, dist[:, P:], dists],
                          axis=1).astype(f)


_INS = ["x_prompt", "x_sample", "cache_da_k", "cache_da_v", "cache_mla_ckv", "cache_mla_krope",
        "ffn1_norm", "ffn1_w_gate", "ffn1_w_up", "ffn1_w_down", "mix_norm", "w_in",
        "da_lambda_q1", "da_lambda_k1", "da_lambda_q2", "da_lambda_k2", "da_subln",
        "mla_q_norm", "mla_w_uq", "mla_kv_norm", "mla_w_ukv", "w_out",
        "ffn2_norm", "ffn2_w_gate", "ffn2_w_up", "ffn2_w_down", "final_norm"]
_OUTS = [(1, SEQ, D), (1, DEC, D),
         (1, 1, SEQ, HEADS, DH), (1, 1, SEQ, HEADS, DH), (1, 1, SEQ, KVL), (1, 1, SEQ, ROPE),
         (1, 1, DEC, HEADS, DH), (1, 1, DEC, HEADS, DH), (1, 1, DEC, KVL), (1, 1, DEC, ROPE)]


def kernel(**inputs):
    import concourse.bacc as bacc
    from concourse.bass_utils import run_bass_kernel_spmd

    nc = bacc.Bacc("TRN2", target_bir_lowering=False, num_devices=1)
    arrays = {f"in_{name}": np.ascontiguousarray(inputs[name]) for name in _INS}
    arrays["in_table"] = constants()
    args = [nc.dram_tensor(name, a.shape, F32, kind="ExternalInput").ap() for name, a in arrays.items()]
    args += [nc.dram_tensor(f"out_{i}", shape, F32, kind="ExternalOutput").ap() for i, shape in enumerate(_OUTS)]
    build(nc, *args)
    r = run_bass_kernel_spmd(nc, [arrays], core_ids=[0])
    return tuple(r.results[0][f"out_{i}"] for i in range(len(_OUTS)))
```
